# Optimizing a Trainium2 kernel written in Bass

```python
import math
import jax
import jax.numpy as jnp
from jax import lax
import numpy as np

D_MODEL = 1024
BATCH = 1
SEQ = 2048
DEPTH = 1
DEC_BATCH = 8
DEC_SEQ = 1
PAST_LEN = 2048
PAGE_SIZE = 128

HEAD_DIM = 64
N_HEADS = 8
D_ATT = N_HEADS * HEAD_DIM
D_CONV = D_MODEL - D_ATT
D_MIX = D_ATT + D_CONV
DILATED_CFGS = ((128, 1), (512, 4), (2048, 16))
WIN_MAX = max(w for w, _ in DILATED_CFGS)
ATT_BLK = 128
CONV_W = 31
NUM_BUCKETS = 32
MAX_DISTANCE = WIN_MAX
N_GROUPS = 4
EXPERTS_PER_GROUP = 8
N_EXPERTS = N_GROUPS * EXPERTS_PER_GROUP
TOP_K = 2
D_EXPERT = 512
EXPERT_BLK = 128
EPS = 1e-6
NEG_INF = -1e30
D_IN = 3 * D_ATT + 2 * D_CONV

kernel_name = 'hybrid_dilated_attn_conformer_conv_hmoe_step'

def rmsnorm(x, g):
    xf = x.astype(jnp.float32)
    y = xf * lax.rsqrt(jnp.mean(xf * xf, axis=-1, keepdims=True) + EPS)
    return (y * g.astype(jnp.float32)).astype(x.dtype)

def layernorm(x, g, b):
    xf = x.astype(jnp.float32)
    xc = xf - jnp.mean(xf, axis=-1, keepdims=True)
    var = jnp.mean(xc * xc, axis=-1, keepdims=True)
    return (xc * lax.rsqrt(var + EPS) * g.astype(jnp.float32) + b.astype(jnp.float32)).astype(x.dtype)

def t5_bucket(dist):
    n = jnp.maximum(dist, 0)
    max_exact = NUM_BUCKETS // 2
    nf = jnp.maximum(n, 1).astype(jnp.float32)
    large = max_exact + (jnp.log(nf / max_exact) / math.log(MAX_DISTANCE / max_exact)
                         * (NUM_BUCKETS - max_exact)).astype(jnp.int32)
    large = jnp.minimum(large, NUM_BUCKETS - 1)
    return jnp.where(n < max_exact, n, large)

def banded_dilated_branch(q, k, v, rel_bias, window, dilation):
    B, S, H, Dh = q.shape
    wsub = window // dilation
    N = S // dilation
    nb = -(-N // ATT_BLK)
    Np = nb * ATT_BLK

    def to_sub(t):
        return t.reshape(B, N, dilation, H, Dh).transpose(0, 2, 3, 1, 4)

    qs = jnp.pad(to_sub(q), ((0, 0), (0, 0), (0, 0), (0, Np - N), (0, 0)))
    kp = jnp.pad(to_sub(k), ((0, 0), (0, 0), (0, 0), (ATT_BLK, Np - N), (0, 0)))
    vp = jnp.pad(to_sub(v), ((0, 0), (0, 0), (0, 0), (ATT_BLK, Np - N), (0, 0)))

    def band(t):
        cur = t[:, :, :, ATT_BLK:].reshape(B, dilation, H, nb, ATT_BLK, Dh)
        prev = t[:, :, :, :Np].reshape(B, dilation, H, nb, ATT_BLK, Dh)
        return jnp.concatenate([prev, cur], axis=4)

    kb, vb = band(kp), band(vp)
    qb = qs.reshape(B, dilation, H, nb, ATT_BLK, Dh)
    i = jnp.arange(ATT_BLK)[:, None]
    j = jnp.arange(2 * ATT_BLK)[None, :]
    rel = i + ATT_BLK - j
    bias = rel_bias[t5_bucket(rel * dilation)].astype(jnp.float32).transpose(2, 0, 1)
    kpos = jnp.arange(nb)[:, None, None] * ATT_BLK - ATT_BLK + j[None]
    valid = (rel >= 0) & (rel <= wsub) & (kpos >= 0)
    s = jnp.einsum('bdhnqe,bdhnke->bdhnqk', qb, kb, preferred_element_type=jnp.float32)
    s = jnp.where(valid[None, None, None], s + bias[None, None, :, None], NEG_INF)
    m = jnp.max(s, axis=-1)
    p = jnp.exp(s - m[..., None])
    l = jnp.sum(p, axis=-1)
    num = jnp.einsum('bdhnqk,bdhnke->bdhnqe', p, vb.astype(jnp.float32))
    num = num.reshape(B, dilation, H, Np, Dh)[:, :, :, :N].transpose(0, 3, 1, 2, 4).reshape(B, S, H, Dh)

    def back(t):
        return t.reshape(B, dilation, H, Np)[:, :, :, :N].transpose(0, 3, 1, 2).reshape(B, S, H)

    return num, back(m), back(l)

def gathered_dilated_branch(q, kext, vext, rel_bias, window, dilation, past_len):
    T = q.shape[1]
    nk = window // dilation + 1
    steps = jnp.arange(nk) * dilation
    t = jnp.arange(T)[:, None]
    idx = kext.shape[1] - T + t - steps[None, :]
    kg = kext[:, idx]
    vg = vext[:, idx]
    s = jnp.einsum('bthe,btkhe->bthk', q, kg, preferred_element_type=jnp.float32)
    bias = rel_bias[t5_bucket(steps)].astype(jnp.float32).T
    valid = (past_len + t - steps[None, :]) >= 0
    s = jnp.where(valid[None, :, None, :], s + bias[None, None], NEG_INF)
    m = jnp.max(s, axis=-1)
    p = jnp.exp(s - m[..., None])
    l = jnp.sum(p, axis=-1)
    num = jnp.einsum('bthk,btkhe->bthe', p, vg.astype(jnp.float32))
    return num, m, l

def combine_branches(branches):
    M = branches[0][1]
    for _, m, _ in branches[1:]:
        M = jnp.maximum(M, m)
    numer = sum(jnp.exp(m - M)[..., None] * num for num, m, _ in branches)
    denom = sum(jnp.exp(m - M) * l for _, m, l in branches)
    return numer / denom[..., None]

def causal_dwconv(u_ext, w, b):
    out = lax.conv_general_dilated(
        u_ext, w[:, None, :].astype(u_ext.dtype), window_strides=(1,), padding='VALID',
        dimension_numbers=('NWC', 'WIO', 'NWC'), feature_group_count=u_ext.shape[-1])
    return out + b

def expert_mlp(xb, w1, w3, w2):
    return (jax.nn.silu(xb @ w1) * (xb @ w3)) @ w2

def hierarchical_moe(h, w_rg, b_rg, w_re, b_re, w_e1, w_e3, w_e2):
    T, D = h.shape
    hf = h.astype(jnp.float32)
    lg = hf @ w_rg.astype(jnp.float32) + b_rg.astype(jnp.float32)
    pg = jax.nn.softmax(lg, axis=-1)
    grp = jnp.argmax(lg, axis=-1)
    p_grp = jnp.take_along_axis(pg, grp[:, None], axis=-1)
    le = (hf @ w_re.astype(jnp.float32) + b_re.astype(jnp.float32)).reshape(T, N_GROUPS, EXPERTS_PER_GROUP)
    le = jnp.take_along_axis(le, grp[:, None, None], axis=1)[:, 0]
    top_p, top_i = lax.top_k(jax.nn.softmax(le, axis=-1), TOP_K)
    wts = p_grp * top_p / jnp.sum(top_p, axis=-1, keepdims=True)
    eid = grp[:, None] * EXPERTS_PER_GROUP + top_i

    A = T * TOP_K
    e_flat = eid.reshape(A).astype(jnp.int32)
    tok = jnp.repeat(jnp.arange(T, dtype=jnp.int32), TOP_K)
    order = jnp.argsort(e_flat)
    e_s, tok_s, w_s = e_flat[order], tok[order], wts.reshape(A)[order]
    counts = jnp.bincount(e_flat, length=N_EXPERTS)
    starts = jnp.cumsum(counts) - counts
    padded = (counts + EXPERT_BLK - 1) // EXPERT_BLK * EXPERT_BLK
    pends = jnp.cumsum(padded)
    pstarts = pends - padded
    dest = pstarts[e_s] + (jnp.arange(A, dtype=jnp.int32) - starts[e_s])
    NB = -(-A // EXPERT_BLK) + N_EXPERTS
    slot_tok = jnp.full((NB * EXPERT_BLK,), T, dtype=jnp.int32).at[dest].set(tok_s)
    xb = jnp.concatenate([h, jnp.zeros((1, D), h.dtype)], axis=0)[slot_tok].reshape(NB, EXPERT_BLK, D)
    blk_e = jnp.minimum(jnp.searchsorted(pends, jnp.arange(NB) * EXPERT_BLK, side='right'), N_EXPERTS - 1)
    yb = lax.map(lambda a: expert_mlp(a[0], w_e1[a[1]], w_e3[a[1]], w_e2[a[1]]), (xb, blk_e))
    y_assign = yb.reshape(NB * EXPERT_BLK, D)[dest]
    return jnp.zeros((T, D), h.dtype).at[tok_s].add(w_s[:, None].astype(h.dtype) * y_assign)

def decoder_layer(x, c, kbuf, vbuf, conv_buf, is_prompt, rel_bias, w_ada, b_ada, g_n1, w_in,
                  conv_w, conv_b, ln_g, ln_b, w_out, g_n2, w_rg, b_rg, w_re, b_re, w_e1, w_e3, w_e2):
    B, T, D = x.shape
    mod = (jax.nn.silu(c) @ w_ada + b_ada)[:, None, :]
    sh1, sc1, gt1, sh2, sc2, gt2 = jnp.split(mod, 6, axis=-1)
    h = rmsnorm(x, g_n1) * (1 + sc1) + sh1
    proj = h @ w_in
    q, k, v, u_val, u_gate = jnp.split(proj, [D_ATT, 2 * D_ATT, 3 * D_ATT, 3 * D_ATT + D_CONV], axis=-1)
    q = q.reshape(B, T, N_HEADS, HEAD_DIM) * (HEAD_DIM ** -0.5)
    k = k.reshape(B, T, N_HEADS, HEAD_DIM)
    v = v.reshape(B, T, N_HEADS, HEAD_DIM)
    kext = jnp.concatenate([kbuf, k], axis=1)
    vext = jnp.concatenate([vbuf, v], axis=1)
    if is_prompt:
        branches = [banded_dilated_branch(q, k, v, rel_bias, w, d) for w, d in DILATED_CFGS]
    else:
        branches = [gathered_dilated_branch(q, kext, vext, rel_bias, w, d, PAST_LEN) for w, d in DILATED_CFGS]
    att = combine_branches(branches).reshape(B, T, D_ATT).astype(x.dtype)
    new_k = kext[:, -WIN_MAX:]
    new_v = vext[:, -WIN_MAX:]
    glu = u_val * jax.nn.sigmoid(u_gate)
    cext = jnp.concatenate([conv_buf, glu], axis=1)
    conv = jax.nn.silu(layernorm(causal_dwconv(cext, conv_w, conv_b), ln_g, ln_b))
    new_conv = cext[:, -(CONV_W - 1):]
    x = x + gt1 * (jnp.concatenate([att, conv], axis=-1) @ w_out)
    h2 = rmsnorm(x, g_n2) * (1 + sc2) + sh2
    x = x + gt2 * hierarchical_moe(h2.reshape(B * T, D), w_rg, b_rg, w_re, b_re, w_e1, w_e3, w_e2).reshape(B, T, D)
    return x, new_k, new_v, new_conv

def setup_inputs(seed: int = 0) -> dict:
    key = jax.random.key(seed)
    ks = jax.random.split(key, 26)
    nrm = lambda k, s, sc: jax.random.normal(k, s, jnp.float32) * sc
    D = D_MODEL
    return {
        'x_prompt': nrm(ks[0], (BATCH, SEQ, D), 1.0),
        'x_sample': nrm(ks[1], (DEC_BATCH, DEC_SEQ, D), 1.0),
        'cache_k': nrm(ks[2], (DEPTH, DEC_BATCH, WIN_MAX, N_HEADS, HEAD_DIM), 1.0),
        'cache_v': nrm(ks[3], (DEPTH, DEC_BATCH, WIN_MAX, N_HEADS, HEAD_DIM), 1.0),
        'state_conv': nrm(ks[4], (DEPTH, DEC_BATCH, CONV_W - 1, D_CONV), 0.5),
        'c_prompt': nrm(ks[5], (BATCH, D), 1.0),
        'c_sample': nrm(ks[6], (DEC_BATCH, D), 1.0),
        'rel_bias': nrm(ks[7], (NUM_BUCKETS, N_HEADS), 0.1),
        'w_ada': nrm(ks[8], (DEPTH, D, 6 * D), 0.5 * D ** -0.5),
        'b_ada': nrm(ks[9], (DEPTH, 6 * D), 0.01),
        'g_norm1': 1.0 + nrm(ks[10], (DEPTH, D), 0.01),
        'w_in': nrm(ks[11], (DEPTH, D, D_IN), D ** -0.5),
        'conv_w': nrm(ks[12], (DEPTH, CONV_W, D_CONV), CONV_W ** -0.5),
        'conv_b': nrm(ks[13], (DEPTH, D_CONV), 0.01),
        'ln_g': 1.0 + nrm(ks[14], (DEPTH, D_CONV), 0.01),
        'ln_b': nrm(ks[15], (DEPTH, D_CONV), 0.01),
        'w_out': nrm(ks[16], (DEPTH, D_MIX, D), D_MIX ** -0.5),
        'g_norm2': 1.0 + nrm(ks[17], (DEPTH, D), 0.01),
        'w_router_group': nrm(ks[18], (DEPTH, D, N_GROUPS), D ** -0.5),
        'b_router_group': nrm(ks[19], (DEPTH, N_GROUPS), 0.01),
        'w_router_expert': nrm(ks[20], (DEPTH, D, N_EXPERTS), D ** -0.5),
        'b_router_expert': nrm(ks[21], (DEPTH, N_EXPERTS), 0.01),
        'w_expert_gate': nrm(ks[22], (DEPTH, N_EXPERTS, D, D_EXPERT), D ** -0.5),
        'w_expert_up': nrm(ks[23], (DEPTH, N_EXPERTS, D, D_EXPERT), D ** -0.5),
        'w_expert_down': nrm(ks[24], (DEPTH, N_EXPERTS, D_EXPERT, D), D_EXPERT ** -0.5),
        'g_final': 1.0 + nrm(ks[25], (D,), 0.01),
    }

def reference(x_prompt, x_sample, cache_k, cache_v, state_conv, c_prompt, c_sample, rel_bias,
              w_ada, b_ada, g_norm1, w_in, conv_w, conv_b, ln_g, ln_b, w_out, g_norm2,
              w_router_group, b_router_group, w_router_expert, b_router_expert,
              w_expert_gate, w_expert_up, w_expert_down, g_final):
    yp, ys = x_prompt, x_sample
    bp = x_prompt.shape[0]
    zero_kv = jnp.zeros((bp, WIN_MAX, N_HEADS, HEAD_DIM), x_prompt.dtype)
    zero_conv = jnp.zeros((bp, CONV_W - 1, D_CONV), x_prompt.dtype)
    kp_l, vp_l, cp_l, ks_l, vs_l, cs_l = [], [], [], [], [], []
    for l in range(DEPTH):
        w = (rel_bias, w_ada[l], b_ada[l], g_norm1[l], w_in[l], conv_w[l], conv_b[l], ln_g[l], ln_b[l],
             w_out[l], g_norm2[l], w_router_group[l], b_router_group[l], w_router_expert[l],
             b_router_expert[l], w_expert_gate[l], w_expert_up[l], w_expert_down[l])
        yp, kp, vp, cp = decoder_layer(yp, c_prompt, zero_kv, zero_kv, zero_conv, True, *w)
        ys, kS, vS, cS = decoder_layer(ys, c_sample, cache_k[l], cache_v[l], state_conv[l], False, *w)
        kp_l.append(kp); vp_l.append(vp); cp_l.append(cp)
        ks_l.append(kS); vs_l.append(vS); cs_l.append(cS)
    y_prompt = rmsnorm(yp, g_final)
    y_sample = rmsnorm(ys, g_final)
    return (y_prompt, y_sample, jnp.stack(kp_l), jnp.stack(vp_l), jnp.stack(cp_l),
            jnp.stack(ks_l), jnp.stack(vs_l), jnp.stack(cs_l))


_drawn_inputs = setup_inputs


def setup_inputs(seed=0):
    import zlib

    import numpy as np

    out = dict(_drawn_inputs(seed))
    spreads = {}
    factors = {'rel_bias': 8.0,
     'b_ada': 3.798,
     'g_norm1': 5.799,
     'conv_b': 8.0,
     'ln_g': 8.0,
     'ln_b': 8.0,
     'g_norm2': 7.69,
     'b_router_group': 8.0,
     'b_router_expert': 15.304,
     'g_final': 32.063}
    for name, (base, spread) in spreads.items():
        noise = np.random.default_rng([zlib.crc32(name.encode()), seed]).standard_normal(out[name].shape)
        drawn = base * np.exp(spread * noise) if base else spread * noise
        out[name] = jnp.asarray(drawn.astype(out[name].dtype))
    for name, factor in factors.items():
        out[name] = (out[name] * factor).astype(out[name].dtype)
    return out
```

```python
from contextlib import ExitStack
import math

import numpy as np
import concourse.bass as bass
import concourse.mybir as mybir
from concourse.alu_op_type import AluOpType as ALU

F32 = mybir.dt.float32
I32 = mybir.dt.int32
U32 = mybir.dt.uint32
ACT = mybir.ActivationFunctionType
AX = mybir.AxisListType
ds = bass.ds

P = 128
SEQ = 2048
DEC = 8
D = 1024
KD = D // P
HEADS = 8
DH = 64
DATT = HEADS * DH
DCONV = D - DATT
KC = DCONV // P
DIN = 3 * DATT + 2 * DCONV
TAPS = 31
DILATIONS = (1, 4, 16)
WSUB = 128
WIN = 2048
BUCKETS = 32
GROUPS = 4
PER = 8
NEXP = GROUPS * PER
DEXP = 512
KF = DEXP // P
EPS = 1e-6
NEG = -1e30
TILES = SEQ // P
ALLT = TILES + 1
ROWS = SEQ + DEC
CAP = (ROWS + P - 1) // P * P
MAXBLK = NEXP + (2 * ROWS) // P
VEC = 384
NUMW = DATT + 2 * HEADS


def t5_bucket(dist):
    n = np.maximum(np.asarray(dist), 0)
    half = BUCKETS // 2
    nf = np.maximum(n, 1).astype(np.float32)
    large = half + (np.log(nf / np.float32(half)) / np.float32(math.log(WIN / half)) * (BUCKETS - half)).astype(np.int32)
    return np.where(n < half, n, np.minimum(large, BUCKETS - 1))


def constant_columns():
    parts = {}
    parts["ident"] = np.eye(P)
    parts["before"] = np.triu(np.ones((P, P)), 1)
    parts["ones"] = np.ones((P, P))
    band = np.zeros((P, len(DILATIONS) * VEC))
    for b, dil in enumerate(DILATIONS):
        for x in range(VEC):
            rel = 255 - x
            if 0 <= rel <= WSUB:
                band[t5_bucket(rel * dil), b * VEC + x] = 1.0
            else:
                band[BUCKETS, b * VEC + x] = NEG
    parts["band"] = band
    dec = np.zeros((P, 3 * P + 3))
    for b, dil in enumerate(DILATIONS):
        for j in range(1, WSUB + 1):
            dec[t5_bucket(j * dil), b * P + WSUB - j] = 1.0
        dec[0, 3 * P + b] = 1.0
    parts["decband"] = dec
    parts["neghalf"] = np.full((P, 1), -0.5)
    parts["eps"] = np.full((P, 1), EPS)
    parts["iota"] = np.tile(np.arange(NEXP), (P, 1))
    parts["thresholds"] = np.tile(np.arange(1, 17) * P, (P, 1))
    parts["lower"] = np.tile((np.arange(NEXP)[None, :] < np.arange(NEXP)[:, None]).reshape(1, -1), (P, 1))
    parts["headmask"] = np.zeros((P, DATT))
    for h in range(HEADS):
        parts["headmask"][h, h * DH:(h + 1) * DH] = 1.0
    parts["rowsel"] = np.zeros((P, DEC * DEC))
    parts["rowcast"] = np.zeros((P, DEC * P))
    for b in range(DEC):
        parts["rowsel"][0:HEADS, b * DEC + b] = 1.0
        parts["rowcast"][b, b * P:(b + 1) * P] = 1.0
    parts["tapsum"] = np.zeros((P, 2 * DEC))
    for t in range(2):
        for r in range(4 * (TAPS - 1)):
            parts["tapsum"][r, t * DEC + 4 * t + r // (TAPS - 1)] = 1.0
    at, cols = {}, []
    n = 0
    for name, a in parts.items():
        at[name] = (n, a.shape[1])
        cols.append(np.asarray(a, np.float32))
        n += a.shape[1]
    return at, np.ascontiguousarray(np.concatenate(cols, axis=1))


def decoder_step(nc, t, const_at, stop_after=99):
    with ExitStack() as whole:
        def persistent(name, shape, dt=F32):
            return whole.enter_context(nc.sbuf_tensor(name, shape, dt))

        K = persistent("K", [P, t["constants"].shape[1]])

        def const(name, rows=P):
            n, w = const_at[name]
            return K[0:rows, n:n + w]

        scratch = {
            "mod": nc.dram_tensor("mod_rows", [DEC + 1, 6 * D], F32).ap(),
            "q": nc.dram_tensor("q_rows", [SEQ, DATT], F32).ap(),
            "conv": nc.dram_tensor("conv_cols", [DCONV, SEQ], F32).ap(),
            "dec": nc.dram_tensor("decode_rows", [4, DEC, DATT], F32).ap(),
            "vec": nc.dram_tensor("band_vectors", [HEADS, 3 * VEC], F32).ap(),
            "band": nc.dram_tensor("band_rows", [3, P, HEADS, VEC], F32).ap(),
            "num": nc.dram_tensor("branch_rows", [3, SEQ, DATT], F32).ap(),
            "stat": nc.dram_tensor("branch_stats", [3, SEQ, 2 * HEADS], F32).ap(),
            "new": nc.dram_tensor("newest_scores", [2, DEC * HEADS], F32).ap(),
            "mix": nc.dram_tensor("decode_mix", [DEC, D], F32).ap(),
            "x2": nc.dram_tensor("x2_rows", [ROWS, D], F32).ap(),
            "h2": nc.dram_tensor("h2_rows", [ROWS, D], F32).ap(),
            "slot": nc.dram_tensor("slot_tokens", [NEXP * CAP, 1], I32).ap(),
            "y": nc.dram_tensor("expert_rows", [MAXBLK * P, D], F32).ap(),
        }
        state = {
            "decbias": persistent("decbias", [DEC * HEADS, 3 * P + 3]),
        }
        setup_and_modulation(nc, t, scratch, const, K, state)
        if stop_after >= 1:
            input_projection(nc, t, scratch, const)
        if stop_after >= 2:
            prompt_attention(nc, t, scratch, const)
        if stop_after >= 3:
            decode_mixers(nc, t, scratch, const, state)
        if stop_after >= 4:
            state["token"] = persistent("token", [P, ALLT], I32)
            for name in ("rank", "expert", "weight"):
                state[name] = persistent(name, [P, ALLT, 2])
            state["count"] = persistent("count", [P, NEXP])
            output_projection_and_routing(nc, t, scratch, const, state)
        if stop_after >= 5:
            state["blocks"] = persistent("blocks", [P, 2 * NEXP], I32)
            state["dest"] = persistent("dest", [P, ALLT, 2], U32)
            expert_tables(nc, const, state)
            experts(nc, t, scratch, const, state)
        if stop_after >= 6:
            combine_and_normalise(nc, t, scratch, const, state)
        return scratch


def stage_semaphores(nc, ctx):
    mine = []

    def sem(name):
        mine.append(nc.alloc_semaphore(name))
        return mine[-1]

    def give_back():
        nc.clear_and_free_semaphores(mine)
        nc.all_engine_barrier()

    ctx.callback(give_back)
    return sem


def setup_and_modulation(nc, t, dr, const, K, state):
    NCH = 6 * D // 512
    with ExitStack() as ctx:
        def sb(name, shape, dt=F32):
            return ctx.enter_context(nc.sbuf_tensor(name, shape, dt))

        def ps(name, shape):
            return ctx.enter_context(nc.psum_tensor(name, shape, F32))

        sem = stage_semaphores(nc, ctx)

        CN = sb("CN", [P, D])
        SG = sb("SG0", [P, D])
        CT = sb("CT", [P, KD, P])
        WA = sb("WA", [P, 2, KD, 512])
        BA = sb("BA", [P, 2, 512])
        MO = sb("MO", [P, 2, 512])
        RB = sb("RB", [P, HEADS])
        RBX = sb("RBX", [P, DEC, HEADS])
        VE = sb("VE", [HEADS, 3 * VEC])
        Z = sb("Z", [P, NEXP * CAP // P], I32)
        TP = ps("TP0", [P, KD, P])
        MP = ps("MP0", [P, 2, 512])
        BP = ps("BP0", [P, 4, 512])
        consts_in, c_in, rb_in = sem("consts_in"), sem("c_in"), sem("rb_in")
        rb_set, rbx_ready, sig_ready, silu_ready = sem("rb_set"), sem("rbx_ready"), sem("sig_ready"), sem("silu_ready")
        ct_in_psum, ct_ready, bias_in_psum, vec_ready = sem("ct_in_psum"), sem("ct_ready"), sem("bias_in_psum"), sem("vec_ready")
        decbias_ready = sem("decbias_ready")
        vec_out, band_out, zero_set, zero_out = sem("vec_out"), sem("band_out"), sem("zero_set"), sem("zero_out")
        w_in = [sem(f"ada_in{p}") for p in range(2)]
        w_used, mod_in_psum, mod_ready = sem("ada_used"), sem("mod_in_psum"), sem("mod_ready")
        mod_out = [sem(f"mod_out{p}") for p in range(2)]

        with nc.Block() as block:
            @block.sync
            def _(sp):
                sp.dma_start(K[:], t["constants"]).then_inc(consts_in, 16)
                sp.dma_start(CN[0:DEC, :], t["c_sample"]).then_inc(c_in, 16)
                sp.dma_start(CN[DEC:P, :], t["c_prompt"].to_broadcast([P - DEC, D])).then_inc(c_in, 16)
                sp.wait_ge(rb_set, 1)
                sp.dma_start(RB[0:BUCKETS, :], t["rel_bias"]).then_inc(rb_in, 16)
                w = t["w_ada"][0].rearrange("(k p) n -> p k n", p=P)
                with sp.Fori(0, NCH // 2) as i:
                    for p in range(2):
                        col = sp.snap((i * 2 + p) * 512)
                        sp.wait_ge(w_used, i * 2 + p + 1)
                        sp.dma_start(WA[:, p], w[:, :, ds(col, 512)]).then_inc(w_in[p], 16)
                        sp.dma_start(BA[:, p], t["b_ada"][0:1, ds(col, 512)].to_broadcast([P, 512])).then_inc(w_in[p], 16)

            @block.gpsimd
            def _(pool):
                pool.memset(RB[:], 1.0).then_inc(rb_set, 1)
                pool.memset(Z[:], 0).then_inc(zero_set, 1)
                pool.wait_ge(zero_set, 1)
                pool.dma_start(dr["slot"].rearrange("(p n) o -> p (n o)", p=P), Z[:]).then_inc(zero_out, 16)
                pool.wait_ge(vec_ready, 1)
                pool.dma_start(dr["vec"], VE[:]).then_inc(vec_out, 16)
                pool.wait_ge(vec_out, 16)
                for b in range(3):
                    pool.dma_start(dr["band"][b], dr["vec"][:, b * VEC:(b + 1) * VEC].partition_broadcast(P)).then_inc(band_out, 16)
                pool.wait_ge(band_out, 48)
                pool.wait_ge(zero_out, 16)

            @block.scalar
            def _(act):
                act.wait_ge(c_in, 32)
                nc.scalar.activation(SG[:], CN[:], ACT.Sigmoid).then_inc(sig_ready, 1)
                act.wait_ge(ct_in_psum, 1)
                nc.scalar.copy(CT[:], TP[:]).then_inc(ct_ready, 1)
                for p in range(2):
                    act.sem_inc(mod_out[p], 16)
                with act.Fori(0, NCH // 2) as i:
                    for p in range(2):
                        col = act.snap((i * 2 + p) * 512)
                        act.wait_ge(mod_ready, i * 2 + p + 1)
                        act.dma_start(dr["mod"][:, ds(col, 512)], MO[0:DEC + 1, p]).then_inc(mod_out[p], 16)
                for p in range(2):
                    act.wait_ge(mod_out[p], 16 * (NCH // 2) + 16)

            @block.vector
            def _(dve):
                dve.wait_ge(sig_ready, 1)
                nc.vector.tensor_tensor(CN[:], CN[:], SG[:], ALU.mult).then_inc(silu_ready, 1)
                dve.wait_ge(rb_in, 16)
                nc.vector.tensor_copy(RBX[0:33], RB[0:33, None, :].to_broadcast([33, DEC, HEADS])).then_inc(rbx_ready, 1)
                dve.wait_ge(bias_in_psum, 1)
                for b in range(3):
                    last = nc.vector.tensor_copy(VE[:, b * VEC:(b + 1) * VEC], BP[0:HEADS, b, 0:VEC])
                last.then_inc(vec_ready, 1)
                nc.vector.tensor_copy(state["decbias"][:], BP[0:DEC * HEADS, 3, 0:3 * P + 3]).then_inc(decbias_ready, 1)
                with dve.Fori(0, NCH // 2) as i:
                    for p in range(2):
                        dve.wait_ge(mod_in_psum, i * 2 + p + 1)
                        dve.wait_ge(mod_out[p], i * 16 + 16)
                        nc.vector.tensor_tensor(MO[:, p], MP[:, p], BA[:, p], ALU.add).then_inc(mod_ready, 1)

            @block.tensor
            def _(pe):
                pe.wait_ge(consts_in, 16)
                pe.wait_ge(silu_ready, 1)
                for k in range(KD):
                    last = nc.tensor.transpose(TP[:, k], CN[:, k * P:(k + 1) * P], const("ident"))
                last.then_inc(ct_in_psum, 1)
                pe.wait_ge(rbx_ready, 1)
                for b in range(3):
                    nc.tensor.matmul(BP[0:HEADS, b, 0:VEC], RB[0:33, :], const("band", 33)[:, b * VEC:(b + 1) * VEC], start=True, stop=True)
                nc.tensor.matmul(BP[0:DEC * HEADS, 3, 0:3 * P + 3], RBX[0:33].rearrange("p a b -> p (a b)"), const("decband", 33),
                                 start=True, stop=True).then_inc(bias_in_psum, 1)
                pe.wait_ge(ct_ready, 1)
                pe.sem_inc(w_used, 2)
                with pe.Fori(0, NCH // 2) as i:
                    for p in range(2):
                        pe.wait_ge(w_in[p], i * 32 + 32)
                        for k in range(KD):
                            mm = nc.tensor.matmul(MP[:, p], CT[:, k], WA[:, p, k], start=k == 0, stop=k == KD - 1)
                        mm.then_inc(mod_in_psum, 1)
                        pe.wait_ge(mod_ready, i * 2 + p + 1)
                        pe.sem_inc(w_used, 1)


def input_projection(nc, t, dr, const):
    with ExitStack() as ctx:
        def sb(name, shape, dt=F32):
            return ctx.enter_context(nc.sbuf_tensor(name, shape, dt))

        def ps(name, shape):
            return ctx.enter_context(nc.psum_tensor(name, shape, F32))

        sem = stage_semaphores(nc, ctx)

        WIN_SB = sb("WIN_SB", [P, KD, DIN])
        GAIN, SHIFT, G1 = sb("GAIN", [P, 2, D]), sb("SHIFT", [P, 2, D]), sb("G1", [P, D])
        X, SQ, H, HT = sb("X", [P, D]), sb("SQ", [P, D]), sb("H", [P, D]), sb("HT", [P, KD, P])
        SSQ, MS, RSTD = sb("SSQ", [P, 1]), sb("MS", [P, 1]), sb("RSTD", [P, 1])
        SIG, GLU = sb("SIG", [P, DCONV]), sb("GLU", [P, DCONV])
        QKV = sb("QKV", [P, 3, DATT])
        CW, TAPW = sb("CW", [TAPS + 1, DCONV]), sb("TAPW", [P, KC, TAPS + 1])
        GEXT = sb("GEXT", [P, KC, TAPS - 1 + P])
        CONV = sb("CONV", [P, KC, P])
        TP = ps("TP1", [P, KD, P])
        PJ = ps("PJ", [P, 5, 512])
        GT = ps("GT", [P, KC, P])

        w_loaded, mods_in, gain_ready, taps_in = sem("w_loaded"), sem("mods_in"), sem("gain_ready"), sem("taps_in")
        taps_psum, taps_ready, ext_zero = sem("taps_psum"), sem("taps_ready"), sem("ext_zero")
        x_in, ssq_ready, ms_ready, rstd_ready = sem("x_in"), sem("ssq_ready"), sem("ms_ready"), sem("rstd_ready")
        h_half, h_ready, h_turned, ht_ready = sem("h_half"), sem("h_ready"), sem("h_turned"), sem("ht_ready")
        chunk_done, sig_done, glu_ready, glu_turned, ext_ready = sem("chunk_done"), sem("sig_done"), sem("glu_ready"), sem("glu_turned"), sem("ext_ready")
        qkv_ready = sem("qkv_ready")
        qkv_out = [sem(f"qkv_out{n}") for n in range(3)]
        conv_step, conv_ready, conv_out, tail_out = sem("conv_step"), sem("conv_ready"), sem("conv_out"), sem("tail_out")
        cache_out = [sem("cache_k_out"), sem("cache_v_out")]
        carry = sem("carry")

        DECT = TILES
        dec = dr["dec"]
        cache = t["cache_k"], t["cache_v"]
        newc = t["new_k_sample"], t["new_v_sample"]

        with nc.Block() as block:
            @block.sync
            def _(sp):
                for n, which in enumerate((1, 0)):
                    dst = (GAIN, SHIFT)[n]
                    sp.dma_start(dst[:, 0], dr["mod"][DEC:DEC + 1, which * D:(which + 1) * D].to_broadcast([P, D])).then_inc(mods_in, 16)
                    sp.dma_start(dst[0:DEC, 1], dr["mod"][0:DEC, which * D:(which + 1) * D]).then_inc(mods_in, 16)
                sp.dma_start(G1[:], t["g_norm1"].to_broadcast([P, D])).then_inc(mods_in, 16)
                sp.dma_start(CW[0:TAPS, :], t["conv_w"][0]).then_inc(taps_in, 16)
                sp.dma_start(CW[TAPS:TAPS + 1, :], t["conv_b"]).then_inc(taps_in, 16)
                sp.dma_start(X[:], t["x_prompt"][0, 0:P, :]).then_inc(x_in, 16)
                sp.dma_start(WIN_SB[:], t["w_in"][0].rearrange("(k p) n -> p k n", p=P)).then_inc(w_loaded, 16)
                columns = dr["conv"].rearrange("(c p) s -> p c s", p=P)
                sp.wait_ge(h_ready, 1)
                sp.dma_start(X[:], t["x_prompt"][0, P:2 * P, :]).then_inc(x_in, 16)
                with sp.Fori(2, TILES) as i:
                    row, conv_at = sp.snap(i * P), sp.snap((i - 2) * P)
                    made, convolved = sp.snap(i), sp.snap(i - 1)
                    sp.wait_ge(h_ready, made)
                    sp.dma_start(X[:], t["x_prompt"][0, ds(row, P), :]).then_inc(x_in, 16)
                    sp.wait_ge(conv_ready, convolved)
                    sp.dma_start(columns[:, :, ds(conv_at, P)], CONV[:]).then_inc(conv_out, 16)
                sp.wait_ge(h_ready, TILES)
                sp.dma_start(X[0:DEC, :], t["x_sample"][:, 0, :]).then_inc(x_in, 16)
                sp.wait_ge(conv_ready, TILES - 1)
                sp.dma_start(columns[:, :, (TILES - 2) * P:(TILES - 1) * P], CONV[:]).then_inc(conv_out, 16)
                sp.wait_ge(glu_ready, TILES)
                sp.dma_start(t["new_conv_prompt"], GLU[P - TAPS + 1:P, :]).then_inc(tail_out, 16)
                sp.wait_ge(conv_ready, TILES)
                sp.dma_start(columns[:, :, (TILES - 1) * P:], CONV[:]).then_inc(conv_out, 16)
                sp.wait_ge(conv_out, 16 * TILES + 16)
                for n in range(3):
                    sp.wait_ge(qkv_out[n], 16 * TILES + 16 + (16 if n == 0 else 32))

            @block.gpsimd
            def _(pool):
                pool.memset(GEXT[:, :, 0:TAPS - 1], 0.0).then_inc(ext_zero, 1)

                def scale(tile):
                    pool.wait_ge(ssq_ready, tile + 1)
                    pool.tensor_tensor(MS[:], SSQ[:], const("eps"), ALU.add).then_inc(ms_ready, 1)
                    pool.wait_ge(ms_ready, tile + 1)
                    pool.tensor_tensor(RSTD[:], MS[:], const("neghalf"), ALU.pow).then_inc(rstd_ready, 1)

                for half in range(2):
                    with pool.Fori(0, DEC) as b:
                        pool.dma_start(newc[half][ds(b, 1), 0:(WIN - 1) * DATT], cache[half][ds(b, 1), DATT:WIN * DATT]).then_inc(cache_out[half], 16)
                        scale(b + half * DEC)
                scale(DECT)
                pool.wait_ge(cache_out[0], 16 * DEC)
                pool.wait_ge(cache_out[1], 16 * DEC)

            @block.scalar
            def _(act):
                for n in range(3):
                    act.sem_inc(qkv_out[n], 16)
                act.sem_inc(conv_out, 16)
                act.sem_inc(qkv_ready, 1)
                act.wait_ge(taps_psum, 1)
                nc.scalar.copy(TAPW[:], GT[:, :, 0:TAPS + 1]).then_inc(taps_ready, 1)

                def squares(tile, rows):
                    act.wait_ge(x_in, tile * 16 + 16)
                    nc.scalar.activation(SQ[0:rows], X[0:rows], ACT.Square, scale=D ** -0.5, accum_out=SSQ[0:rows]).then_inc(ssq_ready, 1)

                def evacuate(tile):
                    act.wait_ge(h_turned, tile + 1)
                    nc.scalar.copy(HT[:], TP[:]).then_inc(ht_ready, 1)
                    act.wait_ge(chunk_done, tile * 5 + 1)
                    nc.scalar.activation(SIG[:], PJ[:, 0], ACT.Sigmoid).then_inc(sig_done, 1)

                def qkv(tile):
                    for n in range(3):
                        act.wait_ge(chunk_done, tile * 5 + 3 + n)
                        act.wait_ge(qkv_out[n], tile * 16 + 16)
                        nc.scalar.mul(QKV[:, n], PJ[:, 2 + n], DH ** -0.5 if n == 0 else 1.0).then_inc(qkv_ready, 1)

                squares(0, P)
                with act.Fori(0, TILES - 1) as i:
                    row = act.snap(i * P)
                    evacuate(i)
                    squares(i + 1, P)
                    qkv(i)
                    for n, dst in enumerate((dr["q"], t["new_k_prompt"], t["new_v_prompt"])):
                        act.wait_ge(qkv_ready, i * 3 + n + 2)
                        act.dma_start(dst[ds(row, P), :], QKV[:, n]).then_inc(qkv_out[n], 16)
                evacuate(TILES - 1)
                squares(DECT, DEC)
                qkv(TILES - 1)
                for n, dst in enumerate((dr["q"], t["new_k_prompt"], t["new_v_prompt"])):
                    act.wait_ge(qkv_ready, TILES * 3 + n - 1)
                    act.dma_start(dst[SEQ - P:, :], QKV[:, n]).then_inc(qkv_out[n], 16)
                evacuate(DECT)
                qkv(DECT)
                for n, dst in enumerate((None, t["new_k_sample"], t["new_v_sample"])):
                    act.wait_ge(qkv_ready, DECT * 3 + n + 2)
                    act.dma_start(dec[n], QKV[0:DEC, n]).then_inc(qkv_out[n], 16)
                    if dst is not None:
                        act.dma_start(dst[:, (WIN - 1) * DATT:], QKV[0:DEC, n]).then_inc(qkv_out[n], 16)

            @block.vector
            def _(dve):
                dve.wait_ge(mods_in, 16 * 5)
                nc.vector.scalar_tensor_tensor(out=GAIN[:, 0], in0=GAIN[:, 0], scalar=1.0, in1=G1[:], op0=ALU.add, op1=ALU.mult).then_inc(gain_ready, 1)
                nc.vector.scalar_tensor_tensor(out=GAIN[0:DEC, 1], in0=GAIN[0:DEC, 1], scalar=1.0, in1=G1[0:DEC], op0=ALU.add, op1=ALU.mult).then_inc(gain_ready, 1)
                dve.wait_ge(gain_ready, 2)

                def modulated(tile, rows, which):
                    dve.wait_ge(rstd_ready, tile + 1)
                    dve.wait_ge(h_turned, tile)
                    nc.vector.scalar_tensor_tensor(out=H[0:rows], in0=X[0:rows], scalar=RSTD[0:rows], in1=GAIN[0:rows, which], op0=ALU.mult, op1=ALU.mult).then_inc(h_half, 1)
                    dve.wait_ge(h_half, tile + 1)
                    nc.vector.tensor_tensor(H[0:rows], H[0:rows], SHIFT[0:rows, which], ALU.add).then_inc(h_ready, 1)

                def glu(tile):
                    dve.wait_ge(sig_done, tile + 1)
                    dve.wait_ge(chunk_done, tile * 5 + 2)
                    nc.vector.tensor_tensor(GLU[:], PJ[:, 1], SIG[:], ALU.mult).then_inc(glu_ready, 1)

                def convolve(tile):
                    dve.wait_ge(glu_turned, tile + 1)
                    nc.vector.tensor_copy(GEXT[:, :, TAPS - 1:], GT[:]).then_inc(ext_ready, 1)
                    dve.wait_ge(ext_ready, tile + 1)
                    dve.wait_ge(conv_out, tile * 16 + 16)
                    for j in range(TAPS):
                        for c in range(KC):
                            if j == 0:
                                ins = nc.vector.tensor_scalar(CONV[:, c], GEXT[:, c, 0:P], TAPW[:, c, 0:1], TAPW[:, c, TAPS:TAPS + 1], ALU.mult, ALU.add)
                            else:
                                dve.wait_ge(conv_step, (j - 1) * KC + c + 1)
                                ins = nc.vector.scalar_tensor_tensor(out=CONV[:, c], in0=GEXT[:, c, j:j + P], scalar=TAPW[:, c, j:j + 1], in1=CONV[:, c], op0=ALU.mult, op1=ALU.add)
                            ins.then_inc(conv_step, 1)
                    dve.wait_ge(conv_step, TAPS * KC)
                    dve.sem_clear(conv_step)
                    nc.vector.tensor_copy(GEXT[:, :, 0:TAPS - 1], GEXT[:, :, P:P + TAPS - 1]).then_inc(conv_ready, 1)
                    dve.wait_ge(conv_ready, tile + 1)

                dve.wait_ge(rstd_ready, 1)
                nc.vector.scalar_tensor_tensor(out=H[:], in0=X[:], scalar=RSTD[:], in1=GAIN[:, 0], op0=ALU.mult, op1=ALU.mult).then_inc(h_half, 1)
                dve.wait_ge(h_half, 1)
                nc.vector.tensor_tensor(H[:], H[:], SHIFT[:, 0], ALU.add).then_inc(h_ready, 1)
                dve.wait_ge(ext_zero, 1)
                dve.wait_ge(taps_ready, 1)
                with dve.Fori(0, TILES - 1) as i:
                    modulated(i + 1, P, 0)
                    glu(i)
                    convolve(i)
                modulated(DECT, DEC, 1)
                glu(TILES - 1)
                convolve(TILES - 1)
                dve.wait_ge(tail_out, 16)
                glu(DECT)

            @block.tensor
            def _(pe):
                pe.wait_ge(taps_in, 32)
                for c in range(KC):
                    last = nc.tensor.transpose(GT[:, c, 0:TAPS + 1], CW[:, c * P:(c + 1) * P], const("ident")[0:TAPS + 1, 0:TAPS + 1])
                last.then_inc(taps_psum, 1)
                pe.wait_ge(taps_ready, 1)
                pe.wait_ge(w_loaded, 16)
                columns = (3 * DATT + DCONV, 3 * DATT, 0, DATT, 2 * DATT)

                def project(tile):
                    pe.wait_ge(h_ready, tile + 1)
                    for k in range(KD):
                        mm = nc.tensor.transpose(TP[:, k], H[:, k * P:(k + 1) * P], const("ident"))
                    mm.then_inc(h_turned, 1)
                    pe.wait_ge(ht_ready, tile + 1)
                    for n, col in enumerate(columns):
                        if n == 2:
                            pe.wait_ge(qkv_ready, tile * 3 + 1)
                        for k in range(KD):
                            mm = nc.tensor.matmul(PJ[:, n], HT[:, k], WIN_SB[:, k, col:col + 512], start=k == 0, stop=k == KD - 1)
                        mm.then_inc(chunk_done, 1)

                def turn_glu(tile):
                    pe.wait_ge(glu_ready, tile + 1)
                    for c in range(KC):
                        mm = nc.tensor.transpose(GT[:, c], GLU[:, c * P:(c + 1) * P], const("ident"))
                    mm.then_inc(glu_turned, 1)

                with pe.Fori(0, TILES) as i:
                    project(i)
                    turn_glu(i)
                project(DECT)

        with nc.Block() as block:
            @block.sync
            def _(sp):
                sp.dma_start(dec[3], GLU[0:DEC]).then_inc(tail_out, 16)
                sp.wait_ge(tail_out, 32)


def dilated(rows, dil, r, first, count):
    v = rows.rearrange("(i d) c -> d i c", d=dil)
    v = v[r] if isinstance(r, int) else v[ds(r, 1)].rearrange("a i c -> (a i) c")
    v = v[first:first + count, :] if isinstance(first, int) else v[ds(first, count), :]
    return v.rearrange("(k p) c -> p k c", p=P) if count > P else v


def prompt_attention(nc, t, dr, const):
    segments = [
        (2, 0, TILES - 1, lambda j: 0, lambda j: j + 1),
        (2, 1, 4, lambda j: j, lambda j: 1),
        (2, 1, 4, lambda j: j, lambda j: 2),
        (2, 1, 4, lambda j: j, lambda j: 3),
        (1, 0, 1, lambda j: 0, lambda j: 0),
        (1, 1, 4, lambda j: j, lambda j: 0),
        (1, 2, 16, lambda j: j, lambda j: 0),
    ]
    starts = [sum(s[2] for s in segments[:n]) for n in range(len(segments))]
    BLOCKS = sum(s[2] for s in segments)
    FULL = sum(s[2] for s in segments if s[0] == 2)
    HH = HEADS // 2
    with ExitStack() as ctx:
        def sb(name, shape, dt=F32):
            return ctx.enter_context(nc.sbuf_tensor(name, shape, dt))

        def ps(name, shape):
            return ctx.enter_context(nc.psum_tensor(name, shape, F32))

        sem = stage_semaphores(nc, ctx)

        BIAS = [sb(f"BIAS{b}", [P, HEADS, 2 * P]) for b in range(3)]
        QN, KN, VN = sb("QN", [P, DATT]), sb("KN", [P, 2, DATT]), sb("VN", [P, 2, DATT])
        QZ = sb("QZ", [P, HEADS, P])
        KT = sb("KT", [P, HH, 2 * P])
        SBX = [sb(f"SBX{h}", [P, HH, 2 * P]) for h in range(2)]
        PR = [sb(f"PR{h}", [P, HH, 2 * P]) for h in range(2)]
        PTS = sb("PTS", [P, 2 * HH, P])
        PAUSE = sb("PAUSE", [P, 1])
        MX, NM, ML = sb("MX", [P, HEADS]), sb("NM", [P, HEADS]), sb("ML", [P, 2 * HEADS])
        O = sb("O", [P, DATT])
        SP_ = [ps(f"S{h}", [P, HH, 2 * P]) for h in range(2)]
        TQ, TB, OP = ps("TQ", [P, HH, P]), ps("TB", [P, 2 * HH, P]), ps("OP", [P, HH, P])

        bias_in, qz_zero = sem("bias_in"), sem("qz_zero")
        qk_in, v_in = sem("qk_in"), sem("v_in")
        qk_turned, kt_ready, s_done, mx_done, nm_ready, m_saved = sem("qk_turned"), sem("kt_ready"), sem("s_done"), sem("mx_done"), sem("nm_ready"), sem("m_saved")
        exp_done, pt_done, pt_ready, pv_done, o_taken = sem("exp_done"), sem("pt_done"), sem("pt_ready"), sem("pv_done"), sem("o_taken")
        o_out, ml_out = sem("o_out"), sem("ml_out")

        with nc.Block() as block:
            @block.sync
            def _(sp):
                def load_qk(g, seg, j):
                    nk, b, _, r, n = seg
                    n1 = n(j)
                    q, k = (dilated(x, DILATIONS[b], r(j), first, c) for x, first, c in (
                        (dr["q"], sp.snap(n1 * P) if not isinstance(n1, int) else n1 * P, P),
                        (t["new_k_prompt"], sp.snap((n1 - nk + 1) * P) if not isinstance(n1, int) else (n1 - nk + 1) * P, nk * P)))
                    if not (isinstance(g, int) and g == 0):
                        sp.wait_ge(qk_turned, g)
                    sp.dma_start(QN[:], q).then_inc(qk_in, 16)
                    sp.dma_start(KN[:] if nk == 2 else KN[:, 0], k).then_inc(qk_in, 16)

                def load_v(g, seg, j):
                    nk, b, _, r, n = seg
                    n1 = n(j)
                    v = dilated(t["new_v_prompt"], DILATIONS[b], r(j), sp.snap((n1 - nk + 1) * P) if not isinstance(n1, int) else (n1 - nk + 1) * P, nk * P)
                    if not (isinstance(g, int) and g == 0):
                        sp.wait_ge(pv_done, g * 2)
                    sp.dma_start(VN[:] if nk == 2 else VN[:, 0], v).then_inc(v_in, 16)

                def store(g, seg, j):
                    nk, b, _, r, n = seg
                    n1 = n(j)
                    first = sp.snap(n1 * P) if not isinstance(n1, int) else n1 * P
                    sp.wait_ge(m_saved, g + 1)
                    sp.wait_ge(exp_done, g * 2 + 4)
                    sp.dma_start(dilated(dr["stat"][b], DILATIONS[b], r(j), first, P), ML[:]).then_inc(ml_out, 16)
                    sp.wait_ge(o_taken, g * 2 + 3)
                    sp.dma_start(dilated(dr["num"][b], DILATIONS[b], r(j), first, P), O[:]).then_inc(o_out, 16)

                for b in range(3):
                    v = dr["band"][b]
                    skew = bass.AP(v.tensor, v.offset + P - 1, [[HEADS * VEC - 1, P], [VEC, HEADS], [1, 2 * P]])
                    sp.dma_start(BIAS[b][:], skew).then_inc(bias_in, 16)
                load_qk(0, segments[0], 0)
                load_v(0, segments[0], 0)
                for n, seg in enumerate(segments):
                    if seg[2] > 1:
                        with sp.Fori(0, seg[2] - 1) as j:
                            g = sp.snap(j + starts[n])
                            load_qk(g + 1, seg, j + 1)
                            load_v(g + 1, seg, j + 1)
                            store(g, seg, j)
                    g = starts[n] + seg[2] - 1
                    if n + 1 < len(segments):
                        load_qk(g + 1, segments[n + 1], 0)
                        load_v(g + 1, segments[n + 1], 0)
                    store(g, seg, seg[2] - 1)
                sp.wait_ge(ml_out, 16 * BLOCKS + 16)
                sp.wait_ge(o_out, 16 * BLOCKS + 16)

            @block.gpsimd
            def _(pool):
                pool.memset(QZ[:], 0.0).then_inc(qz_zero, 1)

            @block.vector
            def _(dve):
                dve.wait_ge(bias_in, 48)
                dve.wait_ge(qz_zero, 1)

                def scores(g, seg):
                    nk, b = seg[0], seg[1]
                    w = nk * P
                    dve.wait_ge(qk_turned, g + 1)
                    nc.vector.tensor_copy(QZ[0:DH, 0::2], TQ[0:DH])
                    nc.vector.tensor_copy(QZ[DH:P, 1::2], TQ[DH:P])
                    nc.vector.tensor_copy(KT[:, :, 0:w].rearrange("p h (k q) -> p h k q", q=P), TB[:, 0:HH * nk].rearrange("p (h k) q -> p h k q", k=nk)).then_inc(kt_ready, 1)
                    for hh in range(2):
                        dve.wait_ge(s_done, g * 2 + hh + 1)
                        dve.wait_ge(exp_done, g * 2 + hh + 1)
                        nc.vector.memset(PAUSE[:], 0.0)
                        for h in range(HH):
                            head = hh * HH + h
                            nc.vector.tensor_tensor_reduce(SBX[hh][:, h, 0:w], SP_[hh][:, h, 0:w], BIAS[b][:, head, 2 * P - w:], 1.0, -3e38, ALU.add, ALU.max,
                                                           MX[:, head:head + 1]).then_inc(mx_done, 1)
                        dve.wait_ge(mx_done, g * 8 + hh * 4 + 4)
                        nc.vector.tensor_scalar(NM[:, hh * HH:hh * HH + HH], MX[:, hh * HH:hh * HH + HH], -1.0, None, ALU.mult).then_inc(nm_ready, 1)
                    dve.wait_ge(ml_out, g * 16 + 16)
                    nc.vector.tensor_copy(ML[:, 0:HEADS], MX[:]).then_inc(m_saved, 1)

                for n, seg in enumerate(segments):
                    with dve.Fori(starts[n], starts[n] + seg[2]) as g:
                        scores(g, seg)

            def by_width(engine, first, ahead, behind):
                first()
                with engine.Fori(0, FULL - 1) as g:
                    ahead(g + 1, 2)
                    behind(g, 2)
                ahead(FULL, 1)
                behind(FULL - 1, 2)
                with engine.Fori(FULL, BLOCKS - 1) as g:
                    ahead(g + 1, 1)
                    behind(g, 1)
                behind(BLOCKS - 1, 1)

            @block.scalar
            def _(act):
                act.sem_inc(exp_done, 2)
                act.sem_inc(ml_out, 16)
                act.sem_inc(o_out, 16)
                act.sem_inc(o_taken, 1)

                def exponentials(g, nk):
                    w = nk * P
                    for hh in range(2):
                        act.wait_ge(nm_ready, g * 2 + hh + 1)
                        act.wait_ge(pt_done, g * 2 + hh + 1)
                        act.wait_ge(ml_out, g * 16 + 16)
                        for h in range(HH):
                            head = hh * HH + h
                            ins = nc.scalar.activation(PR[hh][:, h, 0:w], SBX[hh][:, h, 0:w], ACT.Exp, bias=NM[:, head:head + 1], scale=1.0,
                                                       accum_out=ML[:, HEADS + head:HEADS + head + 1])
                        ins.then_inc(exp_done, 1)

                def evacuate(g, nk):
                    for hh in range(2):
                        act.wait_ge(pt_done, g * 2 + hh + 3)
                        nc.scalar.copy(PTS[:, 0:HH * nk], TB[:, 0:HH * nk]).then_inc(pt_ready, 1)
                        act.wait_ge(pv_done, g * 2 + hh + 1)
                        act.wait_ge(o_out, g * 16 + 16)
                        half = O[:, hh * HH * DH:(hh + 1) * HH * DH].rearrange("p (a b e) -> p a b e", b=2, e=DH)
                        nc.scalar.copy(half[:, :, 0], OP[:, 0::2, 0:DH])
                        nc.scalar.copy(half[:, :, 1], OP[:, 1::2, DH:P]).then_inc(o_taken, 1)

                exponentials(0, 2)
                with act.Fori(0, FULL - 1) as g:
                    evacuate(g, 2)
                    exponentials(g + 1, 2)
                evacuate(FULL - 1, 2)
                exponentials(FULL, 1)
                with act.Fori(FULL, BLOCKS - 1) as g:
                    evacuate(g, 1)
                    exponentials(g + 1, 1)
                evacuate(BLOCKS - 1, 1)

            @block.tensor
            def _(pe):
                pe.sem_inc(pt_done, 2)

                def qk(g, nk):
                    pe.wait_ge(qk_in, g * 32 + 32)
                    for h in range(HH):
                        nc.tensor.transpose(TQ[:, h], QN[:, h * P:(h + 1) * P], const("ident"))
                    for h in range(HH):
                        for k in range(nk):
                            mm = nc.tensor.transpose(TB[:, h * nk + k], KN[:, k, h * P:(h + 1) * P], const("ident"))
                    mm.then_inc(qk_turned, 1)
                    pe.wait_ge(kt_ready, g + 1)
                    for hh in range(2):
                        for h in range(HH):
                            head = hh * HH + h
                            mm = nc.tensor.matmul(SP_[hh][:, h, 0:nk * P], QZ[:, head], KT[:, head // 2, 0:nk * P], start=True, stop=True)
                        mm.then_inc(s_done, 1)

                def pv(g, nk):
                    for hh in range(2):
                        pe.wait_ge(exp_done, g * 2 + hh + 3)
                        for h in range(HH):
                            for k in range(nk):
                                mm = nc.tensor.transpose(TB[:, h * nk + k], PR[hh][:, h, k * P:(k + 1) * P], const("ident"))
                        mm.then_inc(pt_done, 1)
                        pe.wait_ge(v_in, g * 16 + 16)
                        pe.wait_ge(pt_ready, g * 2 + hh + 1)
                        pe.wait_ge(o_taken, g * 2 + hh + 1)
                        for h in range(HH):
                            pair = (hh * HH + h) // 2
                            for k in range(nk):
                                mm = nc.tensor.matmul(OP[:, h], PTS[:, h * nk + k], VN[:, k, pair * P:(pair + 1) * P], start=k == 0, stop=k == nk - 1)
                        mm.then_inc(pv_done, 1)

                by_width(pe, lambda: qk(0, 2), qk, pv)



def decode_mixers(nc, t, dr, const, state):
    TS = TAPS - 1
    KEYS = 3 * P
    BH = DEC * HEADS
    with ExitStack() as ctx:
        def sb(name, shape, dt=F32):
            return ctx.enter_context(nc.sbuf_tensor(name, shape, dt))

        def ps(name, shape):
            return ctx.enter_context(nc.psum_tensor(name, shape, F32))

        sem = stage_semaphores(nc, ctx)

        R = sb("DROWS", [DEC, 4, DATT])
        QB, CK, CV = sb("QB", [P, DATT]), sb("CK", [P, 3, DATT]), sb("CV", [P, 3, DATT])
        TMP, SC = sb("TMP", [P, 3, DATT]), sb("SC", [P, 3, BH])
        QK0, S0, N0 = sb("QK0", [DEC, DATT]), sb("S0D", [DEC, HEADS]), sb("N0", [BH, 1])
        SS, PE_, MXD, NMD, LD, RD = sb("SS", [BH, KEYS + 3]), sb("PE_", [BH, KEYS + 3]), sb("MXD", [BH, 1]), sb("NMD", [BH, 1]), sb("LD", [BH, 1]), sb("RD", [BH, 1])
        P0, P8 = sb("P0", [BH, 1]), sb("P8", [DEC, HEADS])
        PTD, PB, OM = sb("PTD", [P, 3, BH]), sb("PB", [P, 3, HEADS]), sb("OM", [HEADS, DATT])
        ROW, ATT, A0 = sb("ROW", [1, DATT]), sb("ATT", [DEC, DATT]), sb("A0", [DEC, DATT])
        ST, CWR = sb("ST", [4 * TS, 2, DCONV]), sb("CWR", [4 * TS, DCONV])
        WL, CB, LG, LB = sb("WL", [DEC, DCONV]), sb("CB", [DEC, DCONV]), sb("LGD", [DEC, DCONV]), sb("LBD", [DEC, DCONV])
        CVN, BS, MV, VE, RS, TH = sb("CVN", [DEC, DCONV]), sb("BSD", [DEC, 6]), sb("MVD", [DEC, 2]), sb("VED", [DEC, 1]), sb("RSD", [DEC, 1]), sb("THD", [DEC, DCONV])
        MIX = sb("MIXD", [DEC, D])
        STP, PTP, OD, OR, CP = ps("STP", [BH, 3, P]), ps("PTP", [P, 3, BH]), ps("OD", [HEADS, DATT]), ps("OR", [P, DATT]), ps("CP", [DEC, DCONV])

        rows_in, conv_in, k_in, v_in = sem("rows_in"), sem("conv_in"), sem("dk_in"), sem("dv_in")
        mul_done, red_done, s_turned, s0_done, n0_out, n0_in = sem("mul_done"), sem("red_done"), sem("s_turned"), sem("s0_done"), sem("n0_out"), sem("n0_in")
        step, exp_ready, p0_ready, p0_out, p8_in = sem("softmax_step"), sem("dexp_ready"), sem("p0_ready"), sem("p0_out"), sem("p8_in")
        p_turned, ptd_ready, pb_ready, od_done, om_ready, or_done, row_ready, row_out, att_in = (sem("p_turned"), sem("ptd_ready"), sem("pb_ready"), sem("od_done"),
                                                                                               sem("om_ready"), sem("or_done"), sem("row_ready"), sem("row_out"), sem("att_in"))
        row_free = sem("row_free")
        cstep, conv_sum, var_ready, rs_ready, th_ready, mix_ready, mix_out, state_out = (sem("cstep"), sem("conv_sum"), sem("var_ready"), sem("rs_ready"), sem("th_ready"),
                                                                                        sem("mix_ready"), sem("mix_out"), sem("state_out"))

        with nc.Block() as block:
            @block.sync
            def _(sp):
                sp.dma_start(R[:], dr["dec"].rearrange("n b c -> b n c")).then_inc(rows_in, 16)
                with sp.Fori(0, DEC) as b:
                    sp.wait_ge(red_done, b + 1)
                    sp.dma_start(QB[:], dr["dec"][0, ds(b, 1), :].to_broadcast([P, DATT])).then_inc(k_in, 16)
                    for n, dil in enumerate(DILATIONS):
                        keys = t["cache_k"][ds(b, 1), (WIN - P * dil) * DATT:].rearrange("a (p x) -> (a p) x", p=P)[:, 0:DATT]
                        sp.dma_start(CK[:, n], keys).then_inc(k_in, 16)
                with sp.Fori(0, DEC) as b:
                    sp.wait_ge(od_done, b + 1)
                    for n, dil in enumerate(DILATIONS):
                        vals = t["cache_v"][ds(b, 1), (WIN - P * dil) * DATT:].rearrange("a (p x) -> (a p) x", p=P)[:, 0:DATT]
                        sp.dma_start(CV[:, n], vals).then_inc(v_in, 16)

            @block.gpsimd
            def _(pool):
                pool.dma_start(t["new_conv_sample"][:, 0:(TS - 1) * DCONV], t["state_conv"][:, DCONV:]).then_inc(state_out, 16)
                pool.dma_start(t["new_conv_sample"][:, (TS - 1) * DCONV:], dr["dec"][3]).then_inc(state_out, 16)
                for b in range(4):
                    pool.dma_start(CWR[b * TS:(b + 1) * TS, :], t["conv_w"][0, 0:TS, :]).then_inc(conv_in, 16)
                pool.dma_start(ST[:], t["state_conv"].rearrange("b (w c) -> (b w) c", w=TS).rearrange("(n r) c -> r n c", n=2)).then_inc(conv_in, 16)
                for dst, src in ((WL, t["conv_w"][0, TS:TAPS, :]), (CB, t["conv_b"]), (LG, t["ln_g"]), (LB, t["ln_b"])):
                    pool.dma_start(dst[:], src.to_broadcast([DEC, DCONV])).then_inc(conv_in, 16)
                pool.wait_ge(var_ready, 1)
                pool.tensor_tensor(VE[:], MV[:, 1:2], const("eps", DEC), ALU.add).then_inc(rs_ready, 1)
                pool.wait_ge(rs_ready, 1)
                pool.tensor_tensor(RS[:], VE[:], const("neghalf", DEC), ALU.pow).then_inc(rs_ready, 1)
                pool.wait_ge(s0_done, 1)
                pool.dma_start(dr["new"][0].rearrange("(b h) -> b h", b=DEC), S0[:]).then_inc(n0_out, 16)
                pool.wait_ge(n0_out, 16)
                pool.dma_start(N0[:], dr["new"][0].rearrange("(n o) -> n o", o=1)).then_inc(n0_in, 16)
                pool.wait_ge(p0_ready, 1)
                pool.dma_start(dr["new"][1].rearrange("(n o) -> n o", o=1), P0[:]).then_inc(p0_out, 16)
                pool.wait_ge(p0_out, 16)
                pool.dma_start(P8[:], dr["new"][1].rearrange("(b h) -> b h", b=DEC)).then_inc(p8_in, 16)
                with pool.Fori(0, DEC) as b:
                    pool.wait_ge(row_ready, b + 1)
                    pool.dma_start(dr["mix"][ds(b, 1), 0:DATT], ROW[:]).then_inc(row_out, 16)
                    pool.wait_ge(row_out, b * 16 + 16)
                    pool.sem_inc(row_free, 1)
                pool.wait_ge(row_out, 16 * DEC)
                pool.dma_start(ATT[:], dr["mix"][:, 0:DATT]).then_inc(att_in, 16)
                pool.wait_ge(mix_ready, 2)
                pool.dma_start(dr["mix"], MIX[:]).then_inc(mix_out, 16)
                pool.wait_ge(mix_out, 16)
                pool.wait_ge(state_out, 32)

            @block.scalar
            def _(act):
                act.wait_ge(cstep, 8)
                nc.scalar.activation(TH[:], CVN[:], ACT.Tanh, scale=0.5).then_inc(th_ready, 1)
                act.wait_ge(step, 4)
                nc.scalar.activation(PE_[:], SS[:], ACT.Exp, bias=NMD[:], scale=1.0, accum_out=LD[:]).then_inc(exp_ready, 1)

            @block.vector
            def _(dve):
                dve.sem_inc(red_done, 1)
                dve.wait_ge(rows_in, 16)
                nc.vector.tensor_tensor(QK0[:], R[:, 0], R[:, 1], ALU.mult).then_inc(mul_done, 1)
                dve.wait_ge(mul_done, 1)
                nc.vector.tensor_reduce(S0[:], QK0[:].rearrange("b (h e) -> b h e", e=DH), AX.X, ALU.add).then_inc(s0_done, 1)
                dve.wait_ge(conv_in, 16 * 9)
                nc.vector.tensor_tensor(ST[:], ST[:], CWR[:, None, :].to_broadcast([4 * TS, 2, DCONV]), ALU.mult).then_inc(cstep, 1)
                nc.vector.tensor_tensor(WL[:], WL[:], R[:, 3], ALU.mult).then_inc(cstep, 1)
                dve.wait_ge(cstep, 2)
                nc.vector.tensor_tensor(CVN[:], WL[:], CB[:], ALU.add).then_inc(cstep, 1)
                dve.wait_ge(cstep, 3)
                dve.wait_ge(conv_sum, 1)
                nc.vector.tensor_tensor(CVN[:], CP[:], CVN[:], ALU.add).then_inc(cstep, 1)
                dve.wait_ge(cstep, 4)
                nc.vector.bn_stats(BS[:], CVN[:]).then_inc(cstep, 1)
                dve.wait_ge(cstep, 5)
                nc.vector.bn_aggr(MV[:], BS[:]).then_inc(var_ready, 1)
                dve.wait_ge(rs_ready, 2)
                nc.vector.tensor_scalar(CVN[:], CVN[:], MV[:, 0:1], RS[:], ALU.subtract, ALU.mult).then_inc(cstep, 1)
                dve.wait_ge(cstep, 6)
                nc.vector.tensor_tensor(CVN[:], CVN[:], LG[:], ALU.mult).then_inc(cstep, 1)
                dve.wait_ge(cstep, 7)
                nc.vector.tensor_tensor(CVN[:], CVN[:], LB[:], ALU.add).then_inc(cstep, 1)
                dve.wait_ge(th_ready, 1)
                nc.vector.scalar_tensor_tensor(out=MIX[:, DATT:], in0=TH[:], scalar=1.0, in1=CVN[:], op0=ALU.add, op1=ALU.mult).then_inc(mix_ready, 1)
                with dve.Fori(0, DEC) as b:
                    dve.wait_ge(k_in, b * 64 + 64)
                    nc.vector.tensor_tensor(TMP[:], CK[:], QB[:, None, :].to_broadcast([P, 3, DATT]), ALU.mult).then_inc(mul_done, 1)
                    dve.wait_ge(mul_done, b + 2)
                    nc.vector.tensor_reduce(SC[:, :, ds(b * HEADS, HEADS)], TMP[:].rearrange("p n (h e) -> p n h e", e=DH), AX.X, ALU.add).then_inc(red_done, 1)
                dve.wait_ge(s_turned, 1)
                nc.vector.tensor_tensor(SS[:, 0:KEYS], STP[:].rearrange("p n k -> p (n k)"), state["decbias"][:, 0:KEYS], ALU.add).then_inc(step, 1)
                dve.wait_ge(n0_in, 16)
                nc.vector.tensor_scalar(SS[:, KEYS:], state["decbias"][:, KEYS:], N0[:], None, ALU.add).then_inc(step, 1)
                dve.wait_ge(step, 2)
                nc.vector.tensor_reduce(MXD[:], SS[:], AX.X, ALU.max).then_inc(step, 1)
                dve.wait_ge(step, 3)
                nc.vector.tensor_scalar(NMD[:], MXD[:], -1.0, None, ALU.mult).then_inc(step, 1)
                dve.wait_ge(exp_ready, 1)
                nc.vector.reciprocal(RD[:], LD[:]).then_inc(step, 1)
                dve.wait_ge(step, 5)
                nc.vector.tensor_scalar(SS[:], PE_[:], RD[:], None, ALU.mult).then_inc(step, 1)
                dve.wait_ge(step, 6)
                nc.vector.tensor_reduce(P0[:], SS[:, KEYS:], AX.X, ALU.add).then_inc(p0_ready, 1)
                dve.wait_ge(p_turned, 1)
                nc.vector.tensor_copy(PTD[:], PTP[:]).then_inc(ptd_ready, 1)
                dve.wait_ge(ptd_ready, 1)
                with dve.Fori(0, DEC) as b:
                    dve.wait_ge(od_done, b + 1)
                    nc.vector.tensor_copy(PB[:], PTD[:, :, ds(b * HEADS, HEADS)]).then_inc(pb_ready, 1)
                    dve.wait_ge(od_done, b + 2)
                    nc.vector.tensor_tensor(OM[:], OD[:], const("headmask", HEADS), ALU.mult).then_inc(om_ready, 1)
                    dve.wait_ge(or_done, b + 1)
                    dve.wait_ge(row_free, b + 1)
                    nc.vector.tensor_copy(ROW[:], OR[0:1]).then_inc(row_ready, 1)
                dve.wait_ge(att_in, 16)
                dve.wait_ge(p8_in, 16)
                nc.vector.tensor_tensor(A0[:].rearrange("b (h e) -> b h e", e=DH), R[:, 2].rearrange("b (h e) -> b h e", e=DH),
                                        P8[:, :, None].to_broadcast([DEC, HEADS, DH]), ALU.mult).then_inc(step, 1)
                dve.wait_ge(step, 7)
                nc.vector.tensor_tensor(MIX[:, 0:DATT], A0[:], ATT[:], ALU.add).then_inc(mix_ready, 1)

            @block.tensor
            def _(pe):
                pe.sem_inc(od_done, 1)
                pe.sem_inc(row_free, 1)
                pe.wait_ge(cstep, 2)
                for n in range(2):
                    mm = nc.tensor.matmul(CP[:], const("tapsum", 4 * TS)[:, n * DEC:(n + 1) * DEC], ST[:, n], start=n == 0, stop=n == 1)
                mm.then_inc(conv_sum, 1)
                pe.wait_ge(red_done, DEC + 1)
                for n in range(3):
                    mm = nc.tensor.transpose(STP[:, n], SC[:, n], const("ident"))
                mm.then_inc(s_turned, 1)
                pe.wait_ge(p0_ready, 1)
                for n in range(3):
                    mm = nc.tensor.transpose(PTP[:, n], SS[:, n * P:(n + 1) * P], const("ident")[0:BH, 0:BH])
                mm.then_inc(p_turned, 1)
                with pe.Fori(0, DEC) as b:
                    pe.wait_ge(pb_ready, b + 1)
                    pe.wait_ge(v_in, b * 48 + 48)
                    for n in range(3):
                        mm = nc.tensor.matmul(OD[:], PB[:, n], CV[:, n], start=n == 0, stop=n == 2)
                    mm.then_inc(od_done, 1)
                    pe.wait_ge(om_ready, b + 1)
                    nc.tensor.matmul(OR[:], const("ones", HEADS), OM[:], start=True, stop=True).then_inc(or_done, 1)


def output_projection_and_routing(nc, t, dr, const, state):
    with ExitStack() as ctx:
        def sb(name, shape, dt=F32):
            return ctx.enter_context(nc.sbuf_tensor(name, shape, dt))

        def ps(name, shape):
            return ctx.enter_context(nc.psum_tensor(name, shape, F32))

        sem = stage_semaphores(nc, ctx)

        NR = GROUPS + NEXP
        WO = sb("WO", [P, KD, D])
        GATE, GAIN, SHIFT, G2 = sb("GATE2", [P, 2, D]), sb("GAIN2", [P, 2, D]), sb("SHIFT2", [P, 2, D]), sb("G2", [P, D])
        LNG, LNB, WR, BR = sb("LNG", [P, DCONV]), sb("LNB", [P, DCONV]), sb("WR", [P, KD, NR]), sb("BR", [P, NR])
        NB, ST, CC, X = sb("NB", [P, 3, DATT]), sb("STAT", [P, 3, 2 * HEADS]), sb("CC", [P, KC, P]), sb("X3", [P, D])
        BM, BE, BW, BT, BD, BRC = (sb("BM", [P, HEADS]), sb("BE", [P, 3, HEADS]), sb("BW", [P, 3, HEADS]), sb("BT", [P, 3, HEADS]), sb("BD", [P, HEADS]), sb("BRC", [P, HEADS]))
        BS, MV, VE, RS, Y, TH = sb("BS3", [P, 6]), sb("MV3", [P, 2]), sb("VE3", [P, 1]), sb("RS3", [P, 1]), sb("Y3", [P, DCONV]), sb("TH3", [P, DCONV])
        MIX, MT = sb("MIX", [P, D]), sb("MT", [P, KD, P])
        X2, SQ, SSQ, MS, RSTD, H2, H2T = sb("X2", [P, D]), sb("SQ3", [P, D]), sb("SSQ3", [P, 1]), sb("MS3", [P, 1]), sb("RSTD3", [P, 1]), sb("H2", [P, D]), sb("H2T", [P, KD, P])
        LOG, G8, GM, GI, GF, NG = sb("LOG", [P, NR]), sb("G8", [P, 8]), sb("GM", [P, 8]), sb("GI", [P, 8], U32), sb("GF", [P, 1]), sb("NG", [P, 1])
        GE, ZG, OG, LS, L8, V8, I8, I2 = (sb("GE", [P, GROUPS]), sb("ZG", [P, 1]), sb("OG", [P, GROUPS]), sb("LS", [P, GROUPS, PER]), sb("L8", [P, PER]),
                                          sb("V8", [P, 8]), sb("I8", [P, 8], U32), sb("I2", [P, 2]))
        DV, EV, DEN, W1, EID, OH, A, RSEL, R2, SLOT = (sb("DV", [P, 1]), sb("EV", [P, 1]), sb("DEN", [P, 1]), sb("W1R", [P, 2]), sb("EID", [P, 2]), sb("OH", [P, 2, NEXP]),
                                                       sb("AR", [P, NEXP]), sb("RSEL", [P, 2, NEXP]), sb("R2", [P, 2]), sb("SLOT", [P, 2], U32))
        CNT, PAUSE, TOK = sb("CNT", [P, NEXP]), sb("PAUSE3", [P, 1]), sb("TOK", [P, 1], I32)
        placing = sem("placing")
        tok_ready = sem("tok_ready")
        CP, TPS, OP, LP, RP, NP_ = ps("CP3", [P, KC, P]), ps("TPS3", [P, KD, P]), ps("OP3", [P, D]), ps("LP", [P, NR]), ps("RP", [P, NEXP]), ps("NP", [P, NEXP])

        weights_in, mods_in, gain_ready, preset = sem("w3_in"), sem("mods3_in"), sem("gain3_ready"), sem("preset")
        br_in, cc_in, x_in = sem("br_in"), sem("cc_in"), sem("x3_in")
        astep, exp_b, att_ready, conv_turned, bn_done, ln_rs, y_norm, y_ready, th_ready, mix_ready = (
            sem("astep"), sem("exp_b"), sem("att_ready"), sem("conv_turned"), sem("bn_done"), sem("ln_rs"), sem("y_norm"), sem("y_ready"), sem("th3_ready"), sem("mix3_ready"))
        mix_turned, mt_ready, proj_done, x2_half, x2_ready, ssq_ready, rstd_half, rstd_ready, h2_half, h2_ready = (
            sem("mix_turned"), sem("mt_ready"), sem("proj_done"), sem("x2_half"), sem("x2_ready"), sem("ssq3_ready"), sem("rstd3_half"), sem("rstd3_ready"), sem("h2_half"), sem("h2_ready"))
        h2_turned, h2t_ready, logits_done, rstep, gmax_ready, group_exp, gap_ready, gap_exp, picked, rank_done, counted, slot_ready = (
            sem("h2_turned"), sem("h2t_ready"), sem("logits_done"), sem("rstep"), sem("gmax_ready"), sem("group_exp"), sem("gap_ready"), sem("gap_exp"), sem("picked"),
            sem("rank_done"), sem("counted"), sem("slot_ready"))
        att_half, cstep, w_done, kstep = sem("att_half"), sem("choose_step"), sem("w_done"), sem("rank_step")
        slot_free = sem("slot_free")
        x2_out, h2_out, slot_out, count_psum, count_ready = sem("x2_out"), sem("h2_out"), sem("slot_out"), sem("count_psum"), sem("count_ready")
        DECT = TILES

        with nc.Block() as block:
            @block.sync
            def _(sp):
                for n, (dst, part) in enumerate(((GATE, 2), (GAIN, 4), (SHIFT, 3))):
                    sp.dma_start(dst[:, 0], dr["mod"][DEC:DEC + 1, part * D:(part + 1) * D].to_broadcast([P, D])).then_inc(mods_in, 16)
                    sp.dma_start(dst[0:DEC, 1], dr["mod"][0:DEC, part * D:(part + 1) * D]).then_inc(mods_in, 16)
                sp.dma_start(G2[:], t["g_norm2"].to_broadcast([P, D])).then_inc(mods_in, 16)
                sp.dma_start(LNG[:], t["ln_g"].to_broadcast([P, DCONV])).then_inc(mods_in, 16)
                sp.dma_start(LNB[:], t["ln_b"].to_broadcast([P, DCONV])).then_inc(mods_in, 16)
                sp.dma_start(BR[:, 0:GROUPS], t["b_router_group"].to_broadcast([P, GROUPS])).then_inc(mods_in, 16)
                sp.dma_start(BR[:, GROUPS:], t["b_router_expert"].to_broadcast([P, NEXP])).then_inc(mods_in, 16)

                def load(i, row):
                    sp.dma_start(NB[:], dr["num"].rearrange("b s c -> s b c")[ds(row, P)]).then_inc(br_in, 16)
                    sp.dma_start(ST[:], dr["stat"].rearrange("b s c -> s b c")[ds(row, P)]).then_inc(br_in, 16)
                    sp.dma_start(CC[:], dr["conv"].rearrange("(c p) s -> p c s", p=P)[:, :, ds(row, P)]).then_inc(cc_in, 16)

                load(0, 0)
                sp.dma_start(X[:], t["x_prompt"][0, 0:P]).then_inc(x_in, 16)
                sp.dma_start(WR[:, :, 0:GROUPS], t["w_router_group"][0].rearrange("(k p) n -> p k n", p=P)).then_inc(weights_in, 16)
                sp.dma_start(WR[:, :, GROUPS:], t["w_router_expert"][0].rearrange("(k p) n -> p k n", p=P)).then_inc(weights_in, 16)
                sp.dma_start(WO[:], t["w_out"][0].rearrange("(k p) n -> p k n", p=P)).then_inc(weights_in, 16)
                with sp.Fori(1, TILES) as i:
                    row, behind = sp.snap(i * P), sp.snap((i - 1) * P)
                    sp.wait_ge(conv_turned, i)
                    sp.wait_ge(att_ready, i)
                    load(i, row)
                    sp.wait_ge(x2_ready, i)
                    sp.dma_start(X[:], t["x_prompt"][0, ds(row, P)]).then_inc(x_in, 16)
                    sp.dma_start(dr["x2"][ds(behind, P)], X2[:]).then_inc(x2_out, 16)
                    sp.wait_ge(h2_ready, i)
                    sp.dma_start(dr["h2"][ds(behind, P)], H2[:]).then_inc(h2_out, 16)
                sp.wait_ge(mix_turned, TILES)
                sp.dma_start(MIX[0:DEC], dr["mix"]).then_inc(cc_in, 16)
                sp.wait_ge(x2_ready, TILES)
                sp.dma_start(X[0:DEC], t["x_sample"][:, 0]).then_inc(x_in, 16)
                sp.dma_start(dr["x2"][SEQ - P:SEQ], X2[:]).then_inc(x2_out, 16)
                sp.wait_ge(h2_ready, TILES)
                sp.dma_start(dr["h2"][SEQ - P:SEQ], H2[:]).then_inc(h2_out, 16)
                sp.wait_ge(x2_ready, ALLT)
                sp.dma_start(dr["x2"][SEQ:], X2[0:DEC]).then_inc(x2_out, 16)
                sp.wait_ge(h2_ready, ALLT)
                sp.dma_start(dr["h2"][SEQ:], H2[0:DEC]).then_inc(h2_out, 16)
                sp.wait_ge(x2_out, 16 * ALLT + 16)
                sp.wait_ge(h2_out, 16 * ALLT + 16)

            @block.gpsimd
            def _(pool):
                pool.iota(state["token"][:], [[P, ALLT]], base=0, channel_multiplier=1).then_inc(preset, 1)
                pool.memset(CNT[:], 0.0).then_inc(preset, 1)
                pool.memset(G8[:], -3e38).then_inc(preset, 1)

                def normalise(i):
                    pool.wait_ge(bn_done, i * 2 + 2)
                    pool.tensor_tensor(VE[:], MV[:, 1:2], const("eps"), ALU.add).then_inc(ln_rs, 1)
                    pool.wait_ge(ln_rs, i * 2 + 1)
                    pool.tensor_tensor(RS[:], VE[:], const("neghalf"), ALU.pow).then_inc(ln_rs, 1)
                    pool.wait_ge(y_norm, i * 2 + 1)
                    pool.tensor_tensor(Y[:], Y[:], LNG[:], ALU.mult).then_inc(y_norm, 1)
                    pool.wait_ge(y_norm, i * 2 + 2)
                    pool.tensor_tensor(Y[:], Y[:], LNB[:], ALU.add).then_inc(y_ready, 1)

                def scale(i):
                    pool.wait_ge(ssq_ready, i + 1)
                    pool.tensor_tensor(MS[:], SSQ[:], const("eps"), ALU.add).then_inc(rstd_half, 1)
                    pool.wait_ge(rstd_half, i + 1)
                    pool.tensor_tensor(RSTD[:], MS[:], const("neghalf"), ALU.pow).then_inc(rstd_ready, 1)

                def place(i, rows):
                    pool.tensor_copy(TOK[:], state["token"][:, ds(i, 1)]).then_inc(tok_ready, 1)
                    pool.wait_ge(tok_ready, i + 1)
                    pool.wait_ge(slot_ready, i + 1)
                    pool.sem_inc(placing, 1)
                    for n in range(2):
                        pool.indirect_dma_start(dr["slot"], bass.IndirectOffsetOnAxis(ap=SLOT[0:rows, n:n + 1], axis=0),
                                                TOK[0:rows], None).then_inc(slot_out, 16)
                    pool.wait_ge(slot_out, i * 32 + 32)
                    pool.sem_inc(slot_free, 1)

                pool.wait_ge(mods_in, 16 * 11)
                normalise(0)
                normalise(1)
                scale(0)
                with pool.Fori(1, TILES - 1) as i:
                    normalise(i + 1)
                    scale(i)
                    place(i - 1, P)
                scale(TILES - 1)
                place(TILES - 2, P)
                scale(DECT)
                place(TILES - 1, P)
                place(DECT, DEC)
                pool.wait_ge(slot_out, 16 * 2 * ALLT)

            @block.scalar
            def _(act):
                def branch_weights(i):
                    act.wait_ge(astep, i * 5 + 2)
                    nc.scalar.activation(BW[:], BE[:], ACT.Exp).then_inc(exp_b, 1)

                def swish(i):
                    act.wait_ge(y_ready, i + 1)
                    nc.scalar.activation(TH[:], Y[:], ACT.Tanh, scale=0.5).then_inc(th_ready, 1)

                def take_mix(i):
                    act.wait_ge(mix_turned, i + 1)
                    nc.scalar.copy(MT[:, 0:KD // 2], TPS[:, 0:KD // 2])
                    nc.scalar.mul(MT[:, KD // 2:], TPS[:, KD // 2:], 0.5).then_inc(mt_ready, 1)

                def squares(i, rows):
                    act.wait_ge(x2_ready, i + 1)
                    nc.scalar.activation(SQ[0:rows], X2[0:rows], ACT.Square, scale=D ** -0.5, accum_out=SSQ[0:rows]).then_inc(ssq_ready, 1)

                def take_h2(i):
                    act.wait_ge(h2_turned, i + 1)
                    nc.scalar.copy(H2T[:], TPS[:]).then_inc(h2t_ready, 1)

                def route_exps(i):
                    act.wait_ge(gmax_ready, i + 1)
                    nc.scalar.activation(GE[:], LOG[:, 0:GROUPS], ACT.Exp, bias=NG[:], scale=1.0, accum_out=ZG[:]).then_inc(group_exp, 1)
                    act.wait_ge(gap_ready, i + 1)
                    nc.scalar.activation(EV[:], DV[:], ACT.Exp).then_inc(gap_exp, 1)

                act.sem_inc(x2_out, 16)
                act.sem_inc(h2_out, 16)
                act.sem_inc(slot_free, 1)
                branch_weights(0)
                swish(0)
                take_mix(0)
                branch_weights(1)
                swish(1)
                squares(0, P)
                take_mix(1)
                with act.Fori(1, TILES - 1) as i:
                    take_h2(i - 1)
                    route_exps(i - 1)
                    branch_weights(i + 1)
                    swish(i + 1)
                    squares(i, P)
                    take_mix(i + 1)
                take_h2(TILES - 2)
                route_exps(TILES - 2)
                squares(TILES - 1, P)
                take_mix(DECT)
                take_h2(TILES - 1)
                route_exps(TILES - 1)
                squares(DECT, DEC)
                take_h2(DECT)
                route_exps(DECT)

            @block.vector
            def _(dve):
                def stt(out, in0, scalar, in1, op0, op1):
                    return nc.vector.scalar_tensor_tensor(out=out, in0=in0, scalar=scalar, in1=in1, op0=op0, op1=op1)

                def mix(i):
                    dve.wait_ge(br_in, i * 32 + 32)
                    nc.vector.tensor_reduce(BM[:], ST[:, :, 0:HEADS].rearrange("p b h -> p h b"), AX.X, ALU.max).then_inc(astep, 1)
                    dve.wait_ge(astep, i * 5 + 1)
                    nc.vector.tensor_tensor(BE[:], ST[:, :, 0:HEADS], BM[:, None, :].to_broadcast([P, 3, HEADS]), ALU.subtract).then_inc(astep, 1)
                    dve.wait_ge(conv_turned, i + 1)
                    nc.vector.bn_stats(BS[:], CP[:].rearrange("p c t -> p (c t)")).then_inc(bn_done, 1)
                    dve.wait_ge(bn_done, i * 2 + 1)
                    nc.vector.memset(PAUSE[:], 0.0)
                    nc.vector.bn_aggr(MV[:], BS[:]).then_inc(bn_done, 1)
                    dve.wait_ge(exp_b, i + 1)
                    nc.vector.tensor_tensor(BT[:], BW[:], ST[:, :, HEADS:], ALU.mult).then_inc(astep, 1)
                    dve.wait_ge(astep, i * 5 + 3)
                    nc.vector.tensor_reduce(BD[:], BT[:].rearrange("p b h -> p h b"), AX.X, ALU.add).then_inc(astep, 1)
                    dve.wait_ge(astep, i * 5 + 4)
                    nc.vector.reciprocal(BRC[:], BD[:]).then_inc(astep, 1)
                    dve.wait_ge(ln_rs, i * 2 + 2)
                    nc.vector.tensor_scalar(Y[:], CP[:].rearrange("p c t -> p (c t)"), MV[:, 0:1], RS[:], ALU.subtract, ALU.mult).then_inc(y_norm, 1)
                    dve.wait_ge(astep, i * 5 + 5)
                    nc.vector.tensor_tensor(BT[:], BW[:], BRC[:, None, :].to_broadcast([P, 3, HEADS]), ALU.mult).then_inc(att_half, 1)
                    dve.wait_ge(att_half, i * 3 + 1)
                    nb = NB[:].rearrange("p b (h e) -> p (b h) e", e=DH)
                    nc.vector.tensor_tensor(nb, nb, BT[:].rearrange("p b h -> p (b h)")[:, :, None].to_broadcast([P, 3 * HEADS, DH]), ALU.mult).then_inc(att_half, 1)
                    dve.wait_ge(att_half, i * 3 + 2)
                    nc.vector.tensor_tensor(NB[:, 0], NB[:, 0], NB[:, 1], ALU.add).then_inc(att_half, 1)
                    dve.wait_ge(att_half, i * 3 + 3)
                    nc.vector.tensor_tensor(MIX[:, 0:DATT], NB[:, 0], NB[:, 2], ALU.add).then_inc(att_ready, 1)
                    dve.wait_ge(th_ready, i + 1)
                    stt(MIX[:, DATT:], TH[:], 1.0, Y[:], ALU.add, ALU.mult).then_inc(mix_ready, 1)

                def residual(i, rows, which):
                    dve.wait_ge(proj_done, i + 1)
                    dve.wait_ge(x_in, i * 16 + 16)
                    dve.wait_ge(x2_out, i * 16 + 16)
                    nc.vector.tensor_tensor(X2[0:rows], OP[0:rows], GATE[0:rows, which], ALU.mult).then_inc(x2_half, 1)
                    dve.wait_ge(x2_half, i + 1)
                    nc.vector.tensor_tensor(X2[0:rows], X2[0:rows], X[0:rows], ALU.add).then_inc(x2_ready, 1)
                    dve.wait_ge(rstd_ready, i + 1)
                    dve.wait_ge(h2_out, i * 16 + 16)
                    stt(H2[0:rows], X2[0:rows], RSTD[0:rows], GAIN[0:rows, which], ALU.mult, ALU.mult).then_inc(h2_half, 1)
                    dve.wait_ge(h2_half, i + 1)
                    nc.vector.tensor_tensor(H2[0:rows], H2[0:rows], SHIFT[0:rows, which], ALU.add).then_inc(h2_ready, 1)

                RST = 10

                def route(i):
                    at = [0]

                    def step(ins):
                        at[0] += 1
                        ins.then_inc(rstep, 1)
                        dve.wait_ge(rstep, i * RST + at[0])

                    dve.wait_ge(logits_done, i + 1)
                    step(nc.vector.tensor_tensor(LOG[:], LP[:], BR[:], ALU.add))
                    step(nc.vector.tensor_copy(G8[:, 0:GROUPS], LOG[:, 0:GROUPS]))
                    nc.vector.memset(PAUSE[:], 0.0)
                    step(nc.vector.max(GM[:], G8[:]))
                    nc.vector.tensor_scalar(NG[:], GM[:, 0:1], -1.0, None, ALU.mult).then_inc(gmax_ready, 1)
                    step(nc.vector.max_index(GI[:], GM[:], G8[:]))
                    step(nc.vector.tensor_copy(GF[:], GI[:, 0:1]))
                    step(nc.vector.tensor_scalar(OG[:], const("iota")[:, 0:GROUPS], GF[:], None, ALU.is_equal))
                    step(nc.vector.tensor_tensor(LS[:], LOG[:, GROUPS:].rearrange("p (g e) -> p g e", e=PER), OG[:, :, None].to_broadcast([P, GROUPS, PER]), ALU.mult))
                    step(nc.vector.tensor_reduce(L8[:], LS[:].rearrange("p g e -> p e g"), AX.X, ALU.add))
                    nc.vector.memset(PAUSE[:], 0.0)
                    step(nc.vector.max(V8[:], L8[:]))
                    nc.vector.tensor_tensor(DV[:], V8[:, 1:2], V8[:, 0:1], ALU.subtract).then_inc(gap_ready, 1)
                    step(nc.vector.max_index(I8[:], V8[:], L8[:]))
                    assert at[0] == RST

                def choose(i):
                    nc.vector.tensor_copy(I2[:], I8[:, 0:2]).then_inc(cstep, 1)
                    dve.wait_ge(cstep, i * 5 + 1)
                    stt(EID[:], GF[:].to_broadcast([P, 2]), float(PER), I2[:], ALU.mult, ALU.add).then_inc(cstep, 1)
                    dve.wait_ge(cstep, i * 5 + 2)
                    nc.vector.tensor_tensor(OH[:], const("iota")[:, None, :].to_broadcast([P, 2, NEXP]), EID[:, :, None].to_broadcast([P, 2, NEXP]), ALU.is_equal).then_inc(cstep, 1)
                    dve.wait_ge(cstep, i * 5 + 3)
                    nc.vector.tensor_tensor(A[:], OH[:, 0], OH[:, 1], ALU.add).then_inc(picked, 1)
                    dve.wait_ge(gap_exp, i + 1)
                    stt(DEN[:], EV[:], 1.0, ZG[:], ALU.add, ALU.mult).then_inc(cstep, 1)
                    dve.wait_ge(cstep, i * 5 + 4)
                    nc.vector.reciprocal(W1[:, 0:1], DEN[:]).then_inc(cstep, 1)
                    dve.wait_ge(cstep, i * 5 + 5)
                    nc.vector.tensor_tensor(W1[:, 1:2], W1[:, 0:1], EV[:], ALU.mult).then_inc(w_done, 1)
                    dve.wait_ge(w_done, i * 3 + 1)
                    nc.vector.tensor_copy(state["weight"][:, ds(i, 1)] if not isinstance(i, int) else state["weight"][:, i:i + 1], W1[:, None, :]).then_inc(w_done, 1)
                    nc.vector.tensor_copy(state["expert"][:, ds(i, 1)] if not isinstance(i, int) else state["expert"][:, i:i + 1], EID[:, None, :]).then_inc(w_done, 1)

                def rank(i, rows):
                    dve.wait_ge(rank_done, i + 1)
                    nc.vector.tensor_tensor(CNT[0:rows], CNT[0:rows], A[0:rows], ALU.add).then_inc(counted, 1)
                    nc.vector.tensor_tensor(RSEL[:], OH[:], RP[:, None, :].to_broadcast([P, 2, NEXP]), ALU.mult).then_inc(kstep, 1)
                    dve.wait_ge(kstep, i * 3 + 1)
                    nc.vector.tensor_reduce(R2[:], RSEL[:], AX.X, ALU.add).then_inc(kstep, 1)
                    dve.wait_ge(kstep, i * 3 + 2)
                    nc.vector.tensor_copy(state["rank"][:, ds(i, 1)] if not isinstance(i, int) else state["rank"][:, i:i + 1], R2[:, None, :]).then_inc(kstep, 1)
                    dve.wait_ge(slot_free, i + 1)
                    stt(SLOT[:], EID[:], float(CAP), R2[:], ALU.mult, ALU.add).then_inc(slot_ready, 1)
                    dve.wait_ge(counted, i + 1)

                dve.wait_ge(mods_in, 16 * 11)
                stt(GAIN[:, 0], GAIN[:, 0], 1.0, G2[:], ALU.add, ALU.mult).then_inc(gain_ready, 1)
                stt(GAIN[0:DEC, 1], GAIN[0:DEC, 1], 1.0, G2[0:DEC], ALU.add, ALU.mult).then_inc(gain_ready, 1)
                dve.wait_ge(gain_ready, 2)
                dve.wait_ge(preset, 3)
                mix(0)
                dve.wait_ge(mix_turned, 1)
                mix(1)
                residual(0, P, 0)
                with dve.Fori(1, TILES - 1) as i:
                    route(i - 1)
                    choose(i - 1)
                    dve.wait_ge(mix_turned, i + 1)
                    mix(i + 1)
                    residual(i, P, 0)
                    rank(i - 1, P)
                route(TILES - 2)
                choose(TILES - 2)
                residual(TILES - 1, P, 0)
                rank(TILES - 2, P)
                route(TILES - 1)
                choose(TILES - 1)
                residual(DECT, DEC, 1)
                rank(TILES - 1, P)
                route(DECT)
                choose(DECT)
                rank(DECT, DEC)
                dve.wait_ge(count_psum, 1)
                nc.vector.tensor_copy(state["count"][:], NP_[:]).then_inc(count_ready, 1)

            @block.tensor
            def _(pe):
                def turn_conv(i):
                    pe.wait_ge(cc_in, i * 16 + 16)
                    if not (isinstance(i, int) and i == 0):
                        pe.wait_ge(y_norm, i * 2)
                    for c in range(KC):
                        mm = nc.tensor.transpose(CP[:, c], CC[:, c], const("ident"))
                    mm.then_inc(conv_turned, 1)

                def turn_mix(i, dec=False):
                    if dec:
                        pe.wait_ge(cc_in, 16 * ALLT)
                    else:
                        pe.wait_ge(mix_ready, i + 1)
                        pe.wait_ge(att_ready, i + 1)
                    for k in range(KD):
                        mm = nc.tensor.transpose(TPS[:, k], MIX[:, k * P:(k + 1) * P], const("ident"))
                    mm.then_inc(mix_turned, 1)

                def project(i):
                    pe.wait_ge(mt_ready, i + 1)
                    if not (isinstance(i, int) and i == 0):
                        pe.wait_ge(x2_half, i)
                    for n in range(D // 512):
                        for k in range(KD):
                            mm = nc.tensor.matmul(OP[:, n * 512:(n + 1) * 512], MT[:, k], WO[:, k, n * 512:(n + 1) * 512], start=k == 0, stop=k == KD - 1)
                    mm.then_inc(proj_done, 1)

                def logits(i):
                    pe.wait_ge(h2_ready, i + 1)
                    if not (isinstance(i, int) and i == DECT):
                        pe.wait_ge(mt_ready, i + 2)
                    for k in range(KD):
                        mm = nc.tensor.transpose(TPS[:, k], H2[:, k * P:(k + 1) * P], const("ident"))
                    mm.then_inc(h2_turned, 1)
                    pe.wait_ge(h2t_ready, i + 1)
                    for k in range(KD):
                        mm = nc.tensor.matmul(LP[:], H2T[:, k], WR[:, k], start=k == 0, stop=k == KD - 1)
                    mm.then_inc(logits_done, 1)

                def ranks(i, rows):
                    pe.wait_ge(picked, i + 1)
                    if not (isinstance(i, int) and i == 0):
                        pe.wait_ge(counted, i)
                        pe.wait_ge(kstep, i * 3)
                    nc.tensor.matmul(RP[:], const("before", rows), A[0:rows], start=True, stop=False)
                    nc.tensor.matmul(RP[:], const("ones"), CNT[:], start=False, stop=True).then_inc(rank_done, 1)

                turn_conv(0)
                turn_mix(0)
                turn_conv(1)
                pe.wait_ge(weights_in, 48)
                project(0)
                turn_mix(1)
                with pe.Fori(1, TILES - 1) as i:
                    logits(i - 1)
                    turn_conv(i + 1)
                    project(i)
                    ranks(i - 1, P)
                    turn_mix(i + 1)
                logits(TILES - 2)
                project(TILES - 1)
                ranks(TILES - 2, P)
                turn_mix(DECT, dec=True)
                logits(TILES - 1)
                project(DECT)
                ranks(TILES - 1, P)
                logits(DECT)
                ranks(DECT, DEC)
                pe.wait_ge(counted, ALLT)
                nc.tensor.matmul(NP_[:], const("ones"), CNT[:], start=True, stop=True).then_inc(count_psum, 1)



def expert_tables(nc, const, state):
    with ExitStack() as ctx:
        def sb(name, shape, dt=F32):
            return ctx.enter_context(nc.sbuf_tensor(name, shape, dt))

        CMP, NBLK, LOW, START, END = sb("CMP", [P, NEXP, 16]), sb("NBLK", [P, NEXP]), sb("LOW", [P, NEXP, NEXP]), sb("START", [P, NEXP]), sb("END", [P, NEXP])
        SEL, BASE = sb("SEL", [P, ALLT * 2, NEXP]), sb("BASE", [P, ALLT * 2])
        step = stage_semaphores(nc, ctx)("table_step")
        with nc.Block() as block:
            @block.vector
            def _(dve):
                at = [0]

                def chain(ins):
                    at[0] += 1
                    ins.then_inc(step, 1)
                    dve.wait_ge(step, at[0])

                chain(nc.vector.tensor_tensor(CMP[:], state["count"][:, :, None].to_broadcast([P, NEXP, 16]),
                                              const("thresholds")[:, None, :].to_broadcast([P, NEXP, 16]), ALU.is_gt))
                chain(nc.vector.tensor_reduce(NBLK[:], CMP[:], AX.X, ALU.add))
                chain(nc.vector.tensor_scalar(NBLK[:], NBLK[:], 1.0, None, ALU.add))
                chain(nc.vector.tensor_tensor(LOW[:], const("lower").rearrange("p (a b) -> p a b", b=NEXP), NBLK[:, None, :].to_broadcast([P, NEXP, NEXP]), ALU.mult))
                chain(nc.vector.tensor_reduce(START[:], LOW[:], AX.X, ALU.add))
                chain(nc.vector.tensor_tensor(END[:], START[:], NBLK[:], ALU.add))
                chain(nc.vector.tensor_copy(state["blocks"][:, 0:NEXP], START[:]))
                chain(nc.vector.tensor_copy(state["blocks"][:, NEXP:], END[:]))
                expert = state["expert"][:].rearrange("p t n -> p (t n)")
                chain(nc.vector.tensor_tensor(SEL[:], const("iota")[:, None, :].to_broadcast([P, ALLT * 2, NEXP]),
                                              expert[:, :, None].to_broadcast([P, ALLT * 2, NEXP]), ALU.is_equal))
                chain(nc.vector.tensor_tensor(SEL[:], SEL[:], START[:, None, :].to_broadcast([P, ALLT * 2, NEXP]), ALU.mult))
                chain(nc.vector.tensor_reduce(BASE[:], SEL[:], AX.X, ALU.add))
                chain(nc.vector.scalar_tensor_tensor(out=state["dest"][:].rearrange("p t n -> p (t n)"), in0=BASE[:], scalar=float(P),
                                                     in1=state["rank"][:].rearrange("p t n -> p (t n)"), op0=ALU.mult, op1=ALU.add))


def experts(nc, t, dr, const, state):
    with ExitStack() as ctx:
        def sb(name, shape, dt=F32):
            return ctx.enter_context(nc.sbuf_tensor(name, shape, dt))

        def ps(name, shape):
            return ctx.enter_context(nc.psum_tensor(name, shape, F32))

        sem = stage_semaphores(nc, ctx)

        W1, W3, W2 = sb("W1E", [P, KD, DEXP]), sb("W3E", [P, KD, DEXP]), sb("W2E", [P, KF, D])
        fetching = sem("fetching")
        NOROWS = sb("NOROWS", [P, D])
        norows_set, norows_out = sem("norows_set"), sem("norows_out")
        IDX, XG, XT = sb("IDX", [P, 1], I32), sb("XG", [P, D]), sb("XT", [P, KD, P])
        S, G, GT, Y = sb("SE", [P, DEXP]), sb("GE5", [P, DEXP]), sb("GTE", [P, KF, P]), sb("YE", [P, D])
        XP, AP_, BP, GP, YP = ps("XP", [P, KD, P]), ps("AE", [P, DEXP]), ps("BE5", [P, DEXP]), ps("GP", [P, KF, P]), ps("YP", [P, D])
        w1_in, w3_in, w2_in, idx_in, x_in = sem("gate_w_in"), sem("up_w_in"), sem("down_w_in"), sem("idx_in"), sem("xg_in")
        x_turned, xt_ready, a_done, b_done, s_ready, g_ready, g_turned, gt_ready, y_done, y_right, y_left, y_out = (
            sem("x_turned"), sem("xt_ready"), sem("a_done"), sem("b_done"), sem("s_ready"), sem("g_ready"), sem("g_turned"), sem("gt_ready"), sem("y_done"),
            sem("y_right"), sem("y_left"), sem("yrows_out"))
        table = state["blocks"]

        def bounds(engine, e):
            first = engine.value_load(table[0:1, ds(e, 1)], min_val=0, max_val=MAXBLK)
            end = engine.value_load(table[0:1, ds(e + NEXP, 1)], min_val=1, max_val=MAXBLK)
            return first, end

        with nc.Block() as block:
            @block.sync
            def _(sp):
                w1, w3 = (t[n][0].rearrange("e (k p) f -> e p k f", p=P) for n in ("w_expert_gate", "w_expert_up"))
                w2 = t["w_expert_down"][0].rearrange("e (k p) d -> e p k d", p=P)
                with sp.Fori(0, NEXP) as e:
                    first = sp.value_load(table[0:1, ds(e, 1)], min_val=0, max_val=MAXBLK)
                    used = sp.snap(first + 1)
                    for dst, src, done, come in ((W1, w1, a_done, w1_in), (W3, w3, b_done, w3_in), (W2, w2, y_done, w2_in)):
                        sp.wait_ge(done, used)
                        sp.dma_start(dst[:], src[ds(e, 1)].rearrange("a p k f -> (a p) k f")).then_inc(come, 16)

            @block.gpsimd
            def _(pool):
                def gather(b):
                    pool.wait_ge(x_turned, b + 1)
                    pool.sem_inc(fetching, 1)
                    pool.indirect_dma_start(XG[:], None, dr["h2"], bass.IndirectOffsetOnAxis(ap=IDX[:].bitcast(U32), axis=0)).then_inc(x_in, 16)

                with pool.Fori(0, NEXP) as e:
                    first, end = bounds(pool, e)
                    with pool.Fori(first, end) as b:
                        slot = nc.s_assert_within(pool.snap(e * CAP + (b - first) * P), 0, NEXP * CAP - P,
                                                  skip_runtime_bounds_check_because="an expert's blocks stay inside its CAP slots")
                        pool.dma_start(IDX[:], dr["slot"][ds(slot, P), :]).then_inc(idx_in, 16)
                        pool.wait_ge(idx_in, b * 16 + 16)
                        gather(b)
                        pool.wait_ge(x_in, b * 16 + 16)
                blocks = pool.value_load(table[0:1, 2 * NEXP - 1:2 * NEXP], min_val=1, max_val=MAXBLK)
                gather(blocks)

            @block.scalar
            def _(act):
                act.sem_inc(y_out, 16)
                act.sem_inc(y_left, 1)
                blocks = act.value_load(table[0:1, 2 * NEXP - 1:2 * NEXP], min_val=1, max_val=MAXBLK)
                act.wait_ge(norows_set, 1)
                with act.Fori(blocks, MAXBLK) as b:
                    act.dma_start(dr["y"][ds(act.snap(b * P), P)], NOROWS[:]).then_inc(norows_out, 16)

                def take_x(b):
                    act.wait_ge(x_turned, b + 2)
                    nc.scalar.copy(XT[:], XP[:]).then_inc(xt_ready, 1)

                take_x(0)
                with act.Fori(0, NEXP) as e:
                    first, end = bounds(act, e)
                    with act.Fori(first, end) as b:
                        row = act.snap(b * P)
                        act.wait_ge(a_done, b + 2)
                        nc.scalar.activation(S[:], AP_[:], ACT.Silu).then_inc(s_ready, 1)
                        take_x(b + 1)
                        act.wait_ge(y_done, b + 2)
                        act.wait_ge(y_out, b * 16 + 16)
                        nc.scalar.copy(Y[:, 0:D // 2], YP[:, 0:D // 2]).then_inc(y_left, 1)
                        act.wait_ge(y_left, b + 2)
                        act.wait_ge(y_right, b + 2)
                        act.dma_start(dr["y"][ds(row, P)], Y[:]).then_inc(y_out, 16)
                        act.sem_inc(norows_out, 16)
                act.wait_ge(norows_out, MAXBLK * 16)
                act.wait_ge(y_out, blocks * 16 + 16)
                act.sem_inc(y_left, 1)

            @block.vector
            def _(dve):
                dve.sem_inc(y_right, 1)
                nc.vector.memset(NOROWS[:], 0.0).then_inc(norows_set, 1)
                with dve.Fori(0, NEXP) as e:
                    first, end = bounds(dve, e)
                    with dve.Fori(first, end) as b:
                        dve.wait_ge(s_ready, b + 1)
                        dve.wait_ge(b_done, b + 2)
                        nc.vector.tensor_tensor(G[:], S[:], BP[:], ALU.mult).then_inc(g_ready, 1)
                        dve.wait_ge(g_turned, b + 1)
                        nc.vector.tensor_copy(GT[:], GP[:]).then_inc(gt_ready, 1)
                        dve.wait_ge(y_done, b + 2)
                        dve.wait_ge(y_out, b * 16 + 16)
                        nc.vector.tensor_copy(Y[:, D // 2:], YP[:, D // 2:]).then_inc(y_right, 1)

            @block.tensor
            def _(pe):
                for s in (x_turned, a_done, b_done, y_done):
                    pe.sem_inc(s, 1)

                def turn_x(b):
                    pe.wait_ge(x_in, b * 16 + 16)
                    for k in range(KD):
                        mm = nc.tensor.transpose(XP[:, k], XG[:, k * P:(k + 1) * P], const("ident"))
                    mm.then_inc(x_turned, 1)

                turn_x(0)
                with pe.Fori(0, NEXP) as e:
                    first, end = bounds(pe, e)
                    with pe.Fori(first, end) as b:
                        pe.wait_ge(w1_in, e * 16 + 16)
                        pe.wait_ge(xt_ready, b + 1)
                        for k in range(KD):
                            mm = nc.tensor.matmul(AP_[:], XT[:, k], W1[:, k], start=k == 0, stop=k == KD - 1)
                        mm.then_inc(a_done, 1)
                        pe.wait_ge(w3_in, e * 16 + 16)
                        for k in range(KD):
                            mm = nc.tensor.matmul(BP[:], XT[:, k], W3[:, k], start=k == 0, stop=k == KD - 1)
                        mm.then_inc(b_done, 1)
                        turn_x(b + 1)
                        pe.wait_ge(g_ready, b + 1)
                        for k in range(KF):
                            mm = nc.tensor.transpose(GP[:, k], G[:, k * P:(k + 1) * P], const("ident"))
                        mm.then_inc(g_turned, 1)
                        pe.wait_ge(w2_in, e * 16 + 16)
                        pe.wait_ge(gt_ready, b + 1)
                        pe.wait_ge(y_right, b + 1)
                        pe.wait_ge(y_left, b + 1)
                        for n in range(D // 512):
                            for k in range(KF):
                                mm = nc.tensor.matmul(YP[:, n * 512:(n + 1) * 512], GT[:, k], W2[:, k, n * 512:(n + 1) * 512], start=k == 0, stop=k == KF - 1)
                        mm.then_inc(y_done, 1)


def combine_and_normalise(nc, t, dr, const, state):
    with ExitStack() as ctx:
        def sb(name, shape, dt=F32):
            return ctx.enter_context(nc.sbuf_tensor(name, shape, dt))

        sem = stage_semaphores(nc, ctx)

        GATE, GF = sb("GATE6", [P, 2, D]), sb("GF6", [P, D])
        X, Y1, Y2, V, OUT, SQ = (sb("X6", [P, 2, D]), sb("Y16", [P, 2, D]), sb("Y26", [P, 2, D]), sb("V6", [P, 2, D]), sb("OUT6", [P, 2, D]), sb("SQ6", [P, D]))
        SSQ, MS, RSTD, DST = sb("SSQ6", [P, 2]), sb("MS6", [P, 2]), sb("RSTD6", [P, 2]), sb("DST6", [P, 2, 2], U32)
        fetching = sem("fetching6")
        mods_in = sem("mods6_in")
        x_in, y1_in, y2_in, out_out = ([sem(f"{n}6_{p}") for p in range(2)] for n in ("x_in", "y1_in", "y2_in", "out_out"))
        dst_ready, first_scaled, both_added, gated, sum_ready, ssq_ready, rstd_half, rstd_ready, out_ready = (
            sem("dst_ready"), sem("first_scaled"), sem("both_added"), sem("gated"), sem("sum_ready"), sem("ssq6"), sem("rstd6_half"), sem("rstd6"), sem("out6"))
        DECT = TILES
        PAIRS = TILES // 2

        def weight(tile, n, rows):
            return state["weight"][0:rows, ds(tile, 1), n:n + 1].rearrange("p a n -> p (a n)")

        with nc.Block() as block:
            @block.sync
            def _(sp):
                for p in range(2):
                    sp.dma_start(X[:, p], dr["x2"][p * P:(p + 1) * P]).then_inc(x_in[p], 16)
                sp.dma_start(GATE[:, 0], dr["mod"][DEC:DEC + 1, 5 * D:].to_broadcast([P, D])).then_inc(mods_in, 16)
                sp.dma_start(GATE[0:DEC, 1], dr["mod"][0:DEC, 5 * D:]).then_inc(mods_in, 16)
                sp.dma_start(GF[:], t["g_final"].to_broadcast([P, D])).then_inc(mods_in, 16)
                with sp.Fori(0, PAIRS - 1) as i:
                    for p in range(2):
                        row, ahead = sp.snap((i * 2 + p) * P), sp.snap((i * 2 + p + 2) * P)
                        sp.wait_ge(sum_ready, i * 2 + p + 1)
                        sp.dma_start(X[:, p], dr["x2"][ds(ahead, P)]).then_inc(x_in[p], 16)
                        sp.wait_ge(out_ready, i * 2 + p + 3)
                        sp.dma_start(t["y_prompt"][ds(row, P)], OUT[:, p]).then_inc(out_out[p], 16)
                sp.wait_ge(sum_ready, TILES - 1)
                sp.dma_start(X[0:DEC, 0], dr["x2"][SEQ:]).then_inc(x_in[0], 16)
                for p in range(2):
                    sp.wait_ge(out_ready, TILES + 1 + p)
                    sp.dma_start(t["y_prompt"][SEQ - (2 - p) * P:SEQ - (1 - p) * P], OUT[:, p]).then_inc(out_out[p], 16)
                sp.wait_ge(out_ready, ALLT + 2)
                sp.dma_start(t["y_sample"], OUT[0:DEC, 0]).then_inc(out_out[0], 16)
                sp.wait_ge(out_out[0], 16 * (PAIRS + 1) + 16)
                sp.wait_ge(out_out[1], 16 * PAIRS + 16)

            @block.gpsimd
            def _(pool):
                def fetch(p, tile, rows):
                    pool.tensor_copy(DST[:, p], state["dest"][:, ds(tile, 1)].rearrange("p a n -> p (a n)")).then_inc(dst_ready, 1)
                    pool.wait_ge(dst_ready, tile + 1)
                    pool.sem_inc(fetching, 1)
                    for n, (y, come) in enumerate(((Y1, y1_in), (Y2, y2_in))):
                        pool.indirect_dma_start(y[0:rows, p], None, dr["y"], bass.IndirectOffsetOnAxis(ap=DST[0:rows, p, n:n + 1], axis=0)).then_inc(come[p], 16)

                def scale(p, tile):
                    pool.wait_ge(ssq_ready, tile + 1)
                    pool.tensor_tensor(MS[:, p:p + 1], SSQ[:, p:p + 1], const("eps"), ALU.add).then_inc(rstd_half, 1)
                    pool.wait_ge(rstd_half, tile + 1)
                    pool.tensor_tensor(RSTD[:, p:p + 1], MS[:, p:p + 1], const("neghalf"), ALU.pow).then_inc(rstd_ready, 1)

                fetch(0, 0, P)
                fetch(1, 1, P)
                with pool.Fori(0, PAIRS - 1) as i:
                    for p in range(2):
                        pool.wait_ge(both_added, i * 2 + p + 1)
                        fetch(p, i * 2 + p + 2, P)
                        scale(p, i * 2 + p)
                pool.wait_ge(both_added, TILES - 1)
                fetch(0, DECT, DEC)
                for tile in range(TILES - 2, ALLT):
                    scale(tile % 2, tile)

            @block.scalar
            def _(act):
                for p in range(2):
                    act.sem_inc(out_out[p], 16)

                def first(i, p, tile, rows):
                    act.wait_ge(y1_in[p], i * 16 + 16)
                    act.wait_ge(out_ready, tile + 1)
                    nc.scalar.activation(V[0:rows, p], Y1[0:rows, p], ACT.Copy, scale=weight(tile, 0, rows)).then_inc(first_scaled, 1)

                def squares(p, tile, rows):
                    act.wait_ge(sum_ready, tile + 1)
                    nc.scalar.activation(SQ[0:rows], V[0:rows, p], ACT.Square, scale=D ** -0.5, accum_out=SSQ[0:rows, p:p + 1]).then_inc(ssq_ready, 1)

                first(0, 0, 0, P)
                with act.Fori(0, PAIRS - 1) as i:
                    first(i, 1, i * 2 + 1, P)
                    squares(0, i * 2, P)
                    first(i + 1, 0, i * 2 + 2, P)
                    squares(1, i * 2 + 1, P)
                first(PAIRS - 1, 1, TILES - 1, P)
                squares(0, TILES - 2, P)
                first(PAIRS, 0, DECT, DEC)
                squares(1, TILES - 1, P)
                act.wait_ge(ssq_ready, TILES)
                squares(0, DECT, DEC)

            @block.vector
            def _(dve):
                dve.sem_inc(out_ready, 2)

                def add(i, p, tile, rows, which):
                    v = V[0:rows, p]
                    dve.wait_ge(first_scaled, tile + 1)
                    dve.wait_ge(y2_in[p], i * 16 + 16)
                    nc.vector.scalar_tensor_tensor(out=v, in0=Y2[0:rows, p], scalar=weight(tile, 1, rows), in1=v, op0=ALU.mult, op1=ALU.add).then_inc(both_added, 1)
                    dve.wait_ge(both_added, tile + 1)
                    nc.vector.tensor_tensor(v, v, GATE[0:rows, which], ALU.mult).then_inc(gated, 1)
                    dve.wait_ge(gated, tile + 1)
                    dve.wait_ge(x_in[p], i * 16 + 16)
                    nc.vector.tensor_tensor(v, v, X[0:rows, p], ALU.add).then_inc(sum_ready, 1)

                def finish(i, p, tile, rows):
                    dve.wait_ge(rstd_ready, tile + 1)
                    dve.wait_ge(out_out[p], i * 16 + 16)
                    nc.vector.scalar_tensor_tensor(out=OUT[0:rows, p], in0=V[0:rows, p], scalar=RSTD[0:rows, p:p + 1], in1=GF[0:rows], op0=ALU.mult, op1=ALU.mult).then_inc(out_ready, 1)

                dve.wait_ge(mods_in, 48)
                add(0, 0, 0, P, 0)
                with dve.Fori(0, PAIRS - 1) as i:
                    add(i, 1, i * 2 + 1, P, 0)
                    finish(i, 0, i * 2, P)
                    add(i + 1, 0, i * 2 + 2, P, 0)
                    finish(i, 1, i * 2 + 1, P)
                add(PAIRS - 1, 1, TILES - 1, P, 0)
                finish(PAIRS - 1, 0, TILES - 2, P)
                add(PAIRS, 0, DECT, DEC, 1)
                finish(PAIRS - 1, 1, TILES - 1, P)
                finish(PAIRS, 0, DECT, DEC)


OUTPUTS = {
    "y_prompt": (1, SEQ, D), "y_sample": (DEC, 1, D),
    "new_k_prompt": (1, 1, WIN, HEADS, DH), "new_v_prompt": (1, 1, WIN, HEADS, DH), "new_conv_prompt": (1, 1, TAPS - 1, DCONV),
    "new_k_sample": (1, DEC, WIN, HEADS, DH), "new_v_sample": (1, DEC, WIN, HEADS, DH), "new_conv_sample": (1, DEC, TAPS - 1, DCONV),
}
FLAT = {
    "y_prompt": "a s d -> (a s) d", "y_sample": "b a d -> (b a) d",
    "new_k_prompt": "a b s h e -> (a b s) (h e)", "new_v_prompt": "a b s h e -> (a b s) (h e)", "new_conv_prompt": "a b s c -> (a b s) c",
    "new_k_sample": "a b s h e -> (a b) (s h e)", "new_v_sample": "a b s h e -> (a b) (s h e)", "new_conv_sample": "a b s c -> (a b) (s c)",
    "cache_k": "a b s h e -> (a b) (s h e)", "cache_v": "a b s h e -> (a b) (s h e)", "state_conv": "a b s c -> (a b) (s c)",
}


def layout(nc, inputs):
    arrays, t, outs = {}, {}, {}
    given = {name: np.ascontiguousarray(a) for name, a in inputs.items()}
    given["constants"] = constant_columns()[1]
    given["g_final"] = given["g_final"].reshape(1, D)
    for name, a in given.items():
        arrays[f"in_{name}"] = a
        ap = nc.dram_tensor(f"in_{name}", a.shape, mybir.dt.from_np(a.dtype), kind="ExternalInput").ap()
        t[name] = ap.rearrange(FLAT[name]) if name in FLAT else ap
    for name, shape in OUTPUTS.items():
        outs[name] = f"out_{name}"
        t[name] = nc.dram_tensor(outs[name], shape, F32, kind="ExternalOutput").ap().rearrange(FLAT[name])
    return arrays, t, outs


def kernel(**inputs):
    import concourse.bacc as bacc
    from concourse.bass_utils import run_bass_kernel_spmd

    nc = bacc.Bacc("TRN2", target_bir_lowering=False, num_devices=1)
    arrays, t, outs = layout(nc, inputs)
    decoder_step(nc, t, constant_columns()[0])
    r = run_bass_kernel_spmd(nc, [arrays], core_ids=[0])
    return tuple(r.results[0][outs[name]] for name in OUTPUTS)
```

```python
from contextlib import ExitStack
import math

import numpy as np
import concourse.bass as bass
import concourse.mybir as mybir
from concourse.alu_op_type import AluOpType as ALU

F32 = mybir.dt.float32
F32R = mybir.dt.float32r
I32 = mybir.dt.int32
U32 = mybir.dt.uint32
ACT = mybir.ActivationFunctionType
AX = mybir.AxisListType
ds = bass.ds

P = 128
SEQ = 2048
DEC = 8
D = 1024
KD = D // P
HEADS = 8
DH = 64
DATT = HEADS * DH
DCONV = D - DATT
KC = DCONV // P
DIN = 3 * DATT + 2 * DCONV
TAPS = 31
DILATIONS = (1, 4, 16)
WSUB = 128
WIN = 2048
BUCKETS = 32
GROUPS = 4
PER = 8
NEXP = GROUPS * PER
DEXP = 512
KF = DEXP // P
EPS = 1e-6
NEG = -1e30
TILES = SEQ // P
ALLT = TILES + 1
ROWS = SEQ + DEC
CAP = (ROWS + P - 1) // P * P
MAXBLK = NEXP + (2 * ROWS) // P + 1
VEC = 384
NUMW = DATT + 2 * HEADS


def t5_bucket(dist):
    n = np.maximum(np.asarray(dist), 0)
    half = BUCKETS // 2
    nf = np.maximum(n, 1).astype(np.float32)
    large = half + (np.log(nf / np.float32(half)) / np.float32(math.log(WIN / half)) * (BUCKETS - half)).astype(np.int32)
    return np.where(n < half, n, np.minimum(large, BUCKETS - 1))


def constant_columns():
    parts = {}
    parts["ident"] = np.eye(P)
    parts["before"] = np.triu(np.ones((P, P)), 1)
    parts["ones"] = np.ones((P, P))
    band = np.zeros((P, len(DILATIONS) * VEC))
    for b, dil in enumerate(DILATIONS):
        for x in range(VEC):
            rel = 255 - x
            if 0 <= rel <= WSUB:
                band[t5_bucket(rel * dil), b * VEC + x] = 1.0
            else:
                band[BUCKETS, b * VEC + x] = NEG
    parts["band"] = band
    dec = np.zeros((P, 3 * P + 3))
    for b, dil in enumerate(DILATIONS):
        for j in range(1, WSUB + 1):
            dec[t5_bucket(j * dil), b * P + WSUB - j] = 1.0
        dec[0, 3 * P + b] = 1.0
    parts["decband"] = dec
    parts["neghalf"] = np.full((P, 1), -0.5)
    parts["eps"] = np.full((P, 1), EPS)
    parts["iota"] = np.tile(np.arange(NEXP), (P, 1))
    parts["thresholds"] = np.tile(np.arange(1, 17) * P, (P, 1))
    parts["lower"] = np.tile((np.arange(NEXP)[None, :] < np.arange(NEXP)[:, None]).reshape(1, -1), (P, 1))
    parts["headmask"] = np.zeros((P, DATT))
    for h in range(HEADS):
        parts["headmask"][h, h * DH:(h + 1) * DH] = 1.0
    parts["rowsel"] = np.zeros((P, DEC * DEC))
    parts["rowcast"] = np.zeros((P, DEC * P))
    for b in range(DEC):
        parts["rowsel"][0:HEADS, b * DEC + b] = 1.0
        parts["rowcast"][b, b * P:(b + 1) * P] = 1.0
    parts["tapsum"] = np.zeros((P, 2 * DEC))
    for t in range(2):
        for r in range(4 * (TAPS - 1)):
            parts["tapsum"][r, t * DEC + 4 * t + r // (TAPS - 1)] = 1.0
    at, cols = {}, []
    n = 0
    for name, a in parts.items():
        at[name] = (n, a.shape[1])
        cols.append(np.asarray(a, np.float32))
        n += a.shape[1]
    return at, np.ascontiguousarray(np.concatenate(cols, axis=1))


def decoder_step(nc, t, const_at, stop_after=99):
    with ExitStack() as whole:
        def persistent(name, shape, dt=F32):
            return whole.enter_context(nc.sbuf_tensor(name, shape, dt))

        K = persistent("K", [P, t["constants"].shape[1]])

        def const(name, rows=P):
            n, w = const_at[name]
            return K[0:rows, n:n + w]

        scratch = {
            "mod": nc.dram_tensor("mod_rows", [DEC + 1, 6 * D], F32).ap(),
            "q": nc.dram_tensor("q_rows", [SEQ, DATT], F32).ap(),
            "conv": nc.dram_tensor("conv_cols", [DCONV, SEQ], F32).ap(),
            "dec": nc.dram_tensor("decode_rows", [4, DEC, DATT], F32).ap(),
            "vec": nc.dram_tensor("band_vectors", [HEADS, 3 * VEC], F32).ap(),
            "band": nc.dram_tensor("band_rows", [3, P, HEADS, VEC], F32).ap(),
            "num": nc.dram_tensor("branch_rows", [3, SEQ, DATT], F32).ap(),
            "stat": nc.dram_tensor("branch_stats", [3, SEQ, 2 * HEADS], F32).ap(),
            "new": nc.dram_tensor("newest_scores", [2, DEC * HEADS], F32).ap(),
            "mix": nc.dram_tensor("decode_mix", [DEC, D], F32).ap(),
            "x2": nc.dram_tensor("x2_rows", [ROWS, D], F32).ap(),
            "h2": nc.dram_tensor("h2_rows", [ROWS, D], F32).ap(),
            "slot": nc.dram_tensor("slot_tokens", [NEXP * CAP, 1], I32).ap(),
            "y": nc.dram_tensor("expert_rows", [MAXBLK * P, D], F32).ap(),
        }
        state = {
            "decbias": persistent("decbias", [DEC * HEADS, 3 * P + 3]),
        }
        with nc.sbuf_tensor("WIN_SB", [P, KD, DIN], F32) as WIN_SB:
            setup_and_modulation(nc, t, scratch, const, K, state, WIN_SB)
            if stop_after >= 1:
                input_projection(nc, t, scratch, const, WIN_SB)
        if stop_after >= 2:
            prompt_attention(nc, t, scratch, const)
        if stop_after >= 3:
            decode_mixers(nc, t, scratch, const, state)
        if stop_after >= 4:
            state["token"] = persistent("token", [P, ALLT], I32)
            for name in ("rank", "expert", "weight"):
                state[name] = persistent(name, [P, ALLT, 2])
            state["count"] = persistent("count", [P, NEXP])
            output_projection_and_routing(nc, t, scratch, const, state)
        if stop_after >= 5:
            state["blocks"] = persistent("blocks", [P, 2 * NEXP], I32)
            state["dest"] = persistent("dest", [P, ALLT, 2], U32)
            experts(nc, t, scratch, const, state)
        if stop_after >= 6:
            combine_and_normalise(nc, t, scratch, const, state)
        return scratch


def stage_semaphores(nc, ctx):
    mine = []

    def sem(name):
        mine.append(nc.alloc_semaphore(name))
        return mine[-1]

    def give_back():
        nc.clear_and_free_semaphores(mine)
        nc.all_engine_barrier()

    ctx.callback(give_back)
    return sem


def setup_and_modulation(nc, t, dr, const, K, state, WIN_SB):
    NCH = 6 * D // 512
    with ExitStack() as ctx:
        def sb(name, shape, dt=F32):
            return ctx.enter_context(nc.sbuf_tensor(name, shape, dt))

        def ps(name, shape):
            return ctx.enter_context(nc.psum_tensor(name, shape, F32))

        sem = stage_semaphores(nc, ctx)

        CN = sb("CN", [P, D])
        SG = sb("SG0", [P, D])
        CT = sb("CT", [P, KD, P])
        WA = sb("WA", [P, 2, KD, 512])
        BA = sb("BA", [P, 2, 512])
        MO = sb("MO", [P, 2, 512])
        RB = sb("RB", [P, HEADS])
        RBX = sb("RBX", [P, DEC, HEADS])
        VE = sb("VE", [HEADS, 3 * VEC])
        Z = sb("Z", [P, NEXP * CAP // P], I32)
        TP = ps("TP0", [P, KD, P])
        MP = ps("MP0", [P, 2, 512])
        BP = ps("BP0", [P, 4, 512])
        consts_in, c_in, rb_in = sem("consts_in"), sem("c_in"), sem("rb_in")
        rb_set, rbx_ready, sig_ready, silu_ready = sem("rb_set"), sem("rbx_ready"), sem("sig_ready"), sem("silu_ready")
        ct_in_psum, ct_ready, bias_in_psum, vec_ready = sem("ct_in_psum"), sem("ct_ready"), sem("bias_in_psum"), sem("vec_ready")
        decbias_ready = sem("decbias_ready")
        vec_out, band_out, zero_set, zero_out = sem("vec_out"), sem("band_out"), sem("zero_set"), sem("zero_out")
        w_in = [sem(f"ada_in{p}") for p in range(2)]
        w_loaded = sem("w_loaded")
        w_used, mod_in_psum, mod_ready = sem("ada_used"), sem("mod_in_psum"), sem("mod_ready")
        mod_out = [sem(f"mod_out{p}") for p in range(2)]

        with nc.Block() as block:
            @block.sync
            def _(sp):
                sp.dma_start(K[:], t["constants"]).then_inc(consts_in, 16)
                sp.dma_start(CN[0:DEC, :], t["c_sample"]).then_inc(c_in, 16)
                sp.dma_start(CN[DEC:P, :], t["c_prompt"].to_broadcast([P - DEC, D])).then_inc(c_in, 16)
                sp.wait_ge(rb_set, 1)
                sp.dma_start(RB[0:BUCKETS, :], t["rel_bias"]).then_inc(rb_in, 16)
                w = t["w_ada"][0].rearrange("(k p) n -> p k n", p=P)
                with sp.Fori(0, NCH // 2) as i:
                    for p in range(2):
                        col = sp.snap((i * 2 + p) * 512)
                        sp.wait_ge(w_used, i * 2 + p + 1)
                        sp.dma_start(WA[:, p], w[:, :, ds(col, 512)]).then_inc(w_in[p], 16)
                        sp.dma_start(BA[:, p], t["b_ada"][0:1, ds(col, 512)].to_broadcast([P, 512])).then_inc(w_in[p], 16)

            @block.gpsimd
            def _(pool):
                pool.memset(RB[:], 1.0).then_inc(rb_set, 1)
                pool.memset(Z[:], 0).then_inc(zero_set, 1)
                pool.wait_ge(zero_set, 1)
                pool.dma_start(dr["slot"].rearrange("(p n) o -> p (n o)", p=P), Z[:]).then_inc(zero_out, 16)
                pool.wait_ge(vec_ready, 1)
                pool.dma_start(dr["vec"], VE[:]).then_inc(vec_out, 16)
                pool.wait_ge(vec_out, 16)
                for b in range(3):
                    pool.dma_start(dr["band"][b], dr["vec"][:, b * VEC:(b + 1) * VEC].partition_broadcast(P)).then_inc(band_out, 16)
                pool.wait_ge(band_out, 48)
                pool.wait_ge(zero_out, 16)

            @block.scalar
            def _(act):
                act.wait_ge(c_in, 32)
                nc.scalar.activation(SG[:], CN[:], ACT.Sigmoid).then_inc(sig_ready, 1)
                act.wait_ge(ct_in_psum, 1)
                nc.scalar.copy(CT[:], TP[:]).then_inc(ct_ready, 1)
                for k in range(KD):
                    act.dma_start(WIN_SB[:, k], t["w_in"][0, k * P:(k + 1) * P, :]).then_inc(w_loaded, 16)
                for p in range(2):
                    act.sem_inc(mod_out[p], 16)
                with act.Fori(0, NCH // 2) as i:
                    for p in range(2):
                        col = act.snap((i * 2 + p) * 512)
                        act.wait_ge(mod_ready, i * 2 + p + 1)
                        act.dma_start(dr["mod"][:, ds(col, 512)], MO[0:DEC + 1, p]).then_inc(mod_out[p], 16)
                for p in range(2):
                    act.wait_ge(mod_out[p], 16 * (NCH // 2) + 16)
                act.wait_ge(w_loaded, 16 * KD)

            @block.vector
            def _(dve):
                dve.wait_ge(sig_ready, 1)
                nc.vector.tensor_tensor(CN[:], CN[:], SG[:], ALU.mult).then_inc(silu_ready, 1)
                dve.wait_ge(rb_in, 16)
                nc.vector.tensor_copy(RBX[0:33], RB[0:33, None, :].to_broadcast([33, DEC, HEADS])).then_inc(rbx_ready, 1)
                dve.wait_ge(bias_in_psum, 1)
                for b in range(3):
                    last = nc.vector.tensor_copy(VE[:, b * VEC:(b + 1) * VEC], BP[0:HEADS, b, 0:VEC])
                last.then_inc(vec_ready, 1)
                nc.vector.tensor_copy(state["decbias"][:], BP[0:DEC * HEADS, 3, 0:3 * P + 3]).then_inc(decbias_ready, 1)
                with dve.Fori(0, NCH // 2) as i:
                    for p in range(2):
                        dve.wait_ge(mod_in_psum, i * 2 + p + 1)
                        dve.wait_ge(mod_out[p], i * 16 + 16)
                        nc.vector.tensor_tensor(MO[:, p], MP[:, p], BA[:, p], ALU.add).then_inc(mod_ready, 1)

            @block.tensor
            def _(pe):
                pe.wait_ge(consts_in, 16)
                pe.wait_ge(silu_ready, 1)
                for k in range(KD):
                    last = nc.tensor.transpose(TP[:, k], CN[:, k * P:(k + 1) * P], const("ident"))
                last.then_inc(ct_in_psum, 1)
                pe.wait_ge(rbx_ready, 1)
                for b in range(3):
                    nc.tensor.matmul(BP[0:HEADS, b, 0:VEC], RB[0:33, :], const("band", 33)[:, b * VEC:(b + 1) * VEC], start=True, stop=True)
                nc.tensor.matmul(BP[0:DEC * HEADS, 3, 0:3 * P + 3], RBX[0:33].rearrange("p a b -> p (a b)"), const("decband", 33),
                                 start=True, stop=True).then_inc(bias_in_psum, 1)
                pe.wait_ge(ct_ready, 1)
                pe.sem_inc(w_used, 2)
                with pe.Fori(0, NCH // 2) as i:
                    for p in range(2):
                        pe.wait_ge(w_in[p], i * 32 + 32)
                        for k in range(KD):
                            mm = nc.tensor.matmul(MP[:, p], CT[:, k], WA[:, p, k], start=k == 0, stop=k == KD - 1)
                        mm.then_inc(mod_in_psum, 1)
                        pe.wait_ge(mod_ready, i * 2 + p + 1)
                        pe.sem_inc(w_used, 1)


def input_projection(nc, t, dr, const, WIN_SB):
    with ExitStack() as ctx:
        def sb(name, shape, dt=F32):
            return ctx.enter_context(nc.sbuf_tensor(name, shape, dt))

        def ps(name, shape):
            return ctx.enter_context(nc.psum_tensor(name, shape, F32))

        sem = stage_semaphores(nc, ctx)

        GAIN, SHIFT, G1 = sb("GAIN", [P, 2, D]), sb("SHIFT", [P, 2, D]), sb("G1", [P, D])
        X, SQ, H, HT = sb("X", [P, D]), sb("SQ", [P, D]), sb("H", [P, D]), sb("HT", [P, KD, P])
        SSQ, MS, RSTD = sb("SSQ", [P, 1]), sb("MS", [P, 1]), sb("RSTD", [P, 1])
        SIG, GLU = sb("SIG", [P, DCONV]), sb("GLU", [P, DCONV])
        QKV = sb("QKV", [P, 3, DATT])
        CW, TAPW = sb("CW", [TAPS + 1, DCONV]), sb("TAPW", [P, KC, TAPS + 1])
        GEXT = sb("GEXT", [P, KC, TAPS - 1 + P])
        CONV = sb("CONV", [P, KC, P])
        TP = ps("TP1", [P, KD, P])
        PJ = ps("PJ", [P, 5, 512])
        GT = ps("GT", [P, KC, P])

        mods_in, gain_ready, taps_in = sem("mods_in"), sem("gain_ready"), sem("taps_in")
        taps_psum, taps_ready, ext_zero = sem("taps_psum"), sem("taps_ready"), sem("ext_zero")
        x_in, ssq_ready, ms_ready, rstd_ready = sem("x_in"), sem("ssq_ready"), sem("ms_ready"), sem("rstd_ready")
        h_half, h_ready, h_turned, ht_ready = sem("h_half"), sem("h_ready"), sem("h_turned"), sem("ht_ready")
        chunk_done, sig_done, glu_ready, glu_turned, ext_ready = sem("chunk_done"), sem("sig_done"), sem("glu_ready"), sem("glu_turned"), sem("ext_ready")
        qkv_ready = sem("qkv_ready")
        qkv_out = [sem(f"qkv_out{n}") for n in range(3)]
        conv_step, conv_ready, conv_out, tail_out = sem("conv_step"), sem("conv_ready"), sem("conv_out"), sem("tail_out")
        cache_out = [sem("cache_k_out"), sem("cache_v_out")]
        carry = sem("carry")

        DECT = TILES
        dec = dr["dec"]
        cache = t["cache_k"], t["cache_v"]
        newc = t["new_k_sample"], t["new_v_sample"]

        with nc.Block() as block:
            @block.sync
            def _(sp):
                for n, which in enumerate((1, 0)):
                    dst = (GAIN, SHIFT)[n]
                    sp.dma_start(dst[:, 0], dr["mod"][DEC:DEC + 1, which * D:(which + 1) * D].to_broadcast([P, D])).then_inc(mods_in, 16)
                    sp.dma_start(dst[0:DEC, 1], dr["mod"][0:DEC, which * D:(which + 1) * D]).then_inc(mods_in, 16)
                sp.dma_start(G1[:], t["g_norm1"].to_broadcast([P, D])).then_inc(mods_in, 16)
                sp.dma_start(CW[0:TAPS, :], t["conv_w"][0]).then_inc(taps_in, 16)
                sp.dma_start(CW[TAPS:TAPS + 1, :], t["conv_b"]).then_inc(taps_in, 16)
                sp.dma_start(X[:], t["x_prompt"][0, 0:P, :]).then_inc(x_in, 16)
                columns = dr["conv"].rearrange("(c p) s -> p c s", p=P)
                sp.wait_ge(h_ready, 1)
                sp.dma_start(X[:], t["x_prompt"][0, P:2 * P, :]).then_inc(x_in, 16)
                with sp.Fori(2, TILES) as i:
                    row, conv_at = sp.snap(i * P), sp.snap((i - 2) * P)
                    made, convolved = sp.snap(i), sp.snap(i - 1)
                    sp.wait_ge(h_ready, made)
                    sp.dma_start(X[:], t["x_prompt"][0, ds(row, P), :]).then_inc(x_in, 16)
                    sp.wait_ge(conv_ready, convolved)
                    sp.dma_start(columns[:, :, ds(conv_at, P)], CONV[:]).then_inc(conv_out, 16)
                sp.wait_ge(h_ready, TILES)
                sp.dma_start(X[0:DEC, :], t["x_sample"][:, 0, :]).then_inc(x_in, 16)
                sp.wait_ge(conv_ready, TILES - 1)
                sp.dma_start(columns[:, :, (TILES - 2) * P:(TILES - 1) * P], CONV[:]).then_inc(conv_out, 16)
                sp.wait_ge(glu_ready, TILES)
                sp.dma_start(t["new_conv_prompt"], GLU[P - TAPS + 1:P, :]).then_inc(tail_out, 16)
                sp.wait_ge(conv_ready, TILES)
                sp.dma_start(columns[:, :, (TILES - 1) * P:], CONV[:]).then_inc(conv_out, 16)
                sp.wait_ge(conv_out, 16 * TILES + 16)
                for n in range(3):
                    sp.wait_ge(qkv_out[n], 16 * TILES + 16 + (16 if n == 0 else 32))

            @block.gpsimd
            def _(pool):
                pool.memset(GEXT[:, :, 0:TAPS - 1], 0.0).then_inc(ext_zero, 1)

                def scale(tile):
                    pool.wait_ge(ssq_ready, tile + 1)
                    pool.tensor_tensor(MS[:], SSQ[:], const("eps"), ALU.add).then_inc(ms_ready, 1)
                    pool.wait_ge(ms_ready, tile + 1)
                    pool.tensor_tensor(RSTD[:], MS[:], const("neghalf"), ALU.pow).then_inc(rstd_ready, 1)

                for half in range(2):
                    with pool.Fori(0, DEC) as b:
                        pool.dma_start(newc[half][ds(b, 1), 0:(WIN - 1) * DATT], cache[half][ds(b, 1), DATT:WIN * DATT]).then_inc(cache_out[half], 16)
                        scale(b + half * DEC)
                scale(DECT)
                pool.wait_ge(cache_out[0], 16 * DEC)
                pool.wait_ge(cache_out[1], 16 * DEC)

            @block.scalar
            def _(act):
                for n in range(3):
                    act.sem_inc(qkv_out[n], 16)
                act.sem_inc(conv_out, 16)
                act.sem_inc(qkv_ready, 1)
                act.wait_ge(taps_psum, 1)
                nc.scalar.copy(TAPW[:], GT[:, :, 0:TAPS + 1]).then_inc(taps_ready, 1)

                def squares(tile, rows):
                    act.wait_ge(x_in, tile * 16 + 16)
                    nc.scalar.activation(SQ[0:rows], X[0:rows], ACT.Square, scale=D ** -0.5, accum_out=SSQ[0:rows]).then_inc(ssq_ready, 1)

                def evacuate(tile):
                    act.wait_ge(h_turned, tile + 1)
                    nc.scalar.copy(HT[:], TP[:]).then_inc(ht_ready, 1)
                    act.wait_ge(chunk_done, tile * 5 + 1)
                    nc.scalar.activation(SIG[:], PJ[:, 0], ACT.Sigmoid).then_inc(sig_done, 1)

                def qkv(tile):
                    for n in range(3):
                        act.wait_ge(chunk_done, tile * 5 + 3 + n)
                        act.wait_ge(qkv_out[n], tile * 16 + 16)
                        nc.scalar.mul(QKV[:, n], PJ[:, 2 + n], DH ** -0.5 if n == 0 else 1.0).then_inc(qkv_ready, 1)

                squares(0, P)
                with act.Fori(0, TILES - 1) as i:
                    row = act.snap(i * P)
                    evacuate(i)
                    squares(i + 1, P)
                    qkv(i)
                    for n, dst in enumerate((dr["q"], t["new_k_prompt"], t["new_v_prompt"])):
                        act.wait_ge(qkv_ready, i * 3 + n + 2)
                        act.dma_start(dst[ds(row, P), :], QKV[:, n]).then_inc(qkv_out[n], 16)
                evacuate(TILES - 1)
                squares(DECT, DEC)
                qkv(TILES - 1)
                for n, dst in enumerate((dr["q"], t["new_k_prompt"], t["new_v_prompt"])):
                    act.wait_ge(qkv_ready, TILES * 3 + n - 1)
                    act.dma_start(dst[SEQ - P:, :], QKV[:, n]).then_inc(qkv_out[n], 16)
                evacuate(DECT)
                qkv(DECT)
                for n, dst in enumerate((None, t["new_k_sample"], t["new_v_sample"])):
                    act.wait_ge(qkv_ready, DECT * 3 + n + 2)
                    act.dma_start(dec[n], QKV[0:DEC, n]).then_inc(qkv_out[n], 16)
                    if dst is not None:
                        act.dma_start(dst[:, (WIN - 1) * DATT:], QKV[0:DEC, n]).then_inc(qkv_out[n], 16)

            @block.vector
            def _(dve):
                dve.wait_ge(mods_in, 16 * 5)
                nc.vector.scalar_tensor_tensor(out=GAIN[:, 0], in0=GAIN[:, 0], scalar=1.0, in1=G1[:], op0=ALU.add, op1=ALU.mult).then_inc(gain_ready, 1)
                nc.vector.scalar_tensor_tensor(out=GAIN[0:DEC, 1], in0=GAIN[0:DEC, 1], scalar=1.0, in1=G1[0:DEC], op0=ALU.add, op1=ALU.mult).then_inc(gain_ready, 1)
                dve.wait_ge(gain_ready, 2)

                def modulated(tile, rows, which):
                    dve.wait_ge(rstd_ready, tile + 1)
                    dve.wait_ge(h_turned, tile)
                    nc.vector.scalar_tensor_tensor(out=H[0:rows], in0=X[0:rows], scalar=RSTD[0:rows], in1=GAIN[0:rows, which], op0=ALU.mult, op1=ALU.mult).then_inc(h_half, 1)
                    dve.wait_ge(h_half, tile + 1)
                    nc.vector.tensor_tensor(H[0:rows], H[0:rows], SHIFT[0:rows, which], ALU.add).then_inc(h_ready, 1)

                def glu(tile):
                    dve.wait_ge(sig_done, tile + 1)
                    dve.wait_ge(chunk_done, tile * 5 + 2)
                    nc.vector.tensor_tensor(GLU[:], PJ[:, 1], SIG[:], ALU.mult).then_inc(glu_ready, 1)

                def convolve(tile):
                    dve.wait_ge(glu_turned, tile + 1)
                    nc.vector.tensor_copy(GEXT[:, :, TAPS - 1:], GT[:]).then_inc(ext_ready, 1)
                    dve.wait_ge(ext_ready, tile + 1)
                    dve.wait_ge(conv_out, tile * 16 + 16)
                    for j in range(TAPS):
                        for c in range(KC):
                            if j == 0:
                                ins = nc.vector.tensor_scalar(CONV[:, c], GEXT[:, c, 0:P], TAPW[:, c, 0:1], TAPW[:, c, TAPS:TAPS + 1], ALU.mult, ALU.add)
                            else:
                                dve.wait_ge(conv_step, (j - 1) * KC + c + 1)
                                ins = nc.vector.scalar_tensor_tensor(out=CONV[:, c], in0=GEXT[:, c, j:j + P], scalar=TAPW[:, c, j:j + 1], in1=CONV[:, c], op0=ALU.mult, op1=ALU.add)
                            ins.then_inc(conv_step, 1)
                    dve.wait_ge(conv_step, TAPS * KC)
                    dve.sem_clear(conv_step)
                    nc.vector.tensor_copy(GEXT[:, :, 0:TAPS - 1], GEXT[:, :, P:P + TAPS - 1]).then_inc(conv_ready, 1)
                    dve.wait_ge(conv_ready, tile + 1)

                dve.wait_ge(rstd_ready, 1)
                nc.vector.scalar_tensor_tensor(out=H[:], in0=X[:], scalar=RSTD[:], in1=GAIN[:, 0], op0=ALU.mult, op1=ALU.mult).then_inc(h_half, 1)
                dve.wait_ge(h_half, 1)
                nc.vector.tensor_tensor(H[:], H[:], SHIFT[:, 0], ALU.add).then_inc(h_ready, 1)
                dve.wait_ge(ext_zero, 1)
                dve.wait_ge(taps_ready, 1)
                with dve.Fori(0, TILES - 1) as i:
                    modulated(i + 1, P, 0)
                    glu(i)
                    convolve(i)
                modulated(DECT, DEC, 1)
                glu(TILES - 1)
                convolve(TILES - 1)
                dve.wait_ge(tail_out, 16)
                glu(DECT)

            @block.tensor
            def _(pe):
                pe.wait_ge(taps_in, 32)
                for c in range(KC):
                    last = nc.tensor.transpose(GT[:, c, 0:TAPS + 1], CW[:, c * P:(c + 1) * P], const("ident")[0:TAPS + 1, 0:TAPS + 1])
                last.then_inc(taps_psum, 1)
                pe.wait_ge(taps_ready, 1)
                columns = (3 * DATT + DCONV, 3 * DATT, 0, DATT, 2 * DATT)

                def project(tile):
                    pe.wait_ge(h_ready, tile + 1)
                    for k in range(KD):
                        mm = nc.tensor.transpose(TP[:, k], H[:, k * P:(k + 1) * P], const("ident"))
                    mm.then_inc(h_turned, 1)
                    pe.wait_ge(ht_ready, tile + 1)
                    for n, col in enumerate(columns):
                        if n == 2:
                            pe.wait_ge(qkv_ready, tile * 3 + 1)
                        for k in range(KD):
                            mm = nc.tensor.matmul(PJ[:, n], HT[:, k], WIN_SB[:, k, col:col + 512], start=k == 0, stop=k == KD - 1)
                        mm.then_inc(chunk_done, 1)

                def turn_glu(tile):
                    pe.wait_ge(glu_ready, tile + 1)
                    for c in range(KC):
                        mm = nc.tensor.transpose(GT[:, c], GLU[:, c * P:(c + 1) * P], const("ident"))
                    mm.then_inc(glu_turned, 1)

                with pe.Fori(0, TILES) as i:
                    project(i)
                    turn_glu(i)
                project(DECT)

        with nc.Block() as block:
            @block.sync
            def _(sp):
                sp.dma_start(dec[3], GLU[0:DEC]).then_inc(tail_out, 16)
                sp.wait_ge(tail_out, 32)


def dilated(rows, dil, r, first, count):
    v = rows.rearrange("(i d) c -> d i c", d=dil)
    v = v[r] if isinstance(r, int) else v[ds(r, 1)].rearrange("a i c -> (a i) c")
    v = v[first:first + count, :] if isinstance(first, int) else v[ds(first, count), :]
    return v.rearrange("(k p) c -> p k c", p=P) if count > P else v


def prompt_attention(nc, t, dr, const):
    segments = [
        (2, 0, TILES - 1, lambda j: 0, lambda j: j + 1),
        (2, 1, 4, lambda j: j, lambda j: 1),
        (2, 1, 4, lambda j: j, lambda j: 2),
        (2, 1, 4, lambda j: j, lambda j: 3),
        (1, 0, 1, lambda j: 0, lambda j: 0),
        (1, 1, 4, lambda j: j, lambda j: 0),
        (1, 2, 16, lambda j: j, lambda j: 0),
    ]
    starts = [sum(s[2] for s in segments[:n]) for n in range(len(segments))]
    BLOCKS = sum(s[2] for s in segments)
    HH = HEADS // 2
    branch = [s[1] for s in segments for _ in range(s[2])]
    width = [s[0] for s in segments for _ in range(s[2])]
    shape = [(branch[g], width[g - 1] if g else 0, width[g], width[g + 1] if g + 1 < BLOCKS else 0) for g in range(BLOCKS)]

    def rounds(engine, body, parts):
        g = 0
        while g < BLOCKS:
            end = g + 1
            while g > 1 and end < BLOCKS and all(shape[end][n] == shape[g][n] for n in parts):
                end += 1
            if end == g + 1:
                body(g, *shape[g])
            else:
                with engine.Fori(g, end) as i:
                    body(i, *shape[g])
            g = end

    def wait(engine, signal, value):
        if not (isinstance(value, int) and value <= 0):
            engine.wait_ge(signal, value)

    with ExitStack() as ctx:
        def sb(name, shape, dt=F32):
            return ctx.enter_context(nc.sbuf_tensor(name, shape, dt))

        def ps(name, shape):
            return ctx.enter_context(nc.psum_tensor(name, shape, F32))

        sem = stage_semaphores(nc, ctx)

        BIAS = [sb(f"BIAS{b}", [P, HEADS, 2 * P]) for b in range(3)]
        QN, KN, VN = sb("QN", [P, DATT]), sb("KN", [P, 2, DATT]), sb("VN", [P, 2, DATT])
        QZ = sb("QZ", [P, HEADS, P])
        VZ = sb("VZ", [P, 2, 2, DATT])
        KT = sb("KT", [P, HH, 2 * P])
        SBX = [sb(f"SBX{h}", [P, HH, 2 * P]) for h in range(2)]
        PR = [sb(f"PR{h}", [P, HH, 2 * P]) for h in range(2)]
        PTS = sb("PTS", [P, 4, 4, P])
        PAUSE = sb("PAUSE", [P, 1])
        MX, NM, ML = sb("MX", [P, HEADS]), sb("NM", [P, HEADS]), sb("ML", [P, 2 * HEADS])
        O = sb("O", [P, DATT])
        SP_ = [ps(f"S{h}", [P, HH, 2 * P]) for h in range(2)]
        TQ, OP = ps("TQ", [P, HH, P]), ps("OP", [P, DATT])
        TB = [ps(f"TB{n}", [P, 4, P]) for n in range(2)]

        bias_in, qz_zero, vz_zero = sem("bias_in"), sem("qz_zero"), sem("vz_zero")
        q_in, k_in, v_in = sem("q_in"), sem("k_in"), sem("v_in")
        q_turned, k_turned, kt_ready, s_done, mx_done, nm_ready, m_saved = (sem("q_turned"), sem("k_turned"), sem("kt_ready"), sem("s_done"), sem("mx_done"),
                                                                            sem("nm_ready"), sem("m_saved"))
        exp_done, p_turned, first_pt, last_pt, vz_ready, pv_done, o_taken = (sem("exp_done"), sem("probs_turned"), sem("first_pt"), sem("last_pt"), sem("vz_ready"),
                                                                            sem("pv_done"), sem("o_taken"))
        o_out, ml_out, loading, spreading = sem("o_out"), sem("ml_out"), sem("loading"), sem("spreading")

        with nc.Block() as block:
            @block.sync
            def _(sp):
                for b in range(3):
                    v = dr["band"][b]
                    skew = bass.AP(v.tensor, v.offset + P - 1, [[HEADS * VEC - 1, P], [VEC, HEADS], [1, 2 * P]])
                    sp.dma_start(BIAS[b][:], skew).then_inc(bias_in, 16)

                def load(g, seg, j):
                    nk, b, _, r, n = seg
                    n1 = n(j)
                    own, first = (n1 * P, (n1 - nk + 1) * P) if isinstance(n1, int) else (sp.snap(n1 * P), sp.snap((n1 - nk + 1) * P))
                    q = dilated(dr["q"], DILATIONS[b], r(j), own, P)
                    k, v = (dilated(x, DILATIONS[b], r(j), first, nk * P) for x in (t["new_k_prompt"], t["new_v_prompt"]))
                    turned = g * 2 if isinstance(g, int) else sp.snap(g * 2)
                    wait(sp, q_turned, g)
                    sp.dma_start(QN[:], q).then_inc(q_in, 16)
                    wait(sp, k_turned, turned)
                    sp.sem_inc(loading, 1)
                    sp.dma_start(KN[:] if nk == 2 else KN[:, 0], k).then_inc(k_in, 16)
                    wait(sp, vz_ready, g)
                    sp.sem_inc(loading, 1)
                    sp.dma_start(VN[:] if nk == 2 else VN[:, 0], v).then_inc(v_in, 16)

                load(0, segments[0], 0)
                for n, seg in enumerate(segments):
                    start = 1 if n == 0 else 0
                    if seg[2] > 1:
                        with sp.Fori(start, seg[2]) as j:
                            load(sp.snap(j + starts[n]), seg, j)
                    else:
                        load(starts[n], seg, 0)

            @block.gpsimd
            def _(pool):
                pool.memset(QZ[:], 0.0).then_inc(qz_zero, 1)
                pool.memset(VZ[:], 0.0).then_inc(vz_zero, 1)
                pool.wait_ge(vz_zero, 1)

                def spread(g):
                    wait(pool, pv_done, g)
                    pool.wait_ge(v_in, g * 16 + 16)
                    pool.sem_inc(spreading, 1)
                    for odd in range(2):
                        view = [x.rearrange("p k (a b e) -> p k a b e", b=2, e=DH)[:, :, :, odd] for x in (VZ[:, :, odd], VN[:])]
                        ins = pool.tensor_copy(*view)
                    ins.then_inc(vz_ready, 1)

                def store(g, seg, j):
                    nk, b, _, r, n = seg
                    n1 = n(j)
                    first = pool.snap(n1 * P) if not isinstance(n1, int) else n1 * P
                    pool.wait_ge(m_saved, g + 1)
                    pool.wait_ge(exp_done, g * 2 + 2)
                    pool.dma_start(dilated(dr["stat"][b], DILATIONS[b], r(j), first, P), ML[:]).then_inc(ml_out, 16)
                    if not (isinstance(g, int) and g == BLOCKS - 1):
                        spread(g + 1)
                    pool.wait_ge(o_taken, g + 1)
                    pool.dma_start(dilated(dr["num"][b], DILATIONS[b], r(j), first, P), O[:]).then_inc(o_out, 16)

                spread(0)
                for n, seg in enumerate(segments):
                    last = seg[2] - 1 if n == len(segments) - 1 else seg[2]
                    if seg[2] > 1:
                        with pool.Fori(0, last) as j:
                            store(pool.snap(j + starts[n]), seg, j)
                    else:
                        store(starts[n], seg, 0)
                store(BLOCKS - 1, segments[-1], segments[-1][2] - 1)
                pool.wait_ge(ml_out, 16 * BLOCKS)
                pool.wait_ge(o_out, 16 * BLOCKS)

            @block.vector
            def _(dve):
                dve.wait_ge(bias_in, 48)
                dve.wait_ge(qz_zero, 1)

                def take_qk(g, nk):
                    dve.wait_ge(q_turned, g + 1)
                    nc.vector.tensor_copy(QZ[0:DH, 0::2], TQ[0:DH])
                    nc.vector.tensor_copy(QZ[DH:P, 1::2], TQ[DH:P])
                    for u in range(nk):
                        dve.wait_ge(k_turned, g * 2 + (u + 1) * 2 // nk)
                        pairs = slice(u * HH // nk, (u + 1) * HH // nk)
                        nc.vector.tensor_copy(KT[:, pairs, 0:nk * P].rearrange("p h (k q) -> p h k q", q=P),
                                              TB[u][:].rearrange("p (h k) q -> p h k q", k=nk)).then_inc(kt_ready, 2 // nk)

                def maxima(g, b, nk):
                    w = nk * P
                    for hh in range(2):
                        dve.wait_ge(s_done, g * 2 + hh + 1)
                        wait(dve, exp_done, g * 2 + hh - 1 if not isinstance(g, int) or g else 0)
                        nc.vector.memset(PAUSE[:], 0.0)
                        for h in range(HH):
                            head = hh * HH + h
                            nc.vector.tensor_tensor_reduce(SBX[hh][:, h, 0:w], SP_[hh][:, h, 0:w], BIAS[b][:, head, 2 * P - w:], 1.0, -3e38, ALU.add, ALU.max,
                                                           MX[:, head:head + 1]).then_inc(mx_done, 1)
                        dve.wait_ge(mx_done, g * 8 + hh * 4 + 4)
                        nc.vector.tensor_scalar(NM[:, hh * HH:hh * HH + HH], MX[:, hh * HH:hh * HH + HH], -1.0, None, ALU.mult).then_inc(nm_ready, 1)
                    wait(dve, ml_out, g * 16)
                    nc.vector.tensor_copy(ML[:, 0:HEADS], MX[:]).then_inc(m_saved, 1)

                def round_(g, b, before, nk, behind):
                    maxima(g, b, nk)
                    if before == 2:
                        for u in (2, 3):
                            dve.wait_ge(p_turned, g * 4 + u - 3)
                            nc.vector.tensor_copy(PTS[:, u], TB[u % 2][:]).then_inc(last_pt, 1)
                    if behind:
                        take_qk(g + 1, behind)

                take_qk(0, shape[0][2])
                rounds(dve, round_, (0, 1, 2, 3))

            @block.scalar
            def _(act):
                def take_probs(g, nk):
                    for u in range(2):
                        act.wait_ge(p_turned, g * 4 + (u + 1) * 2 // nk)
                        nc.scalar.copy(PTS[:, u], TB[u][:]).then_inc(first_pt, 1)

                def exponentials(g, nk):
                    w = nk * P
                    for hh in range(2):
                        act.wait_ge(nm_ready, g * 2 + hh + 1)
                        if hh:
                            wait(act, p_turned, g * 4)
                        if hh == 0:
                            wait(act, ml_out, g * 16)
                        for h in range(HH):
                            head = hh * HH + h
                            ins = nc.scalar.activation(PR[hh][:, h, 0:w], SBX[hh][:, h, 0:w], ACT.Exp, bias=NM[:, head:head + 1], scale=1.0,
                                                       accum_out=ML[:, HEADS + head:HEADS + head + 1])
                        ins.then_inc(exp_done, 1)

                def take_rows(g):
                    act.wait_ge(pv_done, g + 1)
                    wait(act, o_out, g * 16)
                    nc.scalar.copy(O[:], OP[:]).then_inc(o_taken, 1)

                def round_(g, b, before, nk, behind):
                    if before:
                        take_probs(g - 1, before)
                    exponentials(g, nk)
                    if before:
                        take_rows(g - 1)

                rounds(act, round_, (1, 2))
                take_probs(BLOCKS - 1, shape[-1][2])
                take_rows(BLOCKS - 1)

            @block.tensor
            def _(pe):
                def turn_q(g):
                    pe.wait_ge(q_in, g * 16 + 16)
                    for h in range(HH):
                        mm = nc.tensor.transpose(TQ[:, h], QN[:, h * P:(h + 1) * P], const("ident"))
                    mm.then_inc(q_turned, 1)

                def turn_k(g, nk, u):
                    if u == 0:
                        pe.wait_ge(k_in, g * 16 + 16)
                    for n in range(4):
                        pair, k = u * HH // nk + n // nk, n % nk
                        mm = nc.tensor.transpose(TB[u][:, n], KN[:, k, pair * P:(pair + 1) * P], const("ident"))
                    mm.then_inc(k_turned, 2 // nk)

                def scores(g, nk):
                    for hh in range(2):
                        pe.wait_ge(kt_ready, g * 2 + hh + 1)
                        wait(pe, nm_ready, g * 2 + hh - 1 if not isinstance(g, int) or g else 0)
                        for h in range(HH):
                            head = hh * HH + h
                            mm = nc.tensor.matmul(SP_[hh][:, h, 0:nk * P], QZ[:, head], KT[:, head // 2, 0:nk * P], start=True, stop=True)
                        mm.then_inc(s_done, 1)

                def turn_p(g, nk, u):
                    if u % nk == 0:
                        pe.wait_ge(exp_done, g * 2 + u // nk + 1)
                    for n in range(4):
                        head, k = u * 4 // nk + n // nk, n % nk
                        mm = nc.tensor.transpose(TB[u % 2][:, n], PR[head // HH][:, head % HH, k * P:(k + 1) * P], const("ident"))
                    mm.then_inc(p_turned, 2 // nk)

                def values(g, nk, u):
                    pe.wait_ge(first_pt if u < 2 else last_pt, g * 2 + u % 2 + 1)
                    if u == 0:
                        pe.wait_ge(vz_ready, g + 1)
                        wait(pe, o_taken, g)
                    for n in range(4):
                        head, k = u * 4 // nk + n // nk, n % nk
                        cols = slice(head // 2 * P, head // 2 * P + P)
                        mm = nc.tensor.matmul(OP[:, cols], PTS[:, u, n], VZ[:, k, head % 2, cols], start=head % 2 == 0 and k == 0, stop=head % 2 == 1 and k == nk - 1)
                    if u == 2 * nk - 1:
                        mm.then_inc(pv_done, 1)

                def round_(g, b, before, nk, behind):
                    scores(g, nk)
                    units = 2 * before
                    for u in range(min(units, 2)):
                        turn_p(g - 1, before, u)
                    for u in range(units - 2):
                        values(g - 1, before, u)
                        turn_p(g - 1, before, u + 2)
                    if behind:
                        turn_q(g + 1)
                    for n, u in enumerate(range(max(units - 2, 0), units)):
                        values(g - 1, before, u)
                        if behind and n < behind:
                            turn_k(g + 1, behind, n)
                    if behind and not units:
                        for u in range(behind):
                            turn_k(g + 1, behind, u)

                turn_q(0)
                for u in range(shape[0][2]):
                    turn_k(0, shape[0][2], u)
                rounds(pe, round_, (1, 2, 3))
                for u in range(2 * shape[-1][2]):
                    turn_p(BLOCKS - 1, shape[-1][2], u)
                for u in range(2 * shape[-1][2]):
                    values(BLOCKS - 1, shape[-1][2], u)


def decode_mixers(nc, t, dr, const, state):
    TS = TAPS - 1
    KEYS = 3 * P
    BH = DEC * HEADS
    with ExitStack() as ctx:
        def sb(name, shape, dt=F32):
            return ctx.enter_context(nc.sbuf_tensor(name, shape, dt))

        def ps(name, shape):
            return ctx.enter_context(nc.psum_tensor(name, shape, F32))

        sem = stage_semaphores(nc, ctx)

        R = sb("DROWS", [DEC, 4, DATT])
        QB, CK, CV = sb("QB", [P, DATT]), sb("CK", [P, 3, DATT]), sb("CV", [P, 3, DATT])
        TMP, SC = sb("TMP", [P, 3, DATT]), sb("SC", [P, 3, BH])
        QK0, S0, N0 = sb("QK0", [DEC, DATT]), sb("S0D", [DEC, HEADS]), sb("N0", [BH, 1])
        SS, PE_, MXD, NMD, LD, RD = sb("SS", [BH, KEYS + 3]), sb("PE_", [BH, KEYS + 3]), sb("MXD", [BH, 1]), sb("NMD", [BH, 1]), sb("LD", [BH, 1]), sb("RD", [BH, 1])
        P0, P8 = sb("P0", [BH, 1]), sb("P8", [DEC, HEADS])
        PTD, PB, OM = sb("PTD", [P, 3, BH]), sb("PB", [P, 3, HEADS]), sb("OM", [HEADS, DATT])
        ROW, ATT, A0 = sb("ROW", [1, DATT]), sb("ATT", [DEC, DATT]), sb("A0", [DEC, DATT])
        ST, CWR = sb("ST", [4 * TS, 2, DCONV]), sb("CWR", [4 * TS, DCONV])
        WL, CB, LG, LB = sb("WL", [DEC, DCONV]), sb("CB", [DEC, DCONV]), sb("LGD", [DEC, DCONV]), sb("LBD", [DEC, DCONV])
        CVN, BS, MV, VE, RS, TH = sb("CVN", [DEC, DCONV]), sb("BSD", [DEC, 6]), sb("MVD", [DEC, 2]), sb("VED", [DEC, 1]), sb("RSD", [DEC, 1]), sb("THD", [DEC, DCONV])
        MIX = sb("MIXD", [DEC, D])
        STP, PTP, OD, OR, CP = ps("STP", [BH, 3, P]), ps("PTP", [P, 3, BH]), ps("OD", [HEADS, DATT]), ps("OR", [P, DATT]), ps("CP", [DEC, DCONV])

        rows_in, conv_in, k_in, v_in = sem("rows_in"), sem("conv_in"), sem("dk_in"), sem("dv_in")
        mul_done, red_done, s_turned, s0_done, n0_out, n0_in = sem("mul_done"), sem("red_done"), sem("s_turned"), sem("s0_done"), sem("n0_out"), sem("n0_in")
        step, exp_ready, p0_ready, p0_out, p8_in = sem("softmax_step"), sem("dexp_ready"), sem("p0_ready"), sem("p0_out"), sem("p8_in")
        p_turned, ptd_ready, pb_ready, od_done, om_ready, or_done, row_ready, row_out, att_in = (sem("p_turned"), sem("ptd_ready"), sem("pb_ready"), sem("od_done"),
                                                                                               sem("om_ready"), sem("or_done"), sem("row_ready"), sem("row_out"), sem("att_in"))
        row_free = sem("row_free")
        cstep, conv_sum, var_ready, rs_ready, th_ready, mix_ready, mix_out, state_out = (sem("cstep"), sem("conv_sum"), sem("var_ready"), sem("rs_ready"), sem("th_ready"),
                                                                                        sem("mix_ready"), sem("mix_out"), sem("state_out"))

        with nc.Block() as block:
            @block.sync
            def _(sp):
                sp.dma_start(R[:], dr["dec"].rearrange("n b c -> b n c")).then_inc(rows_in, 16)
                with sp.Fori(0, DEC) as b:
                    sp.wait_ge(red_done, b + 1)
                    sp.dma_start(QB[:], dr["dec"][0, ds(b, 1), :].to_broadcast([P, DATT])).then_inc(k_in, 16)
                    for n, dil in enumerate(DILATIONS):
                        keys = t["cache_k"][ds(b, 1), (WIN - P * dil) * DATT:].rearrange("a (p x) -> (a p) x", p=P)[:, 0:DATT]
                        sp.dma_start(CK[:, n], keys).then_inc(k_in, 16)
                with sp.Fori(0, DEC) as b:
                    sp.wait_ge(od_done, b + 1)
                    for n, dil in enumerate(DILATIONS):
                        vals = t["cache_v"][ds(b, 1), (WIN - P * dil) * DATT:].rearrange("a (p x) -> (a p) x", p=P)[:, 0:DATT]
                        sp.dma_start(CV[:, n], vals).then_inc(v_in, 16)

            @block.gpsimd
            def _(pool):
                pool.dma_start(t["new_conv_sample"][:, 0:(TS - 1) * DCONV], t["state_conv"][:, DCONV:]).then_inc(state_out, 16)
                pool.dma_start(t["new_conv_sample"][:, (TS - 1) * DCONV:], dr["dec"][3]).then_inc(state_out, 16)
                for b in range(4):
                    pool.dma_start(CWR[b * TS:(b + 1) * TS, :], t["conv_w"][0, 0:TS, :]).then_inc(conv_in, 16)
                pool.dma_start(ST[:], t["state_conv"].rearrange("b (w c) -> (b w) c", w=TS).rearrange("(n r) c -> r n c", n=2)).then_inc(conv_in, 16)
                for dst, src in ((WL, t["conv_w"][0, TS:TAPS, :]), (CB, t["conv_b"]), (LG, t["ln_g"]), (LB, t["ln_b"])):
                    pool.dma_start(dst[:], src.to_broadcast([DEC, DCONV])).then_inc(conv_in, 16)
                pool.wait_ge(var_ready, 1)
                pool.tensor_tensor(VE[:], MV[:, 1:2], const("eps", DEC), ALU.add).then_inc(rs_ready, 1)
                pool.wait_ge(rs_ready, 1)
                pool.tensor_tensor(RS[:], VE[:], const("neghalf", DEC), ALU.pow).then_inc(rs_ready, 1)
                pool.wait_ge(s0_done, 1)
                pool.dma_start(dr["new"][0].rearrange("(b h) -> b h", b=DEC), S0[:]).then_inc(n0_out, 16)
                pool.wait_ge(n0_out, 16)
                pool.dma_start(N0[:], dr["new"][0].rearrange("(n o) -> n o", o=1)).then_inc(n0_in, 16)
                pool.wait_ge(p0_ready, 1)
                pool.dma_start(dr["new"][1].rearrange("(n o) -> n o", o=1), P0[:]).then_inc(p0_out, 16)
                pool.wait_ge(p0_out, 16)
                pool.dma_start(P8[:], dr["new"][1].rearrange("(b h) -> b h", b=DEC)).then_inc(p8_in, 16)
                with pool.Fori(0, DEC) as b:
                    pool.wait_ge(row_ready, b + 1)
                    pool.dma_start(dr["mix"][ds(b, 1), 0:DATT], ROW[:]).then_inc(row_out, 16)
                    pool.wait_ge(row_out, b * 16 + 16)
                    pool.sem_inc(row_free, 1)
                pool.wait_ge(row_out, 16 * DEC)
                pool.dma_start(ATT[:], dr["mix"][:, 0:DATT]).then_inc(att_in, 16)
                pool.wait_ge(mix_ready, 2)
                pool.dma_start(dr["mix"], MIX[:]).then_inc(mix_out, 16)
                pool.wait_ge(mix_out, 16)
                pool.wait_ge(state_out, 32)

            @block.scalar
            def _(act):
                act.wait_ge(cstep, 8)
                nc.scalar.activation(TH[:], CVN[:], ACT.Tanh, scale=0.5).then_inc(th_ready, 1)
                act.wait_ge(step, 4)
                nc.scalar.activation(PE_[:], SS[:], ACT.Exp, bias=NMD[:], scale=1.0, accum_out=LD[:]).then_inc(exp_ready, 1)

            @block.vector
            def _(dve):
                dve.sem_inc(red_done, 1)
                dve.wait_ge(rows_in, 16)
                nc.vector.tensor_tensor(QK0[:], R[:, 0], R[:, 1], ALU.mult).then_inc(mul_done, 1)
                dve.wait_ge(mul_done, 1)
                nc.vector.tensor_reduce(S0[:], QK0[:].rearrange("b (h e) -> b h e", e=DH), AX.X, ALU.add).then_inc(s0_done, 1)
                dve.wait_ge(conv_in, 16 * 9)
                nc.vector.tensor_tensor(ST[:], ST[:], CWR[:, None, :].to_broadcast([4 * TS, 2, DCONV]), ALU.mult).then_inc(cstep, 1)
                nc.vector.tensor_tensor(WL[:], WL[:], R[:, 3], ALU.mult).then_inc(cstep, 1)
                dve.wait_ge(cstep, 2)
                nc.vector.tensor_tensor(CVN[:], WL[:], CB[:], ALU.add).then_inc(cstep, 1)
                dve.wait_ge(cstep, 3)
                dve.wait_ge(conv_sum, 1)
                nc.vector.tensor_tensor(CVN[:], CP[:], CVN[:], ALU.add).then_inc(cstep, 1)
                dve.wait_ge(cstep, 4)
                nc.vector.bn_stats(BS[:], CVN[:]).then_inc(cstep, 1)
                dve.wait_ge(cstep, 5)
                nc.vector.bn_aggr(MV[:], BS[:]).then_inc(var_ready, 1)
                dve.wait_ge(rs_ready, 2)
                nc.vector.tensor_scalar(CVN[:], CVN[:], MV[:, 0:1], RS[:], ALU.subtract, ALU.mult).then_inc(cstep, 1)
                dve.wait_ge(cstep, 6)
                nc.vector.tensor_tensor(CVN[:], CVN[:], LG[:], ALU.mult).then_inc(cstep, 1)
                dve.wait_ge(cstep, 7)
                nc.vector.tensor_tensor(CVN[:], CVN[:], LB[:], ALU.add).then_inc(cstep, 1)
                dve.wait_ge(th_ready, 1)
                nc.vector.scalar_tensor_tensor(out=MIX[:, DATT:], in0=TH[:], scalar=1.0, in1=CVN[:], op0=ALU.add, op1=ALU.mult).then_inc(mix_ready, 1)
                with dve.Fori(0, DEC) as b:
                    dve.wait_ge(k_in, b * 64 + 64)
                    nc.vector.tensor_tensor(TMP[:], CK[:], QB[:, None, :].to_broadcast([P, 3, DATT]), ALU.mult).then_inc(mul_done, 1)
                    dve.wait_ge(mul_done, b + 2)
                    nc.vector.tensor_reduce(SC[:, :, ds(b * HEADS, HEADS)], TMP[:].rearrange("p n (h e) -> p n h e", e=DH), AX.X, ALU.add).then_inc(red_done, 1)
                dve.wait_ge(s_turned, 1)
                nc.vector.tensor_tensor(SS[:, 0:KEYS], STP[:].rearrange("p n k -> p (n k)"), state["decbias"][:, 0:KEYS], ALU.add).then_inc(step, 1)
                dve.wait_ge(n0_in, 16)
                nc.vector.tensor_scalar(SS[:, KEYS:], state["decbias"][:, KEYS:], N0[:], None, ALU.add).then_inc(step, 1)
                dve.wait_ge(step, 2)
                nc.vector.tensor_reduce(MXD[:], SS[:], AX.X, ALU.max).then_inc(step, 1)
                dve.wait_ge(step, 3)
                nc.vector.tensor_scalar(NMD[:], MXD[:], -1.0, None, ALU.mult).then_inc(step, 1)
                dve.wait_ge(exp_ready, 1)
                nc.vector.reciprocal(RD[:], LD[:]).then_inc(step, 1)
                dve.wait_ge(step, 5)
                nc.vector.tensor_scalar(SS[:], PE_[:], RD[:], None, ALU.mult).then_inc(step, 1)
                dve.wait_ge(step, 6)
                nc.vector.tensor_reduce(P0[:], SS[:, KEYS:], AX.X, ALU.add).then_inc(p0_ready, 1)
                dve.wait_ge(p_turned, 1)
                nc.vector.tensor_copy(PTD[:], PTP[:]).then_inc(ptd_ready, 1)
                dve.wait_ge(ptd_ready, 1)
                with dve.Fori(0, DEC) as b:
                    dve.wait_ge(od_done, b + 1)
                    nc.vector.tensor_copy(PB[:], PTD[:, :, ds(b * HEADS, HEADS)]).then_inc(pb_ready, 1)
                    dve.wait_ge(od_done, b + 2)
                    nc.vector.tensor_tensor(OM[:], OD[:], const("headmask", HEADS), ALU.mult).then_inc(om_ready, 1)
                    dve.wait_ge(or_done, b + 1)
                    dve.wait_ge(row_free, b + 1)
                    nc.vector.tensor_copy(ROW[:], OR[0:1]).then_inc(row_ready, 1)
                dve.wait_ge(att_in, 16)
                dve.wait_ge(p8_in, 16)
                nc.vector.tensor_tensor(A0[:].rearrange("b (h e) -> b h e", e=DH), R[:, 2].rearrange("b (h e) -> b h e", e=DH),
                                        P8[:, :, None].to_broadcast([DEC, HEADS, DH]), ALU.mult).then_inc(step, 1)
                dve.wait_ge(step, 7)
                nc.vector.tensor_tensor(MIX[:, 0:DATT], A0[:], ATT[:], ALU.add).then_inc(mix_ready, 1)

            @block.tensor
            def _(pe):
                pe.sem_inc(od_done, 1)
                pe.sem_inc(row_free, 1)
                pe.wait_ge(cstep, 2)
                for n in range(2):
                    mm = nc.tensor.matmul(CP[:], const("tapsum", 4 * TS)[:, n * DEC:(n + 1) * DEC], ST[:, n], start=n == 0, stop=n == 1)
                mm.then_inc(conv_sum, 1)
                pe.wait_ge(red_done, DEC + 1)
                for n in range(3):
                    mm = nc.tensor.transpose(STP[:, n], SC[:, n], const("ident"))
                mm.then_inc(s_turned, 1)
                pe.wait_ge(p0_ready, 1)
                for n in range(3):
                    mm = nc.tensor.transpose(PTP[:, n], SS[:, n * P:(n + 1) * P], const("ident")[0:BH, 0:BH])
                mm.then_inc(p_turned, 1)
                with pe.Fori(0, DEC) as b:
                    pe.wait_ge(pb_ready, b + 1)
                    pe.wait_ge(v_in, b * 48 + 48)
                    for n in range(3):
                        mm = nc.tensor.matmul(OD[:], PB[:, n], CV[:, n], start=n == 0, stop=n == 2)
                    mm.then_inc(od_done, 1)
                    pe.wait_ge(om_ready, b + 1)
                    nc.tensor.matmul(OR[:], const("ones", HEADS), OM[:], start=True, stop=True).then_inc(or_done, 1)


def output_projection_and_routing(nc, t, dr, const, state):

    def rounds(engine, body):
        for i in range(-1, 3):
            body(i)
        with engine.Fori(3, TILES - 2) as i:
            body(i)
        for i in range(TILES - 2, ALLT + 3):
            body(i)

    def there(tile, last=TILES):
        return not isinstance(tile, int) or 0 <= tile <= last

    def wait(engine, signal, value):
        if not (isinstance(value, int) and value <= 0):
            engine.wait_ge(signal, value)

    def rows_of(tile):
        return DEC if isinstance(tile, int) and tile == TILES else P

    def which_of(tile):
        return 1 if isinstance(tile, int) and tile == TILES else 0

    with ExitStack() as ctx:
        def sb(name, shape, dt=F32):
            return ctx.enter_context(nc.sbuf_tensor(name, shape, dt))

        def ps(name, shape):
            return ctx.enter_context(nc.psum_tensor(name, shape, F32))

        sem = stage_semaphores(nc, ctx)

        NR = GROUPS + NEXP
        WO = sb("WO", [P, KD, D])
        GATE, GAIN, SHIFT, G2 = sb("GATE2", [P, 2, D]), sb("GAIN2", [P, 2, D]), sb("SHIFT2", [P, 2, D]), sb("G2", [P, D])
        LNG, LNB, WR, BR = sb("LNG", [P, DCONV]), sb("LNB", [P, DCONV]), sb("WR", [P, KD, NR]), sb("BR", [P, NR])
        NB, ST, CC, X = sb("NB", [P, 3, DATT]), sb("STAT", [P, 3, 2 * HEADS]), sb("CC", [P, KC, P]), sb("X3", [P, D])
        BM, BE, BW, BT, BD, BRC = (sb("BM", [P, HEADS]), sb("BE", [P, 3, HEADS]), sb("BW", [P, 3, HEADS]), sb("BT", [P, 3, HEADS]), sb("BD", [P, HEADS]), sb("BRC", [P, HEADS]))
        BS, MV, VE, RS, Y, TH = sb("BS3", [P, 6]), sb("MV3", [P, 2]), sb("VE3", [P, 1]), sb("RS3", [P, 1]), sb("Y3", [P, DCONV]), sb("TH3", [P, DCONV])
        MIX, MT = sb("MIX", [P, D]), sb("MT", [P, KD, P])
        X2, SQ, SSQ, MS, RSTD, H2, H2T = sb("X2", [P, D]), sb("SQ3", [P, D]), sb("SSQ3", [P, 1]), sb("MS3", [P, 1]), sb("RSTD3", [P, 1]), sb("H2", [P, D]), sb("H2T", [P, KD, P])
        LOG, G8, GM, GI, GF, NG = sb("LOG", [P, NR]), sb("G8", [P, 8]), sb("GM", [P, 8]), sb("GI", [P, 8], U32), sb("GF", [P, 1]), sb("NG", [P, 1])
        GE, ZG, OG, LS, L8, V8, I8, I2 = (sb("GE", [P, GROUPS]), sb("ZG", [P, 1]), sb("OG", [P, GROUPS]), sb("LS", [P, GROUPS, PER]), sb("L8", [P, PER]),
                                          sb("V8", [P, 8]), sb("I8", [P, 8], U32), sb("I2", [P, 2]))
        DV, EV, DEN, W1, EID, OH, A, RSEL, R2, SLOT = (sb("DV", [P, 1]), sb("EV", [P, 1]), sb("DEN", [P, 1]), sb("W1R", [P, 2]), sb("EID", [P, 2]), sb("OH", [P, 2, NEXP]),
                                                       sb("AR", [P, NEXP]), sb("RSEL", [P, 2, NEXP]), sb("R2", [P, 2]), sb("SLOT", [P, 2], U32))
        CNT, PAUSE, TOK = sb("CNT", [P, NEXP]), sb("PAUSE3", [P, 1]), sb("TOK", [P, 1], I32)
        placing = sem("placing")
        tok_ready = sem("tok_ready")
        CP, TPS, HPS, OP, SMALL = ps("CP3", [P, KC, P]), ps("TPS3", [P, KD, P]), ps("HPS3", [P, KD, P]), ps("OP3", [P, D]), ps("SMALL", [P, NR + 2 * NEXP])
        LP, RP, NP_ = SMALL[:, 0:NR], SMALL[:, NR:NR + NEXP], SMALL[:, NR + NEXP:]

        weights_in, mods_in, gain_ready, preset = sem("w3_in"), sem("mods3_in"), sem("gain3_ready"), sem("preset")
        br_in, cc_in, x_in = sem("br_in"), sem("cc_in"), sem("x3_in")
        astep, exp_b, att_ready, conv_turned, bn_done, ln_rs, y_norm, y_ready, th_ready, mix_ready = (
            sem("astep"), sem("exp_b"), sem("att_ready"), sem("conv_turned"), sem("bn_done"), sem("ln_rs"), sem("y_norm"), sem("y_ready"), sem("th3_ready"), sem("mix3_ready"))
        mix_turned, mt_ready, proj_done, x2_half, x2_ready, ssq_ready, rstd_half, rstd_ready, h2_half, h2_ready = (
            sem("mix_turned"), sem("mt_ready"), sem("proj_done"), sem("x2_half"), sem("x2_ready"), sem("ssq3_ready"), sem("rstd3_half"), sem("rstd3_ready"), sem("h2_half"), sem("h2_ready"))
        h2_turned, h2t_ready, logits_done, rstep, gmax_ready, group_exp, gap_ready, gap_exp, picked, rank_done, counted, slot_ready = (
            sem("h2_turned"), sem("h2t_ready"), sem("logits_done"), sem("rstep"), sem("gmax_ready"), sem("group_exp"), sem("gap_ready"), sem("gap_exp"), sem("picked"),
            sem("rank_done"), sem("counted"), sem("slot_ready"))
        att_half, cstep, w_done, kstep = sem("att_half"), sem("choose_step"), sem("w_done"), sem("rank_step")
        slot_free, logits_taken, loading = sem("slot_free"), sem("logits_taken"), sem("loading3")
        x2_out, h2_out, slot_out, count_psum, count_ready = sem("x2_out"), sem("h2_out"), sem("slot_out"), sem("count_psum"), sem("count_ready")
        DECT = TILES

        with nc.Block() as block:
            @block.sync
            def _(sp):
                for n, (dst, part) in enumerate(((GATE, 2), (GAIN, 4), (SHIFT, 3))):
                    sp.dma_start(dst[:, 0], dr["mod"][DEC:DEC + 1, part * D:(part + 1) * D].to_broadcast([P, D])).then_inc(mods_in, 16)
                    sp.dma_start(dst[0:DEC, 1], dr["mod"][0:DEC, part * D:(part + 1) * D]).then_inc(mods_in, 16)
                sp.dma_start(G2[:], t["g_norm2"].to_broadcast([P, D])).then_inc(mods_in, 16)
                sp.dma_start(LNG[:], t["ln_g"].to_broadcast([P, DCONV])).then_inc(mods_in, 16)
                sp.dma_start(LNB[:], t["ln_b"].to_broadcast([P, DCONV])).then_inc(mods_in, 16)
                sp.dma_start(BR[:, 0:GROUPS], t["b_router_group"].to_broadcast([P, GROUPS])).then_inc(mods_in, 16)
                sp.dma_start(BR[:, GROUPS:], t["b_router_expert"].to_broadcast([P, NEXP])).then_inc(mods_in, 16)

                def load(i, row):
                    if not isinstance(i, int):
                        sp.sem_inc(loading, 1)
                    sp.dma_start(NB[:], dr["num"].rearrange("b s c -> s b c")[ds(row, P)]).then_inc(br_in, 16)
                    sp.dma_start(ST[:], dr["stat"].rearrange("b s c -> s b c")[ds(row, P)]).then_inc(br_in, 16)
                    sp.dma_start(CC[:], dr["conv"].rearrange("(c p) s -> p c s", p=P)[:, :, ds(row, P)]).then_inc(cc_in, 16)

                def round_(i):
                    row, behind, ahead = ((i * P, (i - 1) * P, (i + 2) * P) if isinstance(i, int) else
                                          (sp.snap(i * P), sp.snap((i - 1) * P), sp.snap((i + 2) * P)))
                    taken = i + 2 if isinstance(i, int) else sp.snap(i + 2)
                    if isinstance(i, int) and i + 1 == DECT:
                        sp.wait_ge(mix_turned, TILES)
                        sp.dma_start(MIX[0:DEC], dr["mix"]).then_inc(cc_in, 16)
                    if there(i - 1):
                        sp.wait_ge(x2_ready, i)
                        n = rows_of(i - 1)
                        sp.dma_start(dr["x2"][ds(behind, n)], X2[0:n]).then_inc(x2_out, 16)
                    if there(i):
                        n = rows_of(i)
                        src = t["x_sample"][:, 0] if n == DEC else t["x_prompt"][0, ds(row, P)]
                        sp.dma_start(X[0:n], src).then_inc(x_in, 16)
                    if there(i + 2, TILES - 1):
                        wait(sp, conv_turned, taken)
                        wait(sp, att_ready, taken)
                        load(i + 2, ahead)
                    if there(i - 1):
                        sp.wait_ge(h2_ready, i)
                        n = rows_of(i - 1)
                        sp.dma_start(dr["h2"][ds(behind, n)], H2[0:n]).then_inc(h2_out, 16)

                load(0, 0)
                sp.dma_start(WR[:, :, 0:GROUPS], t["w_router_group"][0].rearrange("(k p) n -> p k n", p=P)).then_inc(weights_in, 16)
                sp.dma_start(WR[:, :, GROUPS:], t["w_router_expert"][0].rearrange("(k p) n -> p k n", p=P)).then_inc(weights_in, 16)
                sp.dma_start(WO[:], t["w_out"][0].rearrange("(k p) n -> p k n", p=P)).then_inc(weights_in, 16)
                rounds(sp, round_)
                sp.wait_ge(x2_out, 16 * ALLT + 16)
                sp.wait_ge(h2_out, 16 * ALLT + 16)

            @block.gpsimd
            def _(pool):
                pool.iota(state["token"][:], [[P, ALLT]], base=0, channel_multiplier=1).then_inc(preset, 1)
                pool.memset(CNT[:], 0.0).then_inc(preset, 1)
                pool.memset(G8[:], -3e38).then_inc(preset, 1)

                def normalise(i):
                    pool.wait_ge(bn_done, i * 2 + 2)
                    pool.tensor_tensor(VE[:], MV[:, 1:2], const("eps"), ALU.add).then_inc(ln_rs, 1)
                    pool.wait_ge(ln_rs, i * 2 + 1)
                    pool.tensor_tensor(RS[:], VE[:], const("neghalf"), ALU.pow).then_inc(ln_rs, 1)
                    pool.wait_ge(y_norm, i * 2 + 1)
                    pool.tensor_tensor(Y[:], Y[:], LNG[:], ALU.mult).then_inc(y_norm, 1)
                    pool.wait_ge(y_norm, i * 2 + 2)
                    pool.tensor_tensor(Y[:], Y[:], LNB[:], ALU.add).then_inc(y_ready, 1)

                def scale(i):
                    pool.wait_ge(ssq_ready, i + 1)
                    pool.tensor_tensor(MS[:], SSQ[:], const("eps"), ALU.add).then_inc(rstd_half, 1)
                    pool.wait_ge(rstd_half, i + 1)
                    pool.tensor_tensor(RSTD[:], MS[:], const("neghalf"), ALU.pow).then_inc(rstd_ready, 1)

                def place(i, rows):
                    pool.tensor_copy(TOK[:], state["token"][:, ds(i, 1)]).then_inc(tok_ready, 1)
                    pool.wait_ge(tok_ready, i + 1)
                    pool.wait_ge(slot_ready, i + 1)
                    pool.sem_inc(placing, 1)
                    for n in range(2):
                        pool.indirect_dma_start(dr["slot"], bass.IndirectOffsetOnAxis(ap=SLOT[0:rows, n:n + 1], axis=0),
                                                TOK[0:rows], None).then_inc(slot_out, 16)
                    pool.wait_ge(slot_out, i * 32 + 32)
                    pool.sem_inc(slot_free, 1)

                pool.wait_ge(mods_in, 16 * 11)

                def round_(i):
                    if there(i - 1):
                        n = rows_of(i - 1)
                        pool.wait_ge(x2_half, i)
                        pool.wait_ge(x_in, i * 16)
                        pool.tensor_tensor(X2[0:n], X2[0:n], X[0:n], ALU.add).then_inc(x2_ready, 1)
                    if there(i + 1, TILES - 1):
                        normalise(i + 1)
                    if there(i - 1):
                        scale(i - 1)
                        pool.wait_ge(h2_half, i)
                        pool.tensor_tensor(H2[0:n], H2[0:n], SHIFT[0:n, which_of(i - 1)], ALU.add).then_inc(h2_ready, 1)
                    if there(i - 3):
                        place(i - 3, rows_of(i - 3))

                rounds(pool, round_)
                pool.wait_ge(slot_out, 16 * 2 * ALLT)

            @block.scalar
            def _(act):
                def branch_weights(i):
                    act.wait_ge(astep, i * 5 + 2)
                    nc.scalar.activation(BW[:], BE[:], ACT.Exp).then_inc(exp_b, 1)

                def swish(i):
                    act.wait_ge(y_ready, i + 1)
                    nc.scalar.activation(TH[:], Y[:], ACT.Tanh, scale=0.5).then_inc(th_ready, 1)

                def take_mix(i):
                    act.wait_ge(mix_turned, i + 1)
                    nc.scalar.copy(MT[:, 0:KD // 2], TPS[:, 0:KD // 2])
                    nc.scalar.mul(MT[:, KD // 2:], TPS[:, KD // 2:], 0.5).then_inc(mt_ready, 1)

                def squares(i, rows):
                    act.wait_ge(x2_ready, i + 1)
                    nc.scalar.activation(SQ[0:rows], X2[0:rows], ACT.Square, scale=D ** -0.5, accum_out=SSQ[0:rows]).then_inc(ssq_ready, 1)

                def take_h2(i):
                    act.wait_ge(h2_turned, i + 1)
                    nc.scalar.copy(H2T[:], HPS[:]).then_inc(h2t_ready, 1)

                def route_exps(i):
                    act.wait_ge(gmax_ready, i + 1)
                    nc.scalar.activation(GE[:], LOG[:, 0:GROUPS], ACT.Exp, bias=NG[:], scale=1.0, accum_out=ZG[:]).then_inc(group_exp, 1)
                    act.wait_ge(gap_ready, i + 1)
                    nc.scalar.activation(EV[:], DV[:], ACT.Exp).then_inc(gap_exp, 1)

                act.sem_inc(x2_out, 16)
                act.sem_inc(h2_out, 16)
                act.sem_inc(slot_free, 1)

                def round_(i):
                    if there(i + 1, TILES - 1):
                        branch_weights(i + 1)
                    if there(i - 1):
                        squares(i - 1, rows_of(i - 1))
                    if there(i + 1, TILES - 1):
                        swish(i + 1)
                    if there(i + 1):
                        take_mix(i + 1)
                    if there(i - 1):
                        take_h2(i - 1)
                    if there(i - 2):
                        route_exps(i - 2)

                rounds(act, round_)

            @block.vector
            def _(dve):
                def stt(out, in0, scalar, in1, op0, op1):
                    return nc.vector.scalar_tensor_tensor(out=out, in0=in0, scalar=scalar, in1=in1, op0=op0, op1=op1)

                def mix(i):
                    dve.wait_ge(br_in, i * 32 + 32)
                    nc.vector.tensor_reduce(BM[:], ST[:, :, 0:HEADS].rearrange("p b h -> p h b"), AX.X, ALU.max).then_inc(astep, 1)
                    dve.wait_ge(astep, i * 5 + 1)
                    nc.vector.tensor_tensor(BE[:], ST[:, :, 0:HEADS], BM[:, None, :].to_broadcast([P, 3, HEADS]), ALU.subtract).then_inc(astep, 1)
                    dve.wait_ge(conv_turned, i + 1)
                    nc.vector.bn_stats(BS[:], CP[:].rearrange("p c t -> p (c t)")).then_inc(bn_done, 1)
                    dve.wait_ge(bn_done, i * 2 + 1)
                    nc.vector.memset(PAUSE[:], 0.0)
                    nc.vector.bn_aggr(MV[:], BS[:]).then_inc(bn_done, 1)
                    dve.wait_ge(exp_b, i + 1)
                    nc.vector.tensor_tensor(BT[:], BW[:], ST[:, :, HEADS:], ALU.mult).then_inc(astep, 1)
                    dve.wait_ge(astep, i * 5 + 3)
                    nc.vector.tensor_reduce(BD[:], BT[:].rearrange("p b h -> p h b"), AX.X, ALU.add).then_inc(astep, 1)
                    dve.wait_ge(astep, i * 5 + 4)
                    nc.vector.reciprocal(BRC[:], BD[:]).then_inc(astep, 1)
                    dve.wait_ge(ln_rs, i * 2 + 2)
                    nc.vector.tensor_scalar(Y[:], CP[:].rearrange("p c t -> p (c t)"), MV[:, 0:1], RS[:], ALU.subtract, ALU.mult).then_inc(y_norm, 1)
                    dve.wait_ge(astep, i * 5 + 5)
                    nc.vector.tensor_tensor(BT[:], BW[:], BRC[:, None, :].to_broadcast([P, 3, HEADS]), ALU.mult).then_inc(att_half, 1)
                    dve.wait_ge(att_half, i * 3 + 1)
                    nb = NB[:].rearrange("p b (h e) -> p (b h) e", e=DH)
                    nc.vector.tensor_tensor(nb, nb, BT[:].rearrange("p b h -> p (b h)")[:, :, None].to_broadcast([P, 3 * HEADS, DH]), ALU.mult).then_inc(att_half, 1)
                    dve.wait_ge(att_half, i * 3 + 2)
                    nc.vector.tensor_tensor(NB[:, 0], NB[:, 0], NB[:, 1], ALU.add).then_inc(att_half, 1)
                    dve.wait_ge(att_half, i * 3 + 3)
                    nc.vector.tensor_tensor(MIX[:, 0:DATT], NB[:, 0], NB[:, 2], ALU.add).then_inc(att_ready, 1)
                    dve.wait_ge(th_ready, i + 1)
                    stt(MIX[:, DATT:], TH[:], 1.0, Y[:], ALU.add, ALU.mult).then_inc(mix_ready, 1)

                def gated(i, rows, which):
                    dve.wait_ge(proj_done, i + 1)
                    dve.wait_ge(x2_out, i * 16 + 16)
                    wait(dve, h2_half, i)
                    nc.vector.tensor_tensor(X2[0:rows], OP[0:rows], GATE[0:rows, which], ALU.mult).then_inc(x2_half, 1)

                def norm(i, rows, which):
                    dve.wait_ge(rstd_ready, i + 1)
                    dve.wait_ge(h2_out, i * 16 + 16)
                    wait(dve, h2_turned, i)
                    stt(H2[0:rows], X2[0:rows], RSTD[0:rows], GAIN[0:rows, which], ALU.mult, ALU.mult).then_inc(h2_half, 1)

                def take_logits(i):
                    dve.wait_ge(logits_done, i + 1)
                    wait(dve, rank_done, i)
                    nc.vector.tensor_tensor(LOG[:], LP[:], BR[:], ALU.add).then_inc(logits_taken, 1)

                RST = 9

                def route(i):
                    at = [0]

                    def step(ins):
                        at[0] += 1
                        ins.then_inc(rstep, 1)
                        dve.wait_ge(rstep, i * RST + at[0])

                    dve.wait_ge(logits_taken, i + 1)
                    step(nc.vector.tensor_copy(G8[:, 0:GROUPS], LOG[:, 0:GROUPS]))
                    nc.vector.memset(PAUSE[:], 0.0)
                    step(nc.vector.max(GM[:], G8[:]))
                    nc.vector.tensor_scalar(NG[:], GM[:, 0:1], -1.0, None, ALU.mult).then_inc(gmax_ready, 1)
                    step(nc.vector.max_index(GI[:], GM[:], G8[:]))
                    step(nc.vector.tensor_copy(GF[:], GI[:, 0:1]))
                    step(nc.vector.tensor_scalar(OG[:], const("iota")[:, 0:GROUPS], GF[:], None, ALU.is_equal))
                    step(nc.vector.tensor_tensor(LS[:], LOG[:, GROUPS:].rearrange("p (g e) -> p g e", e=PER), OG[:, :, None].to_broadcast([P, GROUPS, PER]), ALU.mult))
                    step(nc.vector.tensor_reduce(L8[:], LS[:].rearrange("p g e -> p e g"), AX.X, ALU.add))
                    nc.vector.memset(PAUSE[:], 0.0)
                    step(nc.vector.max(V8[:], L8[:]))
                    nc.vector.tensor_tensor(DV[:], V8[:, 1:2], V8[:, 0:1], ALU.subtract).then_inc(gap_ready, 1)
                    step(nc.vector.max_index(I8[:], V8[:], L8[:]))
                    assert at[0] == RST

                def choose(i):
                    nc.vector.tensor_copy(I2[:], I8[:, 0:2]).then_inc(cstep, 1)
                    dve.wait_ge(cstep, i * 5 + 1)
                    stt(EID[:], GF[:].to_broadcast([P, 2]), float(PER), I2[:], ALU.mult, ALU.add).then_inc(cstep, 1)
                    dve.wait_ge(cstep, i * 5 + 2)
                    nc.vector.tensor_tensor(OH[:], const("iota")[:, None, :].to_broadcast([P, 2, NEXP]), EID[:, :, None].to_broadcast([P, 2, NEXP]), ALU.is_equal).then_inc(cstep, 1)
                    dve.wait_ge(cstep, i * 5 + 3)
                    nc.vector.tensor_tensor(A[:], OH[:, 0], OH[:, 1], ALU.add).then_inc(picked, 1)
                    dve.wait_ge(gap_exp, i + 1)
                    stt(DEN[:], EV[:], 1.0, ZG[:], ALU.add, ALU.mult).then_inc(cstep, 1)
                    dve.wait_ge(cstep, i * 5 + 4)
                    nc.vector.reciprocal(W1[:, 0:1], DEN[:]).then_inc(cstep, 1)
                    dve.wait_ge(cstep, i * 5 + 5)
                    nc.vector.tensor_tensor(W1[:, 1:2], W1[:, 0:1], EV[:], ALU.mult).then_inc(w_done, 1)
                    dve.wait_ge(w_done, i * 3 + 1)
                    nc.vector.tensor_copy(state["weight"][:, ds(i, 1)] if not isinstance(i, int) else state["weight"][:, i:i + 1], W1[:, None, :]).then_inc(w_done, 1)
                    nc.vector.tensor_copy(state["expert"][:, ds(i, 1)] if not isinstance(i, int) else state["expert"][:, i:i + 1], EID[:, None, :]).then_inc(w_done, 1)

                def rank(i, rows):
                    dve.wait_ge(rank_done, i + 1)
                    nc.vector.tensor_tensor(CNT[0:rows], CNT[0:rows], A[0:rows], ALU.add).then_inc(counted, 1)
                    nc.vector.tensor_tensor(RSEL[:], OH[:], RP[:, None, :].to_broadcast([P, 2, NEXP]), ALU.mult).then_inc(kstep, 1)
                    dve.wait_ge(kstep, i * 3 + 1)
                    nc.vector.tensor_reduce(R2[:], RSEL[:], AX.X, ALU.add).then_inc(kstep, 1)
                    dve.wait_ge(kstep, i * 3 + 2)
                    nc.vector.tensor_copy(state["rank"][:, ds(i, 1)] if not isinstance(i, int) else state["rank"][:, i:i + 1], R2[:, None, :]).then_inc(kstep, 1)
                    dve.wait_ge(slot_free, i + 1)
                    stt(SLOT[:], EID[:], float(CAP), R2[:], ALU.mult, ALU.add).then_inc(slot_ready, 1)
                    dve.wait_ge(counted, i + 1)

                dve.wait_ge(mods_in, 16 * 11)
                stt(GAIN[:, 0], GAIN[:, 0], 1.0, G2[:], ALU.add, ALU.mult).then_inc(gain_ready, 1)
                stt(GAIN[0:DEC, 1], GAIN[0:DEC, 1], 1.0, G2[0:DEC], ALU.add, ALU.mult).then_inc(gain_ready, 1)
                dve.wait_ge(gain_ready, 2)
                dve.wait_ge(preset, 3)

                def round_(i):
                    if there(i - 1):
                        gated(i - 1, rows_of(i - 1), which_of(i - 1))
                    if there(i - 2):
                        take_logits(i - 2)
                    if there(i - 3):
                        rank(i - 3, rows_of(i - 3))
                    if there(i + 1, TILES - 1):
                        wait(dve, mix_turned, i + 1)
                        mix(i + 1)
                    if there(i - 1):
                        norm(i - 1, rows_of(i - 1), which_of(i - 1))
                    if there(i - 2):
                        route(i - 2)
                        choose(i - 2)

                rounds(dve, round_)
                dve.wait_ge(count_psum, 1)
                nc.vector.tensor_copy(state["count"][:], NP_[:]).then_inc(count_ready, 1)

            @block.tensor
            def _(pe):
                def turn_conv(i):
                    pe.wait_ge(cc_in, i * 16 + 16)
                    if not (isinstance(i, int) and i == 0):
                        pe.wait_ge(y_norm, i * 2)
                    for c in range(KC):
                        mm = nc.tensor.transpose(CP[:, c], CC[:, c], const("ident"))
                    mm.then_inc(conv_turned, 1)

                def turn_mix(i, dec=False):
                    if dec:
                        pe.wait_ge(cc_in, 16 * ALLT)
                    else:
                        pe.wait_ge(mix_ready, i + 1)
                        pe.wait_ge(att_ready, i + 1)
                    for k in range(KD):
                        mm = nc.tensor.transpose(TPS[:, k], MIX[:, k * P:(k + 1) * P], const("ident"))
                    mm.then_inc(mix_turned, 1)

                def project(i):
                    pe.wait_ge(mt_ready, i + 1)
                    if not (isinstance(i, int) and i == 0):
                        pe.wait_ge(x2_half, i)
                    for n in range(D // 512):
                        for k in range(KD):
                            mm = nc.tensor.matmul(OP[:, n * 512:(n + 1) * 512], MT[:, k], WO[:, k, n * 512:(n + 1) * 512], start=k == 0, stop=k == KD - 1)
                    mm.then_inc(proj_done, 1)

                def logits(i):
                    pe.wait_ge(h2_ready, i + 1)
                    for k in range(KD):
                        mm = nc.tensor.transpose(HPS[:, k], H2[:, k * P:(k + 1) * P], const("ident"))
                    mm.then_inc(h2_turned, 1)
                    pe.wait_ge(h2t_ready, i + 1)
                    wait(pe, logits_taken, i)
                    wait(pe, kstep, i * 3 - 3)
                    for k in range(KD):
                        mm = nc.tensor.matmul(LP[:], H2T[:, k], WR[:, k], start=k == 0, stop=k == KD - 1)
                    mm.then_inc(logits_done, 1)

                def ranks(i, rows):
                    pe.wait_ge(picked, i + 1)
                    if not (isinstance(i, int) and i == 0):
                        pe.wait_ge(counted, i)
                        pe.wait_ge(kstep, i * 3)
                    nc.tensor.matmul(RP[:], const("before", rows), A[0:rows], start=True, stop=False)
                    nc.tensor.matmul(RP[:], const("ones"), CNT[:], start=False, stop=True).then_inc(rank_done, 1)


                def round_(i):
                    if there(i + 1, TILES - 1):
                        turn_conv(i + 1)
                    if there(i):
                        if isinstance(i, int) and i == 0:
                            pe.wait_ge(weights_in, 48)
                        project(i)
                    if there(i + 1):
                        turn_mix(i + 1, dec=isinstance(i, int) and i + 1 == DECT)
                    if there(i - 1):
                        logits(i - 1)
                    if there(i - 2):
                        ranks(i - 2, rows_of(i - 2))

                rounds(pe, round_)
                pe.wait_ge(counted, ALLT)
                pe.wait_ge(kstep, ALLT * 3)
                nc.tensor.matmul(NP_[:], const("ones"), CNT[:], start=True, stop=True).then_inc(count_psum, 1)



def experts(nc, t, dr, const, state):
    with ExitStack() as ctx:
        def sb(name, shape, dt=F32):
            return ctx.enter_context(nc.sbuf_tensor(name, shape, dt))

        def ps(name, shape):
            return ctx.enter_context(nc.psum_tensor(name, shape, F32))

        sem = stage_semaphores(nc, ctx)

        W1, W3, W2 = sb("W1E", [P, KD, DEXP]), sb("W3E", [P, KD, DEXP]), sb("W2E", [P, KF, D])
        fetching = sem("fetching")
        NOROWS = sb("NOROWS", [P, D])
        norows_set, norows_out = sem("norows_set"), sem("norows_out")
        IDX, XG, XH, XL = sb("IDX", [P, 1], I32), sb("XG", [P, D]), sb("XH", [P, KD, P], F32R), sb("XL", [P, KD, P], F32R)
        S, G, GH, GL, Y = sb("SE", [P, DEXP]), sb("GE5", [P, DEXP]), sb("GH", [P, KF, P], F32R), sb("GL", [P, KF, P], F32R), sb("YE", [P, D])
        HI = [sb(f"HI{n}", [P, KD * DEXP], F32R) for n in range(3)]
        LO = [sb(f"LO{n}", [P, KD * DEXP], F32R) for n in range(3)]
        HALF = KD * DEXP // 2
        hi_ready, lo_ready = ([sem(f"{x}_ready{n}") for n in range(3)] for x in ("hi", "lo"))
        xh_ready, gh_ready = sem("xh_ready"), sem("gh_ready")
        XP, AP_, BP, GP, YP = ps("XP", [P, KD, P]), ps("AE", [P, DEXP]), ps("BE5", [P, DEXP]), ps("GP", [P, KF, P]), ps("YP", [P, D])
        w1_in, w3_in, w2_in, idx_in, x_in = sem("gate_w_in"), sem("up_w_in"), sem("down_w_in"), sem("idx_in"), sem("xg_in")
        x_turned, xt_ready, a_done, b_done, s_ready, g_ready, g_turned, gt_ready, y_done, y_right, y_left, y_out = (
            sem("x_turned"), sem("xt_ready"), sem("a_done"), sem("b_done"), sem("s_ready"), sem("g_ready"), sem("g_turned"), sem("gt_ready"), sem("y_done"),
            sem("y_right"), sem("y_left"), sem("yrows_out"))
        table = state["blocks"]
        CMP, NBLK, LOW, START, END = sb("CMP", [P, NEXP, 16]), sb("NBLK", [P, NEXP]), sb("LOW", [P, NEXP, NEXP]), sb("START", [P, NEXP]), sb("END", [P, NEXP])
        SEL, BASE = sb("SEL", [P, ALLT * 2, NEXP]), sb("BASE", [P, ALLT * 2])
        step, table_ready = sem("table_step"), sem("table_ready")

        def tables(dve):
            at = [0]

            def then(ins):
                at[0] += 1
                ins.then_inc(step, 1)
                dve.wait_ge(step, at[0])

            then(nc.vector.tensor_tensor(CMP[:], state["count"][:, :, None].to_broadcast([P, NEXP, 16]),
                                         const("thresholds")[:, None, :].to_broadcast([P, NEXP, 16]), ALU.is_gt))
            then(nc.vector.tensor_reduce(NBLK[:], CMP[:], AX.X, ALU.add))
            then(nc.vector.tensor_scalar(NBLK[:], NBLK[:], 1.0, None, ALU.add))
            then(nc.vector.tensor_tensor(LOW[:], const("lower").rearrange("p (a b) -> p a b", b=NEXP), NBLK[:, None, :].to_broadcast([P, NEXP, NEXP]), ALU.mult))
            then(nc.vector.tensor_reduce(START[:], LOW[:], AX.X, ALU.add))
            then(nc.vector.tensor_tensor(END[:], START[:], NBLK[:], ALU.add))
            then(nc.vector.tensor_copy(table[:, 0:NEXP], START[:]))
            nc.vector.tensor_copy(table[:, NEXP:], END[:]).then_inc(table_ready, 1)
            dve.wait_ge(table_ready, 1)

        def destinations(dve):
            at = [7]

            def then(ins):
                at[0] += 1
                ins.then_inc(step, 1)
                dve.wait_ge(step, at[0])

            expert = state["expert"][:].rearrange("p t n -> p (t n)")
            then(nc.vector.tensor_tensor(SEL[:], const("iota")[:, None, :].to_broadcast([P, ALLT * 2, NEXP]),
                                         expert[:, :, None].to_broadcast([P, ALLT * 2, NEXP]), ALU.is_equal))
            then(nc.vector.tensor_tensor(SEL[:], SEL[:], START[:, None, :].to_broadcast([P, ALLT * 2, NEXP]), ALU.mult))
            then(nc.vector.tensor_reduce(BASE[:], SEL[:], AX.X, ALU.add))
            then(nc.vector.scalar_tensor_tensor(out=state["dest"][:].rearrange("p t n -> p (t n)"), in0=BASE[:], scalar=float(P),
                                                in1=state["rank"][:].rearrange("p t n -> p (t n)"), op0=ALU.mult, op1=ALU.add))

        def bounds(engine, e):
            first = engine.value_load(table[0:1, ds(e, 1)], min_val=0, max_val=MAXBLK)
            end = engine.value_load(table[0:1, ds(e + NEXP, 1)], min_val=1, max_val=MAXBLK)
            return first, end

        def first_and_last(engine, e):
            first, end = bounds(engine, e)
            return first, engine.snap(end - 1)

        raw = [w[:].rearrange("p k n -> p (k n)") for w in (W1, W3, W2)]
        come = (w1_in, w3_in, w2_in)

        with nc.Block() as block:
            @block.sync
            def _(sp):
                w1, w3 = (t[n][0].rearrange("e (k p) f -> e p k f", p=P) for n in ("w_expert_gate", "w_expert_up"))
                w2 = t["w_expert_down"][0].rearrange("e (k p) d -> e p k d", p=P)
                weights = ((W1, w1, w1_in), (W3, w3, w3_in), (W2, w2, w2_in))
                for dst, src, come in weights:
                    sp.dma_start(dst[:], src[0]).then_inc(come, 16)
                with sp.Fori(1, NEXP) as e:
                    split = sp.snap(e * 2)
                    for n, (dst, src, come) in enumerate(weights):
                        sp.wait_ge(lo_ready[n], split)
                        sp.dma_start(dst[:], src[ds(e, 1)].rearrange("a p k f -> (a p) k f")).then_inc(come, 16)

            @block.gpsimd
            def _(pool):
                def gather(b):
                    pool.wait_ge(x_turned, b + 1)
                    pool.sem_inc(fetching, 1)
                    pool.indirect_dma_start(XG[:], None, dr["h2"], bass.IndirectOffsetOnAxis(ap=IDX[:].bitcast(U32), axis=0)).then_inc(x_in, 16)

                pool.wait_ge(table_ready, 1)
                with pool.Fori(0, NEXP) as e:
                    first, end = bounds(pool, e)
                    with pool.Fori(first, end) as b:
                        slot = nc.s_assert_within(pool.snap(e * CAP + (b - first) * P), 0, NEXP * CAP - P,
                                                  skip_runtime_bounds_check_because="an expert's blocks stay inside its CAP slots")
                        pool.dma_start(IDX[:], dr["slot"][ds(slot, P), :]).then_inc(idx_in, 16)
                        pool.wait_ge(idx_in, b * 16 + 16)
                        gather(b)
                        pool.wait_ge(x_in, b * 16 + 16)
                blocks = pool.value_load(table[0:1, 2 * NEXP - 1:2 * NEXP], min_val=1, max_val=MAXBLK)
                gather(blocks)

            @block.scalar
            def _(act):
                act.sem_inc(y_out, 16)
                act.sem_inc(y_left, 1)
                act.wait_ge(table_ready, 1)
                blocks = act.value_load(table[0:1, 2 * NEXP - 1:2 * NEXP], min_val=1, max_val=MAXBLK)

                def take_x(b):
                    act.wait_ge(x_turned, b + 2)
                    nc.scalar.copy(XH[:], XP[:]).then_inc(xh_ready, 1)

                def upper(n, e):
                    act.wait_ge(come[n], e * 16 + 16)
                    for half in range(2):
                        cols = slice(half * HALF, half * HALF + HALF)
                        nc.scalar.copy(HI[n][:, cols], raw[n][:, cols]).then_inc(hi_ready[n], 1)

                for n in range(3):
                    upper(n, 0)
                take_x(0)
                act.wait_ge(norows_set, 1)
                with act.Fori(blocks, MAXBLK) as b:
                    act.dma_start(dr["y"][ds(act.snap(b * P), P)], NOROWS[:]).then_inc(norows_out, 16)

                def block_(b, split):
                    row = act.snap(b * P)
                    act.wait_ge(a_done, b + 2)
                    nc.scalar.activation(S[:], AP_[:], ACT.Silu).then_inc(s_ready, 1)
                    split(0)
                    act.wait_ge(g_turned, b + 1)
                    nc.scalar.copy(GH[:], GP[:]).then_inc(gh_ready, 1)
                    take_x(b + 1)
                    split(1)
                    act.wait_ge(y_done, b + 2)
                    act.wait_ge(y_out, b * 16 + 16)
                    nc.scalar.copy(Y[:, 0:D // 2], YP[:, 0:D // 2]).then_inc(y_left, 1)
                    act.wait_ge(y_left, b + 2)
                    act.wait_ge(y_right, b + 2)
                    act.dma_start(dr["y"][ds(row, P)], Y[:]).then_inc(y_out, 16)
                    act.sem_inc(norows_out, 16)
                    split(2)

                with act.Fori(0, NEXP - 1) as e:
                    first, last = first_and_last(act, e)
                    with act.If(last > first):
                        with act.Fori(first, last) as b:
                            block_(b, lambda n: None)
                    block_(last, lambda n: upper(n, e + 1))
                first, end = bounds(act, NEXP - 1)
                with act.Fori(first, end) as b:
                    block_(b, lambda n: None)
                act.wait_ge(norows_out, MAXBLK * 16)
                act.wait_ge(y_out, blocks * 16 + 16)
                act.sem_inc(y_left, 1)

            @block.vector
            def _(dve):
                dve.sem_inc(y_right, 1)
                nc.vector.memset(NOROWS[:], 0.0).then_inc(norows_set, 1)
                tables(dve)
                destinations(dve)

                def lower(n, e, halves=(0, 1)):
                    for half in halves:
                        dve.wait_ge(hi_ready[n], e * 2 + half + 1)
                        cols = slice(half * HALF, half * HALF + HALF)
                        nc.vector.tensor_tensor(LO[n][:, cols], raw[n][:, cols], HI[n][:, cols], ALU.subtract).then_inc(lo_ready[n], 1)

                def rest_x(b):
                    dve.wait_ge(xh_ready, b + 1)
                    nc.vector.tensor_tensor(XL[:], XP[:], XH[:], ALU.subtract).then_inc(xt_ready, 1)

                def block_(b, split):
                    split(0, (0,))
                    dve.wait_ge(s_ready, b + 1)
                    dve.wait_ge(b_done, b + 2)
                    nc.vector.tensor_tensor(G[:], S[:], BP[:], ALU.mult).then_inc(g_ready, 1)
                    dve.wait_ge(gh_ready, b + 1)
                    nc.vector.tensor_tensor(GL[:], GP[:], GH[:], ALU.subtract).then_inc(gt_ready, 1)
                    rest_x(b + 1)
                    split(0, (1,))
                    split(1, (0, 1))
                    dve.wait_ge(y_done, b + 2)
                    dve.wait_ge(y_out, b * 16 + 16)
                    nc.vector.tensor_copy(Y[:, D // 2:], YP[:, D // 2:]).then_inc(y_right, 1)
                    split(2, (0, 1))

                for n in range(3):
                    lower(n, 0)
                rest_x(0)
                with dve.Fori(0, NEXP - 1) as e:
                    first, last = first_and_last(dve, e)
                    with dve.If(last > first):
                        with dve.Fori(first, last) as b:
                            block_(b, lambda n, halves: None)
                    block_(last, lambda n, halves: lower(n, e + 1, halves))
                first, end = bounds(dve, NEXP - 1)
                with dve.Fori(first, end) as b:
                    block_(b, lambda n, halves: None)

            @block.tensor
            def _(pe):
                for s in (x_turned, a_done, b_done, y_done):
                    pe.sem_inc(s, 1)

                def turn_x(b):
                    pe.wait_ge(x_in, b * 16 + 16)
                    for k in range(KD):
                        mm = nc.tensor.transpose(XP[:, k], XG[:, k * P:(k + 1) * P], const("ident"))
                    mm.then_inc(x_turned, 1)

                pe.wait_ge(table_ready, 1)
                def products(out, x, k, n, cols, first, last):
                    hi, lo = x
                    for at, (a, w) in enumerate(((hi, HI[n]), (lo, HI[n]), (hi, LO[n]))):
                        mm = nc.tensor.matmul(out, a[:, k], w[:, cols], start=first and at == 0, stop=last and at == 2)
                    return mm

                turn_x(0)
                with pe.Fori(0, NEXP) as e:
                    first, end = bounds(pe, e)
                    with pe.Fori(first, end) as b:
                        pe.wait_ge(lo_ready[0], e * 2 + 2)
                        pe.wait_ge(xt_ready, b + 1)
                        for k in range(KD):
                            mm = products(AP_[:], (XH, XL), k, 0, slice(k * DEXP, (k + 1) * DEXP), k == 0, k == KD - 1)
                        mm.then_inc(a_done, 1)
                        pe.wait_ge(lo_ready[1], e * 2 + 2)
                        for k in range(KD):
                            mm = products(BP[:], (XH, XL), k, 1, slice(k * DEXP, (k + 1) * DEXP), k == 0, k == KD - 1)
                        mm.then_inc(b_done, 1)
                        turn_x(b + 1)
                        pe.wait_ge(g_ready, b + 1)
                        for k in range(KF):
                            mm = nc.tensor.transpose(GP[:, k], G[:, k * P:(k + 1) * P], const("ident"))
                        mm.then_inc(g_turned, 1)
                        pe.wait_ge(lo_ready[2], e * 2 + 2)
                        pe.wait_ge(gt_ready, b + 1)
                        pe.wait_ge(y_right, b + 1)
                        pe.wait_ge(y_left, b + 1)
                        for n in range(D // 512):
                            for k in range(KF):
                                mm = products(YP[:, n * 512:(n + 1) * 512], (GH, GL), k, 2, slice(k * D + n * 512, k * D + n * 512 + 512), k == 0, k == KF - 1)
                        mm.then_inc(y_done, 1)


def combine_and_normalise(nc, t, dr, const, state):
    with ExitStack() as ctx:
        def sb(name, shape, dt=F32):
            return ctx.enter_context(nc.sbuf_tensor(name, shape, dt))

        sem = stage_semaphores(nc, ctx)

        GATE, GF = sb("GATE6", [P, 2, D]), sb("GF6", [P, D])
        X, Y1, Y2, V, OUT, SQ = (sb("X6", [P, 2, D]), sb("Y16", [P, 2, D]), sb("Y26", [P, 2, D]), sb("V6", [P, 2, D]), sb("OUT6", [P, 2, D]), sb("SQ6", [P, D]))
        SSQ, MS, RSTD, DST = sb("SSQ6", [P, 2]), sb("MS6", [P, 2]), sb("RSTD6", [P, 2]), sb("DST6", [P, 2, 2], U32)
        fetching = sem("fetching6")
        mods_in = sem("mods6_in")
        x_in, y1_in, y2_in, out_out = ([sem(f"{n}6_{p}") for p in range(2)] for n in ("x_in", "y1_in", "y2_in", "out_out"))
        dst_ready, first_scaled, both_added, gated, sum_ready, ssq_ready, rstd_half, rstd_ready, out_ready = (
            sem("dst_ready"), sem("first_scaled"), sem("both_added"), sem("gated"), sem("sum_ready"), sem("ssq6"), sem("rstd6_half"), sem("rstd6"), sem("out6"))
        DECT = TILES
        PAIRS = TILES // 2

        def weight(tile, n, rows):
            return state["weight"][0:rows, ds(tile, 1), n:n + 1].rearrange("p a n -> p (a n)")

        with nc.Block() as block:
            @block.sync
            def _(sp):
                for p in range(2):
                    sp.dma_start(X[:, p], dr["x2"][p * P:(p + 1) * P]).then_inc(x_in[p], 16)
                sp.dma_start(GATE[:, 0], dr["mod"][DEC:DEC + 1, 5 * D:].to_broadcast([P, D])).then_inc(mods_in, 16)
                sp.dma_start(GATE[0:DEC, 1], dr["mod"][0:DEC, 5 * D:]).then_inc(mods_in, 16)
                sp.dma_start(GF[:], t["g_final"].to_broadcast([P, D])).then_inc(mods_in, 16)
                with sp.Fori(0, PAIRS - 1) as i:
                    for p in range(2):
                        row, ahead = sp.snap((i * 2 + p) * P), sp.snap((i * 2 + p + 2) * P)
                        sp.wait_ge(sum_ready, i * 2 + p + 1)
                        sp.dma_start(X[:, p], dr["x2"][ds(ahead, P)]).then_inc(x_in[p], 16)
                        sp.wait_ge(out_ready, i * 2 + p + 3)
                        sp.dma_start(t["y_prompt"][ds(row, P)], OUT[:, p]).then_inc(out_out[p], 16)
                sp.wait_ge(sum_ready, TILES - 1)
                sp.dma_start(X[0:DEC, 0], dr["x2"][SEQ:]).then_inc(x_in[0], 16)
                for p in range(2):
                    sp.wait_ge(out_ready, TILES + 1 + p)
                    sp.dma_start(t["y_prompt"][SEQ - (2 - p) * P:SEQ - (1 - p) * P], OUT[:, p]).then_inc(out_out[p], 16)
                sp.wait_ge(out_ready, ALLT + 2)
                sp.dma_start(t["y_sample"], OUT[0:DEC, 0]).then_inc(out_out[0], 16)
                sp.wait_ge(out_out[0], 16 * (PAIRS + 1) + 16)
                sp.wait_ge(out_out[1], 16 * PAIRS + 16)

            @block.gpsimd
            def _(pool):
                def fetch(p, tile, rows):
                    pool.tensor_copy(DST[:, p], state["dest"][:, ds(tile, 1)].rearrange("p a n -> p (a n)")).then_inc(dst_ready, 1)
                    pool.wait_ge(dst_ready, tile + 1)
                    pool.sem_inc(fetching, 1)
                    for n, (y, come) in enumerate(((Y1, y1_in), (Y2, y2_in))):
                        pool.indirect_dma_start(y[0:rows, p], None, dr["y"], bass.IndirectOffsetOnAxis(ap=DST[0:rows, p, n:n + 1], axis=0)).then_inc(come[p], 16)

                def scale(p, tile):
                    pool.wait_ge(ssq_ready, tile + 1)
                    pool.tensor_tensor(MS[:, p:p + 1], SSQ[:, p:p + 1], const("eps"), ALU.add).then_inc(rstd_half, 1)
                    pool.wait_ge(rstd_half, tile + 1)
                    pool.tensor_tensor(RSTD[:, p:p + 1], MS[:, p:p + 1], const("neghalf"), ALU.pow).then_inc(rstd_ready, 1)

                fetch(0, 0, P)
                fetch(1, 1, P)
                with pool.Fori(0, PAIRS - 1) as i:
                    for p in range(2):
                        pool.wait_ge(both_added, i * 2 + p + 1)
                        fetch(p, i * 2 + p + 2, P)
                        scale(p, i * 2 + p)
                pool.wait_ge(both_added, TILES - 1)
                fetch(0, DECT, DEC)
                for tile in range(TILES - 2, ALLT):
                    scale(tile % 2, tile)

            @block.scalar
            def _(act):
                for p in range(2):
                    act.sem_inc(out_out[p], 16)

                def first(i, p, tile, rows):
                    act.wait_ge(y1_in[p], i * 16 + 16)
                    act.wait_ge(out_ready, tile + 1)
                    nc.scalar.activation(V[0:rows, p], Y1[0:rows, p], ACT.Copy, scale=weight(tile, 0, rows)).then_inc(first_scaled, 1)

                def squares(p, tile, rows):
                    act.wait_ge(sum_ready, tile + 1)
                    nc.scalar.activation(SQ[0:rows], V[0:rows, p], ACT.Square, scale=D ** -0.5, accum_out=SSQ[0:rows, p:p + 1]).then_inc(ssq_ready, 1)

                first(0, 0, 0, P)
                with act.Fori(0, PAIRS - 1) as i:
                    first(i, 1, i * 2 + 1, P)
                    squares(0, i * 2, P)
                    first(i + 1, 0, i * 2 + 2, P)
                    squares(1, i * 2 + 1, P)
                first(PAIRS - 1, 1, TILES - 1, P)
                squares(0, TILES - 2, P)
                first(PAIRS, 0, DECT, DEC)
                squares(1, TILES - 1, P)
                act.wait_ge(ssq_ready, TILES)
                squares(0, DECT, DEC)

            @block.vector
            def _(dve):
                dve.sem_inc(out_ready, 2)

                def add(i, p, tile, rows, which):
                    v = V[0:rows, p]
                    dve.wait_ge(first_scaled, tile + 1)
                    dve.wait_ge(y2_in[p], i * 16 + 16)
                    nc.vector.scalar_tensor_tensor(out=v, in0=Y2[0:rows, p], scalar=weight(tile, 1, rows), in1=v, op0=ALU.mult, op1=ALU.add).then_inc(both_added, 1)
                    dve.wait_ge(both_added, tile + 1)
                    nc.vector.tensor_tensor(v, v, GATE[0:rows, which], ALU.mult).then_inc(gated, 1)
                    dve.wait_ge(gated, tile + 1)
                    dve.wait_ge(x_in[p], i * 16 + 16)
                    nc.vector.tensor_tensor(v, v, X[0:rows, p], ALU.add).then_inc(sum_ready, 1)

                def finish(i, p, tile, rows):
                    dve.wait_ge(rstd_ready, tile + 1)
                    dve.wait_ge(out_out[p], i * 16 + 16)
                    nc.vector.scalar_tensor_tensor(out=OUT[0:rows, p], in0=V[0:rows, p], scalar=RSTD[0:rows, p:p + 1], in1=GF[0:rows], op0=ALU.mult, op1=ALU.mult).then_inc(out_ready, 1)

                dve.wait_ge(mods_in, 48)
                add(0, 0, 0, P, 0)
                with dve.Fori(0, PAIRS - 1) as i:
                    add(i, 1, i * 2 + 1, P, 0)
                    finish(i, 0, i * 2, P)
                    add(i + 1, 0, i * 2 + 2, P, 0)
                    finish(i, 1, i * 2 + 1, P)
                add(PAIRS - 1, 1, TILES - 1, P, 0)
                finish(PAIRS - 1, 0, TILES - 2, P)
                add(PAIRS, 0, DECT, DEC, 1)
                finish(PAIRS - 1, 1, TILES - 1, P)
                finish(PAIRS, 0, DECT, DEC)


OUTPUTS = {
    "y_prompt": (1, SEQ, D), "y_sample": (DEC, 1, D),
    "new_k_prompt": (1, 1, WIN, HEADS, DH), "new_v_prompt": (1, 1, WIN, HEADS, DH), "new_conv_prompt": (1, 1, TAPS - 1, DCONV),
    "new_k_sample": (1, DEC, WIN, HEADS, DH), "new_v_sample": (1, DEC, WIN, HEADS, DH), "new_conv_sample": (1, DEC, TAPS - 1, DCONV),
}
FLAT = {
    "y_prompt": "a s d -> (a s) d", "y_sample": "b a d -> (b a) d",
    "new_k_prompt": "a b s h e -> (a b s) (h e)", "new_v_prompt": "a b s h e -> (a b s) (h e)", "new_conv_prompt": "a b s c -> (a b s) c",
    "new_k_sample": "a b s h e -> (a b) (s h e)", "new_v_sample": "a b s h e -> (a b) (s h e)", "new_conv_sample": "a b s c -> (a b) (s c)",
    "cache_k": "a b s h e -> (a b) (s h e)", "cache_v": "a b s h e -> (a b) (s h e)", "state_conv": "a b s c -> (a b) (s c)",
}


def layout(nc, inputs):
    arrays, t, outs = {}, {}, {}
    given = {name: np.ascontiguousarray(a) for name, a in inputs.items()}
    given["constants"] = constant_columns()[1]
    given["g_final"] = given["g_final"].reshape(1, D)
    for name, a in given.items():
        arrays[f"in_{name}"] = a
        ap = nc.dram_tensor(f"in_{name}", a.shape, mybir.dt.from_np(a.dtype), kind="ExternalInput").ap()
        t[name] = ap.rearrange(FLAT[name]) if name in FLAT else ap
    for name, shape in OUTPUTS.items():
        outs[name] = f"out_{name}"
        t[name] = nc.dram_tensor(outs[name], shape, F32, kind="ExternalOutput").ap().rearrange(FLAT[name])
    return arrays, t, outs


def kernel(**inputs):
    import concourse.bacc as bacc
    from concourse.bass_utils import run_bass_kernel_spmd

    nc = bacc.Bacc("TRN2", target_bir_lowering=False, num_devices=1)
    arrays, t, outs = layout(nc, inputs)
    decoder_step(nc, t, constant_columns()[0])
    r = run_bass_kernel_spmd(nc, [arrays], core_ids=[0])
    return tuple(r.results[0][outs[name]] for name in OUTPUTS)
```
